# Optimizing a Trainium2 kernel written in Bass

```python
import math
import jax
import jax.numpy as jnp
from jax import lax
import numpy as np

D_MODEL = 4096
BATCH = 1
SEQ = 256
DEPTH = 1

HEAD_DIM = 128
W_A = D_MODEL // 4
W_B = D_MODEL // 2
W_C = D_MODEL - W_A - W_B
D_MIX = W_A + W_B + W_C
H_A = W_A // HEAD_DIM
DQK_A = HEAD_DIM // 2
DV_A = HEAD_DIM
GATE_CAP = 15.0
H_B = W_B // HEAD_DIM
HKV_B = 4
Q_LORA = 896
IDX_H = 16
IDX_D = 64
TOPK = 256
QBLK = 128
H_C = W_C // HEAD_DIM
DK_C = HEAD_DIM
DV_C = HEAD_DIM
CONV_K = 4
CHUNK = 64
EPS = 1e-6

IN_SPLITS = (H_A * DQK_A, H_A * DQK_A, W_A, H_A, H_A, W_A, W_A,
             Q_LORA, HKV_B * HEAD_DIM, HKV_B * HEAD_DIM, IDX_D, IDX_H, W_B,
             3 * W_C, H_C, H_C, W_C)
N_IN = sum(IN_SPLITS)

kernel_name = "hymba_style_mlstm_dsa_gdn_hybrid"

def rms_norm(x, g):
    xf = x.astype(jnp.float32)
    y = xf * lax.rsqrt(jnp.mean(xf * xf, axis=-1, keepdims=True) + EPS)
    return (y * g.astype(jnp.float32)).astype(x.dtype)

def layer_norm(x, g, b):
    xf = x.astype(jnp.float32)
    mu = jnp.mean(xf, axis=-1, keepdims=True)
    xc = xf - mu
    y = xc * lax.rsqrt(jnp.mean(xc * xc, axis=-1, keepdims=True) + EPS)
    return (y * g.astype(jnp.float32) + b.astype(jnp.float32)).astype(x.dtype)

def l2_normalize(x):
    xf = x.astype(jnp.float32)
    return (xf * lax.rsqrt(jnp.sum(xf * xf, axis=-1, keepdims=True) + EPS)).astype(x.dtype)

def soft_cap(x):
    return GATE_CAP * jnp.tanh(x / GATE_CAP)

def causal_depthwise_conv(x, w):
    width, ch = w.shape
    return lax.conv_general_dilated(x, w[:, None, :].astype(x.dtype), window_strides=(1,),
                                    padding=[(width - 1, 0)],
                                    dimension_numbers=('NWC', 'WIO', 'NWC'),
                                    feature_group_count=ch)

def to_chunks(a, n_chunks):
    b = a.shape[0]
    a = a.astype(jnp.float32).reshape((b, n_chunks, CHUNK) + a.shape[2:])
    return jnp.moveaxis(jnp.moveaxis(a, 1, 0), 2, 3)

def from_chunks(a):
    n, b, h, l, d = a.shape
    return jnp.moveaxis(jnp.moveaxis(a, 3, 2), 0, 1).reshape(b, n * l, h, d)

def mlstm_chunked(q, k, v, i_pre, f_pre):
    b, s, h, dk = q.shape
    dv = v.shape[-1]
    n_chunks = s // CHUNK
    qc = to_chunks(q, n_chunks) * dk ** -0.5
    kc = to_chunks(k, n_chunks)
    vc = to_chunks(v, n_chunks)
    log_f = jax.nn.log_sigmoid(to_chunks(f_pre, n_chunks))
    log_i = to_chunks(i_pre, n_chunks)
    causal = jnp.tril(jnp.ones((CHUNK, CHUNK), bool))

    def step(carry, xs):
        c_st, n_st, m_st = carry
        qj, kj, vj, lfj, lij = xs
        bj = jnp.cumsum(lfj, axis=-1)
        d_log = jnp.where(causal, bj[..., :, None] - bj[..., None, :] + lij[..., None, :], -jnp.inf)
        inter = bj + m_st[..., None]
        m_j = jnp.maximum(inter, jnp.max(d_log, axis=-1))
        p = jnp.exp(d_log - m_j[..., None]) * jnp.einsum('bhjd,bhsd->bhjs', qj, kj)
        w_inter = jnp.exp(inter - m_j)
        num = p @ vj + w_inter[..., None] * jnp.einsum('bhjd,bhdv->bhjv', qj, c_st)
        den = jnp.sum(p, axis=-1) + w_inter * jnp.einsum('bhjd,bhd->bhj', qj, n_st)
        h_out = num / jnp.maximum(jnp.abs(den), jnp.exp(-m_j))[..., None]
        u = bj[..., -1:] - bj + lij
        m_new = jnp.maximum(bj[..., -1] + m_st, jnp.max(u, axis=-1))
        w_u = jnp.exp(u - m_new[..., None])
        decay = jnp.exp(bj[..., -1] + m_st - m_new)
        c_st = decay[..., None, None] * c_st + jnp.einsum('bhs,bhsd,bhsv->bhdv', w_u, kj, vj)
        n_st = decay[..., None] * n_st + jnp.einsum('bhs,bhsd->bhd', w_u, kj)
        return (c_st, n_st, m_new), h_out

    init = (jnp.zeros((b, h, dk, dv), jnp.float32), jnp.zeros((b, h, dk), jnp.float32),
            jnp.zeros((b, h), jnp.float32))
    _, hs = lax.scan(step, init, (qc, kc, vc, log_f, log_i))
    return from_chunks(hs).astype(v.dtype)

def gated_delta_chunked(q, k, v, g, beta):
    b, s, h, dk = q.shape
    dv = v.shape[-1]
    n_chunks = s // CHUNK
    qc = to_chunks(q, n_chunks) * dk ** -0.5
    kc = to_chunks(k, n_chunks)
    vc = to_chunks(v, n_chunks)
    gc = jnp.cumsum(to_chunks(g, n_chunks), axis=-1)
    bc = to_chunks(beta, n_chunks)
    causal = jnp.tril(jnp.ones((CHUNK, CHUNK), bool))
    strict = jnp.tril(jnp.ones((CHUNK, CHUNK), bool), -1)
    diff = gc[..., :, None] - gc[..., None, :]
    gamma = jnp.where(causal, jnp.exp(jnp.where(causal, diff, 0.0)), 0.0)
    kb = kc * bc[..., None]
    a_kk = jnp.where(strict, jnp.einsum('nbhid,nbhjd->nbhij', kb, kc) * gamma, 0.0)
    eye = jnp.eye(CHUNK, dtype=jnp.float32)
    rhs = jnp.concatenate([vc * bc[..., None], kb * jnp.exp(gc)[..., None]], axis=-1)
    sol = lax.linalg.triangular_solve(eye + a_kk, rhs, left_side=True, lower=True)
    u, w = sol[..., :dv], sol[..., dv:]
    a_qk = jnp.einsum('nbhid,nbhjd->nbhij', qc, kc) * gamma
    decay_q = jnp.exp(gc)
    decay_k = jnp.exp(gc[..., -1:] - gc)

    def step(state, xs):
        qj, kj, uj, wj, aj, dqj, dkj, glast = xs
        v_new = uj - wj @ state
        o = (qj * dqj[..., None]) @ state + aj @ v_new
        state = jnp.exp(glast)[..., None, None] * state + jnp.einsum('bhld,bhlv->bhdv', kj * dkj[..., None], v_new)
        return state, o

    s0 = jnp.zeros((b, h, dk, dv), jnp.float32)
    _, o = lax.scan(step, s0, (qc, kc, u, w, a_qk, decay_q, decay_k, gc[..., -1]))
    return from_chunks(o).astype(v.dtype)

def dsa_sparse_attention(q, k, v, q_idx, k_idx, w_idx, k_sel):
    b, s, h, dh = q.shape
    hkv = k.shape[2]
    nb = s // QBLK

    def blocks(a):
        return jnp.moveaxis(a.reshape((b, nb, QBLK) + a.shape[2:]), 1, 0)

    q_blocks = blocks(q.reshape(b, s, hkv, h // hkv, dh))
    qi_blocks = blocks(q_idx)
    w_blocks = blocks(w_idx)
    pos_blocks = jnp.arange(s).reshape(nb, QBLK)
    key_pos = jnp.arange(s)
    gather = jax.vmap(lambda seq, ind: seq[ind])

    def one_block(args):
        q_blk, qi_blk, w_blk, t = args
        logits = jnp.einsum('bqhd,bsd->bqhs', qi_blk, k_idx)
        score = jnp.einsum('bqhs,bqh->bqs', jax.nn.relu(logits), w_blk).astype(jnp.float32)
        score = jnp.where((key_pos[None, :] <= t[:, None])[None], score, -jnp.inf)
        _, idx = lax.top_k(score, k_sel)
        valid = idx <= t[None, :, None]
        k_g = gather(k, idx)
        v_g = gather(v, idx)
        sc = jnp.einsum('bqhgd,bqkhd->bqhgk', q_blk, k_g).astype(jnp.float32) * dh ** -0.5
        sc = jnp.where(valid[:, :, None, None, :], sc, -jnp.inf)
        p = jax.nn.softmax(sc, axis=-1).astype(v.dtype)
        return jnp.einsum('bqhgk,bqkhd->bqhgd', p, v_g)

    out = lax.map(one_block, (q_blocks, qi_blocks, w_blocks, pos_blocks))
    return jnp.moveaxis(out, 0, 1).reshape(b, s, h * dh)

def setup_inputs(seed: int = 0) -> dict:
    key = jax.random.key(seed)
    ks = jax.random.split(key, 18)
    f32 = jnp.float32
    L = DEPTH

    def nrm(k, shape, scale):
        return scale * jax.random.normal(k, shape, f32)

    x = jax.random.normal(ks[0], (BATCH, SEQ, D_MODEL), f32)
    norm_g = 1.0 + nrm(ks[1], (L, D_MODEL), 0.02)
    w_in = nrm(ks[2], (L, D_MODEL, N_IN), D_MODEL ** -0.5)
    w_out = nrm(ks[3], (L, D_MIX, D_MODEL), D_MIX ** -0.5)
    m_ib = nrm(ks[4], (L, H_A), 0.1)
    m_fb = 3.0 + nrm(ks[5], (L, H_A), 0.5)
    m_norm_g = 1.0 + nrm(ks[6], (L, W_A), 0.02)
    a_cq_g = 1.0 + nrm(ks[7], (L, Q_LORA), 0.02)
    a_wuq = nrm(ks[8], (L, Q_LORA, W_B), Q_LORA ** -0.5)
    a_wuqi = nrm(ks[9], (L, Q_LORA, IDX_H * IDX_D), Q_LORA ** -0.5)
    a_qn_g = 1.0 + nrm(ks[10], (L, HEAD_DIM), 0.02)
    a_kn_g = 1.0 + nrm(ks[11], (L, HEAD_DIM), 0.02)
    a_ki_g = 1.0 + nrm(ks[12], (L, IDX_D), 0.02)
    a_ki_b = nrm(ks[13], (L, IDX_D), 0.02)
    d_conv_w = nrm(ks[14], (L, CONV_K, 3 * W_C), CONV_K ** -0.5)
    d_a_log = jnp.log(jax.random.uniform(ks[15], (L, H_C), f32, 1.0, 16.0))
    dt = jnp.exp(jax.random.uniform(ks[16], (L, H_C), f32, math.log(1e-3), math.log(1e-1)))
    d_dt_bias = dt + jnp.log(-jnp.expm1(-dt))
    d_norm_g = 1.0 + nrm(ks[17], (L, DV_C), 0.02)
    return {"x": x, "norm_g": norm_g, "w_in": w_in, "w_out": w_out,
            "m_ib": m_ib, "m_fb": m_fb, "m_norm_g": m_norm_g,
            "a_cq_g": a_cq_g, "a_wuq": a_wuq, "a_wuqi": a_wuqi, "a_qn_g": a_qn_g,
            "a_kn_g": a_kn_g, "a_ki_g": a_ki_g, "a_ki_b": a_ki_b,
            "d_conv_w": d_conv_w, "d_a_log": d_a_log, "d_dt_bias": d_dt_bias, "d_norm_g": d_norm_g}

def reference(x, norm_g, w_in, w_out, m_ib, m_fb, m_norm_g, a_cq_g, a_wuq, a_wuqi, a_qn_g,
              a_kn_g, a_ki_g, a_ki_b, d_conv_w, d_a_log, d_dt_bias, d_norm_g):
    B, S, _ = x.shape
    k_sel = min(TOPK, S // 4)
    split_points = np.cumsum(IN_SPLITS)[:-1].tolist()
    for l in range(DEPTH):
        h = rms_norm(x, norm_g[l])
        proj = jnp.einsum('bsd,dn->bsn', h, w_in[l])
        (aq, ak, av, ai, af, ao, az,
         bcq, bk, bv, bki, bwi, bz,
         cqkv, cb, ca, cz) = jnp.split(proj, split_points, axis=-1)

        h_a = mlstm_chunked(aq.reshape(B, S, H_A, DQK_A), ak.reshape(B, S, H_A, DQK_A),
                            av.reshape(B, S, H_A, DV_A),
                            soft_cap(ai + m_ib[l]), soft_cap(af + m_fb[l]))
        h_a = rms_norm(h_a, m_norm_g[l].reshape(H_A, DV_A)).reshape(B, S, W_A)
        y_a = jax.nn.sigmoid(ao) * h_a * jax.nn.silu(az)

        c_q = rms_norm(bcq, a_cq_g[l])
        q_b = rms_norm(jnp.einsum('bsr,rn->bsn', c_q, a_wuq[l]).reshape(B, S, H_B, HEAD_DIM), a_qn_g[l])
        k_b = rms_norm(bk.reshape(B, S, HKV_B, HEAD_DIM), a_kn_g[l])
        v_b = bv.reshape(B, S, HKV_B, HEAD_DIM)
        q_idx = jnp.einsum('bsr,rn->bsn', c_q, a_wuqi[l]).reshape(B, S, IDX_H, IDX_D)
        k_idx = layer_norm(bki, a_ki_g[l], a_ki_b[l])
        w_idx = bwi * (IDX_H ** -0.5 * IDX_D ** -0.5)
        y_b = dsa_sparse_attention(q_b, k_b, v_b, q_idx, k_idx, w_idx, k_sel) * jax.nn.silu(bz)

        qkv = jax.nn.silu(causal_depthwise_conv(cqkv, d_conv_w[l]))
        q_c, k_c, v_c = jnp.split(qkv, 3, axis=-1)
        q_c = l2_normalize(q_c.reshape(B, S, H_C, DK_C))
        k_c = l2_normalize(k_c.reshape(B, S, H_C, DK_C))
        beta = jax.nn.sigmoid(cb.astype(jnp.float32))
        g = -jnp.exp(d_a_log[l].astype(jnp.float32)) * jax.nn.softplus(
            ca.astype(jnp.float32) + d_dt_bias[l].astype(jnp.float32))
        o_c = gated_delta_chunked(q_c, k_c, v_c.reshape(B, S, H_C, DV_C), g, beta)
        y_c = (rms_norm(o_c, d_norm_g[l]) * jax.nn.silu(cz.reshape(B, S, H_C, DV_C))).reshape(B, S, W_C)

        y = jnp.concatenate([y_a, y_b, y_c], axis=-1)
        x = x + jnp.einsum('bsm,md->bsd', y, w_out[l])
    return x


_drawn_inputs = setup_inputs


def setup_inputs(seed=0):
    import zlib

    import numpy as np

    out = dict(_drawn_inputs(seed))
    spreads = {}
    factors = {'norm_g': 3.459,
     'm_ib': 8.0,
     'm_norm_g': 8.0,
     'a_cq_g': 7.461,
     'a_qn_g': 8.0,
     'a_kn_g': 8.0,
     'a_ki_g': 7.654,
     'a_ki_b': 8.0,
     'd_norm_g': 8.0}
    for name, (base, spread) in spreads.items():
        noise = np.random.default_rng([zlib.crc32(name.encode()), seed]).standard_normal(out[name].shape)
        drawn = base * np.exp(spread * noise) if base else spread * noise
        out[name] = jnp.asarray(drawn.astype(out[name].dtype))
    for name, factor in factors.items():
        out[name] = (out[name] * factor).astype(out[name].dtype)
    return out
```

```python
from contextlib import ExitStack

import concourse.bass as bass
from concourse import mybir

F32 = mybir.dt.float32
F32R = mybir.dt.float32r
BF16 = mybir.dt.bfloat16
ALU = mybir.AluOpType
ACT = mybir.ActivationFunctionType
AX_X = mybir.AxisListType.X

P = 128
D = 4096
SEQ = 256
M = SEQ // P
KT = D // P
HEAD = 128
W_A, W_B, W_C = D // 4, D // 2, D // 4
H_A, H_B, H_C = W_A // HEAD, W_B // HEAD, W_C // HEAD
DQK = HEAD // 2
GATE_CAP = 15.0
HKV = 4
GRP = H_B // HKV
Q_LORA = 896
QKT = Q_LORA // P
IDX_H, IDX_D = 16, 64
TOPK = min(256, SEQ // 4)
CONV_K = 4
EPS = 1e-6
NEG = -1e30
BIG = 3.3e38

C_AQ = 0
C_AK = C_AQ + H_A * DQK
C_AV = C_AK + H_A * DQK
C_AI = C_AV + W_A
C_AO = C_AI + 2 * H_A
C_AZ = C_AO + W_A
C_BCQ = C_AZ + W_A
C_BK = C_BCQ + Q_LORA
C_BV = C_BK + HKV * HEAD
C_BKI = C_BV + HKV * HEAD
C_BZ = C_BKI + IDX_D + IDX_H
C_CQKV = C_BZ + W_B
C_CB = C_CQKV + 3 * W_C
C_CZ = C_CB + 2 * H_C
N_IN = C_CZ + W_C

G_AI, G_AF, G_CB, G_CA, G_KI, G_WI, G_W = 0, 8, 16, 24, 32, 96, 112

R_NORM, R_CQ, R_QN, R_KN, R_KIG, R_KIB, R_MN, R_DN, R_N = 0, 32, 39, 40, 41, 42, 43, 51, 52
N_TAP = CONV_K * 3 * W_C // P
CH = 3 * W_C // P

RAW_BUFS = 4
SPLIT_BUFS = 3
AHEAD = SPLIT_BUFS - 1
LEVELS = 7
UNITS = [(hg, m) for hg in range(H_C // 4) for m in range(M)]

USES = {"gt": 2, "gb": 1, "kx": 1, "conv": 1, "cn": 1, "ca": 2, "cg": 2, "ct": 1, "cm": 1, "cu": 1, "cv": 1,
        "ck": 1, "cs": 1, "cr": 1, "co": 2, "bt": 1, "bkt": 2, "bit": 2, "bsc": 2, "bqt": 2, "bs": 1, "bp": 1,
        "bo": 1, "at": 2, "ae": 2, "ap": 1, "yt": 1}


def plan():
    wide = 2
    blocks = []

    def block(kind, arg, operand, kts, per, width, matrix, col):
        blocks.append(dict(kind=kind, arg=arg, operand=operand, kts=kts, per=per, width=width, matrix=matrix,
                           col=col))

    full = list(range(KT))

    def project(kind, arg, col, width=512):
        block(kind, arg, "h", full, wide, width, "w_in", col)

    block("gates", 0, "h", full, 8, G_W, "w_in", 0)
    for j in range(6):
        project("conv", j, C_CQKV + 512 * j)
    for j in range(2):
        project("silu", W_A + W_B + 512 * j, C_CZ + 512 * j)
    project("cq", 0, C_BCQ)
    project("cq", 512, C_BCQ + 512, Q_LORA - 512)
    project("bkv", 0, C_BK)
    project("bkv", 512, C_BV)
    for j in range(4):
        project("silu", W_A + 512 * j, C_BZ + 512 * j)
    for j in range(2):
        block("bi", j, "cq", list(range(QKT)), wide, 512, "wuqi", 512 * j)
    for j in range(4):
        project(("ao", "az")[j // 2], 512 * (j % 2), (C_AO, C_AZ)[j // 2] + 512 * (j % 2))
        block("bq", j, "cq", list(range(QKT)), wide, 512, "wuq", 512 * j)
    project("aqk", 0, C_AQ)
    project("aqk", 1, C_AK)
    project("av", 0, C_AV)
    project("av", 1, C_AV + 512)
    kt_a = W_A // P
    for n in range(D // 512):
        block("out1", n, "y", full[kt_a:], wide, 512, "w_out", 512 * n)
    for n in range(D // 512):
        block("out2", n, "y", full[:kt_a], wide, 512, "w_out", 512 * n)

    chunks, last = [], []
    for b, blk in enumerate(blocks):
        for i in range(0, len(blk["kts"]), blk["per"]):
            chunks.append((b, blk["kts"][i:i + blk["per"]]))
        last.append(len(chunks) - 1)

    woven = [[] for _ in chunks]

    def end(kind, arg=0):
        return next(last[b] for b, x in enumerate(blocks) if x["kind"] == kind and x["arg"] == arg)

    def weave(at, pieces):
        for piece in pieces:
            woven[at] += piece if isinstance(piece, list) else [piece]
            at += 1
        return at

    for b, x in enumerate(blocks):
        woven[last[b]].append(("evac", b))
    g = weave(end("gates") + 1, [("gt", 0), ("gs", 0), ("gb", 0), ("kx", 0)])
    for j in range(6):
        at = weave(end("conv", j) + 1, [("conv", 2 * j), ("conv", 2 * j + 1)])
    at = weave(at, [("csq", 0)])
    for i in range(8):
        at = weave(at, [[("cn", i)] + ([("csq", i + 1)] if i < 7 else [])])
    for u, (hg, m) in enumerate(UNITS):
        at = weave(at, [("ca", u), ("cg", u)])
        for lv in range(1, LEVELS):
            at = weave(at, [("ct", (u, lv)), ("cm", (u, lv)), ("cu", (u, lv))])
        at = weave(at, [("cv", u), ("ck", u) if m == 0 else ("cs", u), ("cr", u), ("co", u)])
    at = max(at, end("bkv", 512) + 1)
    at = weave(at, [("bn", 0)] + [("bt", i) for i in range(4)] + [("bkn", 0), ("bkt", 0)])
    assert at <= end("silu", W_A + 512 * 3) + 1, (at, end("silu", W_A + 512 * 3))
    at = weave(end("bi", 0) + 1, [("bit", 0)] + [("bsc", (0, p)) for p in range(4)])
    at = weave(max(at, end("bi", 1) + 1), [("bit", 1)] + [("bsc", (1, p)) for p in range(4)])
    at = weave(at, [("btk", (0, i)) for i in range(3)] + [("btk", (1, i)) for i in range(3)])
    assert at <= end("bq", 0) + 1
    for g in range(HKV):
        at = weave(end("bq", g) + 1, [("bqn", g), ("bqt", g)])
        for v in range(3):
            at = weave(at, [("bs", (g, v)), ("bp", (g, v)), ("bo", (g, v))])
    assert at <= end("aqk", 0)
    weave(end("aqk", 0) + 1, [("at", 0)])
    weave(end("aqk", 1) + 1, [("at", 1)])
    first = end("av", 1)
    woven[first] += [("yt", 4), ("yt", 5)]
    at = weave(first + 1, [("yt", i) for i in range(6, 16)])
    for h in range(H_A):
        at = weave(at, [("ae", h), ("ap", h)])
    at = weave(at, [("yt", i) for i in range(4)])
    assert at <= end("out1", 7)

    use, order = 0, {}
    for slot in woven:
        for i, (name, arg) in enumerate(slot):
            slot[i] = (name, arg, use)
            order[name] = order.get(name, 0) + 1
            use += USES.get(name, 0)
    return blocks, chunks, last, woven, use


def hybrid_kernel(nc, x, norm_g, w_in, w_out, m_ib, m_fb, m_norm_g, a_cq_g, a_wuq, a_wuqi, a_qn_g, a_kn_g,
                  a_ki_g, a_ki_b, d_conv_w, d_a_log, d_dt_bias, d_norm_g, out):
    blocks, chunks, last, woven, _ = plan()
    NX = 2 * KT // 4
    U0 = NX + 2

    matrix = {
        "w_in": w_in[0].rearrange("(kt p) n -> p kt n", p=P),
        "w_out": w_out[0].rearrange("(kt p) n -> p kt n", p=P),
        "wuq": a_wuq[0].rearrange("(kt p) n -> p kt n", p=P),
        "wuqi": a_wuqi[0].rearrange("(kt p) n -> p kt n", p=P),
    }
    x_dram = x[0].rearrange("(m p) d -> p m d", p=P)
    out_dram = out[0].rearrange("(m p) d -> p m d", p=P)

    with ExitStack() as ctx:
        def sb(name, shape, dt=F32, stack=ctx):
            return stack.enter_context(nc.sbuf_tensor(name, shape, dt))

        def sem(name):
            return ctx.enter_context(nc.semaphore(name))

        acc = [[ctx.enter_context(nc.psum_tensor(f"acc{b}{m}", [P, 512], F32)) for m in range(M)] for b in range(2)]
        mix = [ctx.enter_context(nc.psum_tensor(f"mix{b}", [P, 512], F32)) for b in range(4)]

        op_hi = sb("op_hi", [P, KT, SEQ], F32R)
        op_lo = sb("op_lo", [P, KT, SEQ], F32R)
        w_raw = sb("w_raw", [P, RAW_BUFS, 1024])
        w_hi = sb("w_hi", [P, SPLIT_BUFS, 1024], F32R)
        w_lo = sb("w_lo", [P, SPLIT_BUFS, 1024], F32R)
        y = sb("y", [P, M, D])
        kv = sb("kv", [P, M, 1024])
        sig = sb("sig", [P, M, 512])
        ident = sb("ident", [P, P])
        ones = sb("ones", [P, P])
        sel = sb("sel", [8, 8, P])
        level = sb("level", [P, LEVELS, P], BF16)
        tri = sb("tri", [P, 3, P], BF16)
        cap = sb("cap", [P, P], BF16)
        low = sb("low", [P, P], BF16)
        par = sb("par", [P, R_N + N_TAP])
        small = sb("small", [P, M, G_W])
        rows = sb("rows", [8, 6, SEQ])
        gcol = sb("gcol", [P, 9, 8])
        gder = sb("gder", [P, 6, 8])
        hcol = sb("hcol", [8, 8])
        eps = sb("eps", [P, 1])
        ssq = sb("ssq", [P, 8])
        rstd = sb("rstd", [P, 4])
        st = sb("st", [P, 48])
        kdup = sb("kdup", [P, M, P])
        kiT = sb("kiT", [P, SEQ])

        def region(names):
            with ExitStack() as stack:
                return [sb(n, s, d, stack) for n, s, d in names]

        xs, par_in, tap_in = region([("xs", [P, M, D], F32), ("par_in", [P, P], F32), ("tap_in", [P, P], F32)])
        cT, c_kb, c_gam, c_at, c_bt, c_u, c_v, c_kd, c_s = region(
            [("cT", [P, CH, SEQ], F32)] + [(n, [P, 4, P], F32) for n in
             ("c_kb", "c_gam", "c_at", "c_bt", "c_u", "c_v", "c_kd", "c_s")])
        cq_hi, cq_lo, qs, b_sq, b_qT, b_kT, sc, b_s, b_p, b_pT, top8 = region(
            [("cq_hi", [P, QKT, SEQ], F32R), ("cq_lo", [P, QKT, SEQ], F32R), ("qs", [P, M, 512], F32),
             ("b_sq", [P, 1024], F32), ("b_qT", [P, 4, SEQ], F32), ("b_kT", [P, HKV, SEQ], F32),
             ("sc", [P, 3 * P], F32), ("b_s", [P, 512], F32), ("b_p", [P, 512], F32),
             ("b_pT", [P, 4, P], F32), ("top8", [P, 8], F32)])
        a_s, a_qT, a_kT, a_v, a_m, a_p, a_h, a_sq, acc0 = region(
            [("a_s", [P, M, 512], F32), ("a_qT", [P, 4, SEQ], F32), ("a_kT", [P, 4, SEQ], F32),
             ("a_v", [P, M, H_A, HEAD + 1], F32), ("a_m", [P, 3 * P], F32), ("a_p", [P, 3 * P], F32),
             ("a_h", [P, M, P], F32), ("a_sq", [P, P], F32), ("acc0", [P, M, W_A], F32)])

        par_in_ready = sem("par_in_ready")
        x_ready = [sem(f"x_ready{q}") for q in range(4)]
        raw_ready = [sem(f"raw_ready{b}") for b in range(RAW_BUFS)]
        const_ready = sem("const_ready")
        pool_step = sem("pool_step")
        head_ready = sem("head_ready")
        x_hi_ready = sem("x_hi_ready")
        ss_ready = sem("ss_ready")
        rstd_ready = sem("rstd_ready")
        hi_ready = sem("hi_ready")
        lo_ready = sem("lo_ready")
        split_used = sem("split_used")
        acc_ready = sem("acc_ready")
        acc_read = [sem(f"acc_read{b}") for b in range(2)]
        filled = [sem(f"filled{b}") for b in range(4)]
        emptied = [sem(f"emptied{b}") for b in range(4)]
        act_step = sem("act_step")
        dve_step = sem("dve_step")
        sig_exp = sem("sig_exp")
        g_act = sem("g_act")
        g_dve = sem("g_dve")
        g_rows = sem("g_rows")
        g_cols = sem("g_cols")
        k_dve = sem("k_dve")
        k_act = sem("k_act")
        k_dup = sem("k_dup")
        conv_y = sem("conv_y")
        conv_exp = sem("conv_exp")
        conv_ready = sem("conv_ready")
        c_sq = sem("c_sq")
        c_r = sem("c_r")
        c_nd = sem("c_nd")
        c_gam_ready = sem("c_gam_ready")
        c_u0 = sem("c_u0")
        c_y = sem("c_y")
        c_osq = sem("c_osq")
        c_oss = sem("c_oss")
        c_or = sem("c_or")
        b_act = sem("b_act")
        b_dve = sem("b_dve")
        cq_norm = sem("cq_norm")
        cq_hi_ready = sem("cq_hi_ready")
        bk_norm = sem("bk_norm")
        b_score = sem("b_score")
        bq_norm = sem("bq_norm")
        b_max = sem("b_max")
        b_exp = sem("b_exp")
        a_one = sem("a_one")
        a_exp = sem("a_exp")
        a_y = sem("a_y")
        a_ss = sem("a_ss")
        y_hi_ready = sem("y_hi_ready")
        x_again = sem("x_again")
        out_done = sem("out_done")

        block = ctx.enter_context(nc.Block())

        def raw_dmas(c):
            b, kts = chunks[c]
            k0, n = kts[0], len(kts)
            blk = blocks[b]
            dst = w_raw[:, c % RAW_BUFS, 0:n * blk["width"]].rearrange("p (k n) -> p k n", k=n)
            src = matrix[blk["matrix"]][:, k0:k0 + n, :]
            if blk["kind"] == "gates":
                return [(dst[:, :, g:g + w], src[:, :, col:col + w]) for g, col, w in
                        ((G_AI, C_AI, 16), (G_CB, C_CB, 16), (G_KI, C_BKI, IDX_D + IDX_H))]
            return [(dst, src[:, :, blk["col"]:blk["col"] + blk["width"]])]

        def raw_count(c):
            return 16 * sum(3 if blocks[chunks[i][0]]["kind"] == "gates" else 1
                            for i in range(c % RAW_BUFS, c + 1, RAW_BUFS))

        def split_ap(tensor, c):
            b, kts = chunks[c]
            return tensor[:, c % SPLIT_BUFS, 0:len(kts) * blocks[b]["width"]]

        def bank(use):
            return mix[use % 4]

        def wait_filled(eng, use):
            eng.wait_ge(filled[use % 4], use // 4 + 1)

        def wait_emptied(eng, use):
            if use >= 4:
                eng.wait_ge(emptied[use % 4], use // 4)

        use_of = {(name, arg): U0 + use for slot in woven for name, arg, use in slot}

        def wait_read(eng, name, arg, i=0):
            use = use_of[name, arg] + i
            eng.wait_ge(emptied[use % 4], use // 4 + 1)

        def wait_stored(eng, kind, arg=0):
            b = next(i for i, x_ in enumerate(blocks) if x_["kind"] == kind and x_["arg"] == arg)
            eng.wait_ge(acc_read[b % 2], b // 2 + 1)

        def conv_stage(j):
            return y[:, :, W_A + 512 * (j % 2):W_A + 512 * (j % 2) + 512]

        def out_acc(n):
            return acc0[:, :, 512 * n:512 * n + 512] if n < 2 else y[:, :, 512 * n:512 * n + 512]

        def y_gain(kt):
            if kt < W_A // P:
                return par[:, R_MN + kt:R_MN + kt + 1]
            return par[:, R_DN:R_DN + 1] if kt >= (W_A + W_B) // P else None

        gate_order = [b for b, x_ in enumerate(blocks) if x_["kind"] in ("silu", "ao", "az")]
        @block.sync
        def _(sp):
            for r, a in ((R_NORM, norm_g[0].rearrange("(r p) -> r p", p=P)),
                         (R_CQ, a_cq_g[0].rearrange("(r p) -> r p", p=P)), (R_QN, a_qn_g), (R_KN, a_kn_g),
                         (R_MN, m_norm_g[0].rearrange("(r p) -> r p", p=P)), (R_DN, d_norm_g)):
                sp.dma_start(par_in[r:r + a.shape[0], :], a).then_inc(par_in_ready, 16)
            for r, a in ((R_KIG, a_ki_g), (R_KIB, a_ki_b)):
                for i in range(2):
                    sp.dma_start(par_in[r:r + 1, i * IDX_D:(i + 1) * IDX_D], a).then_inc(par_in_ready, 16)
            sp.dma_start(tap_in[0:N_TAP, :], d_conv_w[0].rearrange("t (c p) -> (t c) p", p=P)).then_inc(
                par_in_ready, 16)
            for i, a in enumerate((m_ib, m_fb, d_a_log, d_dt_bias)):
                sp.dma_start(hcol[:, i:i + 1], a.rearrange("o h -> h o")).then_inc(par_in_ready, 16)
            for q in range(4):
                sp.dma_start(xs[:, :, 1024 * q:1024 * q + 1024], x_dram[:, :, 1024 * q:1024 * q + 1024]).then_inc(
                    x_ready[q], 16)
            for c in range(len(chunks)):
                if c >= RAW_BUFS:
                    sp.wait_ge(lo_ready, c - RAW_BUFS + 1)
                for dst, src in raw_dmas(c):
                    sp.dma_start(dst, src).then_inc(raw_ready[c % RAW_BUFS], 16)

        PAR_DMAS = 16 * 15

        @block.gpsimd
        def _(pool):
            steps = [0]

            def step(ins):
                steps[0] += 1
                ins.then_inc(pool_step, 1)
                pool.wait_ge(pool_step, steps[0])

            def select(view, op, fill, base, pattern, cm):
                step(nc.gpsimd.affine_select(out=view, in_=view, compare_op=op, fill=fill, base=base,
                                             pattern=pattern, channel_multiplier=cm))

            step(nc.gpsimd.memset(ident[:], 0.0))
            select(ident[:], ALU.not_equal, 1.0, 0, [[-1, P]], 1)
            step(nc.gpsimd.memset(ones[:], 1.0))
            step(nc.gpsimd.memset(eps[:], EPS))
            nc.gpsimd.memset(st[:], 0.0).then_inc(const_ready, 1)
            step(nc.gpsimd.memset(sel[:], 0.0))
            select(sel[:], ALU.not_equal, 1.0, 0, [[-1, 8], [0, P]], 1)
            step(nc.gpsimd.memset(tri[:], 0.0))
            for i in (0, 2):
                select(tri[:, i, :], ALU.is_ge, NEG, 0, [[1, P]], -1)
            step(nc.gpsimd.memset(cap[:], BIG))
            select(cap[:], ALU.is_ge, -BIG, 0, [[-1, P]], 1)
            step(nc.gpsimd.memset(low[:], 0.0))
            select(low[:], ALU.is_ge, NEG, 0, [[-1, P]], 1)
            step(nc.gpsimd.memset(level[:], 0.0))
            select(level[:, 0, :].rearrange("p (j c) -> p j c", c=2)[:, :, 1], ALU.not_equal, 1.0, 0,
                   [[-2, P // 2]], 1)
            for lv in range(1, LEVELS):
                b = 1 << lv
                n = P // (2 * b)
                v = level[:, lv, :].rearrange("p (j c r) -> p j c r", c=2, r=b)[:, :, 0, :]
                step(nc.gpsimd.memset(v, 1.0))
                select(v, ALU.is_ge, 0.0, -b, [[-2 * b, n], [0, b]], 1)
                select(v, ALU.is_ge, 0.0, 2 * b - 1, [[2 * b, n], [0, b]], -1)
            nc.gpsimd.engine_nop().then_inc(const_ready, 1)
            for i in range(12, 16):
                wait_read(pool, "yt", i)
            for n in range(D // 512):
                pool.dma_start(out_acc(n), x_dram[:, :, 512 * n:512 * n + 512]).then_inc(x_again, 16)
            for n in range(D // 512):
                wait_stored(pool, "out2", n)
                pool.dma_start(out_dram[:, :, 512 * n:512 * n + 512], out_acc(n)).then_inc(out_done, 16)
            pool.wait_ge(out_done, 16 * (D // 512))

        @block.tensor
        def _(pe):
            def end_fill(ins, use):
                ins.then_inc(filled[use % 4], 1)

            def turn(dst, src, n=P):
                return nc.tensor.transpose(dst, src, ident[0:n, 0:n])

            def chunk(c):
                b, kts = chunks[c]
                blk = blocks[b]
                w = blk["width"]
                if kts[0] == blk["kts"][0] and b >= 2:
                    pe.wait_ge(acc_read[b % 2], b // 2)
                pe.wait_ge(lo_ready, c + 1)
                hi, lo = {"h": (op_hi, op_lo), "cq": (cq_hi, cq_lo), "y": (op_hi, op_lo)}[blk["operand"]]
                hv = split_ap(w_hi, c).rearrange("p (k n) -> p k n", k=len(kts))
                lv = split_ap(w_lo, c).rearrange("p (k n) -> p k n", k=len(kts))
                for i, kt in enumerate(kts):
                    if b == 0:
                        use = 2 + kt // 2
                        pe.wait_ge(emptied[use % 4], use // 4 + 1)
                    if blk["operand"] == "cq":
                        wait_read(pe, "bt", kt // 2)
                    if blk["kind"] in ("out1", "out2") and blk["arg"] == 0:
                        wait_read(pe, "yt", kt // 2)
                    for m in range(M):
                        o = acc[b % 2][m][:, 0:w]
                        tok = slice(m * P, m * P + P)
                        nc.tensor.matmul(o, hi[:, kt, tok], hv[:, i, :], start=(kt == blk["kts"][0]), stop=False)
                        nc.tensor.matmul(o, hi[:, kt, tok], lv[:, i, :], start=False, stop=False)
                        last_mm = nc.tensor.matmul(o, lo[:, kt, tok], hv[:, i, :], start=False,
                                                   stop=(kt == blk["kts"][-1]))
                if c == last[b]:
                    last_mm.then_inc(acc_ready, 1)
                    pe_done[0] += 1
                else:
                    last_mm.then_inc(split_used, 1)

            pe_done = [0]

            def gt(_, use):
                wait_stored(pe, "gates")
                for i in range(4):
                    u = use + i // 2
                    if i % 2 == 0:
                        wait_emptied(pe, u)
                    for m in range(M):
                        ins = turn(bank(u)[0:8, (i % 2) * SEQ + m * P:(i % 2) * SEQ + m * P + P],
                                   small[:, m, 8 * i:8 * i + 8])
                    if i % 2:
                        end_fill(ins, u)

            def gb(_, use):
                pe.wait_ge(g_rows, 2)
                wait_emptied(pe, use)
                for i, (r, m) in enumerate(((2, 0), (2, 1), (3, 0), (3, 1), (5, 0), (0, 0), (0, 1), (4, 0), (4, 1))):
                    ins = turn(bank(use)[:, 8 * i:8 * i + 8], rows[:, r, m * P:m * P + P], 8)
                end_fill(ins, use)

            def kx(_, use):
                pe.wait_ge(k_dup, 1)
                wait_emptied(pe, use)
                for m in range(M):
                    ins = turn(bank(use)[:, m * P:m * P + P], kdup[:, m, :])
                end_fill(ins, use)

            def conv(i, use):
                wait_stored(pe, "conv", i // 2)
                wait_emptied(pe, use)
                for j in range(2):
                    for m in range(M):
                        ins = turn(bank(use)[:, j * SEQ + m * P:j * SEQ + m * P + P],
                                   conv_stage(i // 2)[:, m, (i % 2) * SEQ + j * P:(i % 2) * SEQ + j * P + P])
                end_fill(ins, use)

            def cn(i, use):
                pe.wait_ge(c_sq, i + 1)
                wait_emptied(pe, use)
                end_fill(nc.tensor.matmul(bank(use)[:], ones[:], c_kb[:].rearrange("p a b -> p (a b)"),
                                          start=True, stop=True), use)

            def ca(u, use):
                hg, m = UNITS[u]
                for i, r in enumerate((3, 2)):
                    wait_emptied(pe, use + i)
                    for a in range(4):
                        ins = nc.tensor.matmul(bank(use + i)[:, a * P:a * P + P], sel[:, 4 * hg + a, :],
                                               rows[:, r, m * P:m * P + P], start=True, stop=True)
                    end_fill(ins, use + i)

            def cg(u, use):
                hg, m = UNITS[u]
                tok = slice(m * P, m * P + P)
                wait_read(pe, "ca", u)
                for i in range(2):
                    wait_emptied(pe, use + i)
                    for a in range(4):
                        h = 4 * hg + a
                        ins = nc.tensor.matmul(bank(use + i)[:, a * P:a * P + P], cT[:, 8 + h, tok],
                                               c_kb[:, a, :] if i == 0 else cT[:, h, tok], start=True, stop=True)
                    end_fill(ins, use + i)

            def ct(arg, use):
                u, lv = arg
                if lv == 1:
                    pe.wait_ge(c_u0, u + 1)
                else:
                    wait_read(pe, "cu", (u, lv - 1))
                wait_emptied(pe, use)
                for a in range(4):
                    ins = turn(bank(use)[:, a * P:a * P + P], c_u[:, a, :])
                end_fill(ins, use)

            def heads4(use, lhs, rhs):
                wait_emptied(pe, use)
                for a in range(4):
                    ins = nc.tensor.matmul(bank(use)[:, a * P:a * P + P], lhs(a), rhs(a), start=True, stop=True)
                end_fill(ins, use)

            def cm(arg, use):
                u, lv = arg
                wait_read(pe, "ct", arg)
                heads4(use, lambda a: c_at[:, a, :], lambda a: c_gam[:, a, :])

            def cu(arg, use):
                u, lv = arg
                wait_read(pe, "cm", arg)
                heads4(use, lambda a: c_kb[:, a, :], lambda a: c_u[:, a, :])

            def cv(u, use):
                hg, m = UNITS[u]
                wait_emptied(pe, use)
                for a in range(4):
                    ins = turn(bank(use)[:, a * P:a * P + P], cT[:, 16 + 4 * hg + a, m * P:m * P + P])
                end_fill(ins, use)

            def ck(u, use):
                hg, m = UNITS[u]
                wait_emptied(pe, use)
                for a in range(4):
                    ins = turn(bank(use)[:, a * P:a * P + P], cT[:, 8 + 4 * hg + a, m * P:m * P + P])
                end_fill(ins, use)

            def cs(u, use):
                hg, m = UNITS[u]
                wait_read(pe, "co", u - 1, 1)
                heads4(use, lambda a: cT[:, 8 + 4 * hg + a, m * P:m * P + P], lambda a: c_s[:, a, :])

            def cr(u, use):
                wait_read(pe, "cu", (u, LEVELS - 1))
                wait_read(pe, "cv" if UNITS[u][1] == 0 else "cs", u)
                heads4(use, lambda a: c_u[:, a, :], lambda a: c_v[:, a, :])

            def co(u, use):
                hg, m = UNITS[u]
                wait_read(pe, "cr", u)
                heads4(use, lambda a: c_bt[:, a, :], lambda a: c_v[:, a, :])
                if m == 0:
                    wait_read(pe, "ck", u)
                    heads4(use + 1, lambda a: c_kd[:, a, :], lambda a: c_v[:, a, :])
                else:
                    heads4(use + 1, lambda a: cT[:, 4 * hg + a, m * P:m * P + P], lambda a: c_s[:, a, :])

            def bt(i, use):
                pe.wait_ge(cq_norm, 2)
                wait_emptied(pe, use)
                for j in range(min(2, QKT - 2 * i)):
                    for m in range(M):
                        ins = turn(bank(use)[:, j * SEQ + m * P:j * SEQ + m * P + P],
                                   y[:, m, (2 * i + j) * P:(2 * i + j) * P + P])
                end_fill(ins, use)

            def turn8(use, src):
                for i in range(4):
                    u = use + i // 2
                    if i % 2 == 0:
                        wait_emptied(pe, u)
                    for m in range(M):
                        ins = turn(bank(u)[:, (i % 2) * SEQ + m * P:(i % 2) * SEQ + m * P + P],
                                   src[:, m, i * P:i * P + P])
                    if i % 2:
                        end_fill(ins, u)

            def bkt(_, use):
                pe.wait_ge(bk_norm, 2)
                turn8(use, kv[:, :, 0:512])

            def bit(j, use):
                wait_stored(pe, "bi", j)
                turn8(use, qs)

            def bsc(arg, use):
                j, p = arg
                wait_read(pe, "kx", 0)
                wait_read(pe, "bit", j, p // 2)
                for s in range(2):
                    half = slice(64 * s, 64 * s + 64)
                    wait_emptied(pe, use + s)
                    nc.tensor.matmul(bank(use + s)[:, 0:P], b_qT[half, p, 0:P], kiT[half, 0:P], start=True,
                                     stop=True)
                    end_fill(nc.tensor.matmul(bank(use + s)[:, P:3 * P], b_qT[half, p, P:SEQ], kiT[half, :],
                                              start=True, stop=True), use + s)

            def bqt(g, use):
                pe.wait_ge(bq_norm, 2 * (g + 1))
                turn8(use, qs)

            def bs(arg, use):
                g, v = arg
                for i in range(2):
                    wait_read(pe, "bkt", 0, i)
                    wait_read(pe, "bqt", g, i)
                wait_emptied(pe, use)
                for i in range(4 if v == 0 else 2):
                    if v == 0:
                        ins = nc.tensor.matmul(bank(use)[:, i * P:i * P + P], b_qT[:, i, 0:P], b_kT[:, g, 0:P],
                                               start=True, stop=True)
                    else:
                        ins = nc.tensor.matmul(bank(use)[:, i * SEQ:i * SEQ + SEQ], b_qT[:, 2 * v - 2 + i, P:SEQ],
                                               b_kT[:, g, :], start=True, stop=True)
                end_fill(ins, use)

            def bp(arg, use):
                g, v = arg
                pe.wait_ge(b_exp, 3 * g + v + 1)
                wait_emptied(pe, use)
                for i in range(4):
                    ins = turn(bank(use)[:, i * P:i * P + P], b_p[:, i * P:i * P + P])
                end_fill(ins, use)

            def bo(arg, use):
                g, v = arg
                wait_read(pe, "bp", arg)
                wait_emptied(pe, use)
                for i in range(4):
                    val = kv[:, 0 if v == 0 else i % 2, 512 + g * P:512 + g * P + P]
                    o = i if v == 0 else i // 2
                    ins = nc.tensor.matmul(bank(use)[:, o * P:o * P + P], b_pT[:, i, :], val,
                                           start=(v == 0 or i % 2 == 0), stop=(v == 0 or i % 2 == 1))
                end_fill(ins, use)

            def at(j, use):
                wait_stored(pe, "aqk", j)
                turn8(use, a_s)

            def ae(h, use):
                half = slice(64 * (h % 2), 64 * (h % 2) + 64)
                for i in range(2):
                    wait_read(pe, "at", 0, i)
                    wait_read(pe, "at", 1, i)
                for i in range(2):
                    wait_emptied(pe, use + i)
                    b = bank(use + i)
                    if i == 0:
                        nc.tensor.matmul(b[:, 0:SEQ], sel[:, h, :], rows[:, 1, :], start=True, stop=True)
                        ins = nc.tensor.matmul(b[:, SEQ:3 * P], sel[:, h, :], rows[:, 1, P:SEQ], start=True,
                                               stop=True)
                    else:
                        nc.tensor.matmul(b[:, 0:SEQ], a_kT[half, h // 2, 0:P], a_qT[half, h // 2, :], start=True,
                                         stop=True)
                        ins = nc.tensor.matmul(b[:, SEQ:3 * P], a_kT[half, h // 2, P:SEQ],
                                               a_qT[half, h // 2, P:SEQ], start=True, stop=True)
                    end_fill(ins, use + i)

            def ap(h, use):
                wait_read(pe, "ae", h, 1)
                pe.wait_ge(a_one, 1)
                wait_stored(pe, "av", 1)
                wait_emptied(pe, use)
                w = HEAD + 1
                b = bank(use)
                nc.tensor.matmul(b[:, 0:w], a_p[:, 0:P], a_v[:, 0, h, :], start=True, stop=True)
                nc.tensor.matmul(b[:, 256:256 + w], a_p[:, P:2 * P], a_v[:, 0, h, :], start=True, stop=False)
                end_fill(nc.tensor.matmul(b[:, 256:256 + w], a_p[:, 2 * P:3 * P], a_v[:, 1, h, :], start=False,
                                          stop=True), use)

            def yt(i, use):
                if i < 4:
                    pe.wait_ge(a_y, H_A)
                elif i < 12:
                    wait_read(pe, "bo", (HKV - 1, 2))
                else:
                    pe.wait_ge(c_y, len(UNITS))
                wait_emptied(pe, use)
                for j in range(2):
                    for m in range(M):
                        ins = turn(bank(use)[:, j * SEQ + m * P:j * SEQ + m * P + P],
                                   y[:, m, (2 * i + j) * P:(2 * i + j) * P + P])
                end_fill(ins, use)

            pieces = dict(gt=gt, gb=gb, kx=kx, conv=conv, cn=cn, ca=ca, cg=cg, ct=ct, cm=cm, cu=cu, cv=cv, ck=ck,
                          cs=cs, cr=cr, co=co, bt=bt, bkt=bkt, bit=bit, bsc=bsc, bqt=bqt, bs=bs, bp=bp, bo=bo,
                          at=at, ae=ae, ap=ap, yt=yt)

            pe.wait_ge(const_ready, 1)
            pe.wait_ge(par_in_ready, PAR_DMAS)
            end_fill(turn(bank(0)[:, 0:R_N], par_in[0:R_N, :], R_N), 0)
            end_fill(turn(bank(1)[:, 0:N_TAP], tap_in[0:N_TAP, :], N_TAP), 1)
            for i in range(NX):
                use = 2 + i
                pe.wait_ge(x_ready[i // 4], 16)
                wait_emptied(pe, use)
                for j in range(2):
                    for m in range(M):
                        ins = turn(bank(use)[:, j * SEQ + m * P:j * SEQ + m * P + P],
                                   xs[:, m, (2 * i + j) * P:(2 * i + j) * P + P])
                end_fill(ins, use)
            for c in range(len(chunks)):
                chunk(c)
                if c == 4:
                    pe.wait_ge(const_ready, 2)
                for name, arg, use in woven[c]:
                    if name in pieces:
                        pieces[name](arg, U0 + use)

        @block.scalar
        def _(act):
            steps = [0]
            func = nc.scalar.activation

            def step(ins):
                steps[0] += 1
                ins.then_inc(act_step, 1)
                act.wait_ge(act_step, steps[0])

            def done_bank(ins, use):
                ins.then_inc(emptied[use % 4], 1)

            def split_hi(c):
                act.wait_ge(raw_ready[c % RAW_BUFS], raw_count(c))
                if c >= SPLIT_BUFS:
                    d = c - SPLIT_BUFS
                    b = chunks[d][0]
                    if d == last[b]:
                        act.wait_ge(acc_ready, b + 1)
                    else:
                        act.wait_ge(split_used, d + 1 - b)
                n = len(chunks[c][1]) * blocks[chunks[c][0]]["width"]
                func(split_ap(w_hi, c), w_raw[:, c % RAW_BUFS, 0:n], ACT.Copy).then_inc(hi_ready, 1)

            def rsqrt_mean(out_, in_, n):
                step(func(out_, in_, ACT.Ln, bias=eps[:], scale=1.0 / n))
                return func(out_, out_, ACT.Exp, scale=-0.5)

            def evac(b, _):
                blk = blocks[b]
                kind, arg, w = blk["kind"], blk["arg"], blk["width"]
                if kind in ("out1", "out2"):
                    return
                if b == 0:
                    act.wait_ge(ss_ready, 9)
                    step(func(rstd[:, 0:2], ssq[:, 0:2], ACT.Ln, bias=eps[:], scale=1.0 / D))
                    step(func(rstd[:, 0:2], rstd[:, 0:2], ACT.Exp, scale=-0.5))
                    func(rstd[:, 2:4], rstd[:, 0:2], ACT.Copy, scale=-1.0).then_inc(rstd_ready, 1)
                    act.wait_ge(rstd_ready, 1)
                act.wait_ge(acc_ready, b + 1)
                if kind in ("silu", "ao", "az"):
                    n = gate_order.index(b)
                    if n:
                        before = gate_order[n - 1]
                        act.wait_ge(acc_read[before % 2], before // 2 + 1)
                    for m in range(M):
                        ins = func(sig[:, m, :], acc[b % 2][m][:], ACT.Exp, scale=rstd[:, 2 + m:3 + m])
                    ins.then_inc(sig_exp, 1)
                    return
                for m in range(M):
                    src = acc[b % 2][m][:, 0:w]
                    if kind == "gates":
                        dst = small[:, m, :]
                    elif kind == "conv":
                        dst = conv_stage(arg)[:, m, :]
                    elif kind == "cq":
                        dst = y[:, m, arg:arg + w]
                    elif kind == "bkv":
                        dst = kv[:, m, arg:arg + w]
                    elif kind in ("bi", "bq"):
                        dst = qs[:, m, :]
                    elif kind == "aqk":
                        dst = a_s[:, m, :]
                    else:
                        dst = a_v[:, m, 4 * arg:4 * arg + 4, 0:HEAD]
                        src = src.rearrange("p (h d) -> p h d", h=4)
                    if kind in ("bi", "bq"):
                        ins = func(dst, src, ACT.Copy)
                    else:
                        ins = func(dst, src, ACT.Copy, scale=rstd[:, m:m + 1])
                    if m == 0:
                        step(ins)
                ins.then_inc(acc_read[b % 2], 1)

            def gt(_, use):
                wait_filled(act, use)
                act.wait_ge(head_ready, 1)
                b = bank(use)
                func(rows[:, 0, :], b[0:8, 0:SEQ], ACT.Tanh, bias=hcol[:, 4:5], scale=1 / GATE_CAP).then_inc(g_act, 1)
                done_bank(func(rows[:, 1, :], b[0:8, SEQ:2 * SEQ], ACT.Tanh, bias=hcol[:, 5:6],
                               scale=1 / GATE_CAP), use)
                act.wait_ge(emptied[use % 4], use // 4 + 1)
                step(func(rows[:, 1, :], rows[:, 1, :], ACT.Exp, scale=-GATE_CAP))
                func(rows[:, 1, :], rows[:, 1, :], ACT.Ln, bias=1.0).then_inc(g_act, 1)
                wait_filled(act, use + 1)
                b = bank(use + 1)
                func(rows[:, 3, :], b[0:8, 0:SEQ], ACT.Exp, scale=-1.0).then_inc(g_act, 1)
                done_bank(func(rows[:, 2, :], b[0:8, SEQ:2 * SEQ], ACT.Identity, bias=hcol[:, 3:4]), use + 1)
                act.wait_ge(g_dve, 1)
                step(func(rows[:, 4, :], rows[:, 4, :], ACT.Exp, scale=-1.0))
                func(rows[:, 4, :], rows[:, 4, :], ACT.Ln, bias=1.0).then_inc(g_act, 1)

            def gs(_, use):
                act.wait_ge(g_dve, 2)
                func(rows[:, 5, 0:P], rows[:, 2, 0:P], ACT.Exp, bias=rows[:, 2, P - 1:P], scale=-1.0).then_inc(
                    g_rows, 1)
                act.wait_ge(g_dve, 3)
                func(rows[:, 4, :], rows[:, 4, :], ACT.Exp).then_inc(g_rows, 1)

            def gb(_, use):
                act.wait_ge(g_cols, 1)
                func(gder[:, 2:4, :], gcol[:, 0:2, :], ACT.Exp).then_inc(g_cols, 1)

            def kx(_, use):
                act.wait_ge(k_dve, 1)
                step(func(st[:, 20:22], st[:, 20:22], ACT.Ln, bias=eps[:]))
                func(st[:, 20:22], st[:, 20:22], ACT.Exp, scale=-0.5).then_inc(k_act, 1)

            def conv(i, use):
                wait_filled(act, use)
                for j in range(2):
                    c = 2 * i + j
                    ins = func(cT[:, c, :], bank(use)[:, j * SEQ:j * SEQ + SEQ], ACT.Copy,
                               scale=par[:, R_N + 3 * CH + c:R_N + 3 * CH + c + 1])
                ins.then_inc(conv_y, 1)
                wait_read(act, "conv", i)
                if i:
                    act.wait_ge(conv_ready, i)
                func(c_kb[:].rearrange("p a b -> p (a b)"), cT[:, 2 * i:2 * i + 2, :].rearrange("p c t -> p (c t)"),
                     ACT.Exp, scale=-1.0).then_inc(conv_exp, 1)

            def csq(i, use):
                act.wait_ge(conv_ready, 12)
                func(c_kb[:].rearrange("p a b -> p (a b)"), cT[:, 2 * i:2 * i + 2, :].rearrange("p c t -> p (c t)"),
                     ACT.Square).then_inc(c_sq, 1)

            def cn(i, use):
                wait_filled(act, use)
                if i:
                    act.wait_ge(c_nd, i)
                g = c_gam[:].rearrange("p a b -> p (a b)")
                done_bank(func(g, bank(use)[:], ACT.Ln, bias=eps[:]), use)
                act.wait_ge(emptied[use % 4], use // 4 + 1)
                func(g, g, ACT.Exp, scale=-0.5).then_inc(c_r, 1)

            def ca(u, use):
                hg, m = UNITS[u]
                wait_read(act, "ca", u, 1)
                act.wait_ge(g_cols, 3)
                for a in range(4):
                    ins = func(c_gam[:, a, :], c_gam[:, a, :], ACT.Exp, bias=gder[:, m, 4 * hg + a:4 * hg + a + 1])
                ins.then_inc(c_gam_ready, 1)

            def ct(arg, use):
                wait_filled(act, use)
                done_bank(func(c_gam[:].rearrange("p a b -> p (a b)"), bank(use)[:], ACT.Copy), use)

            def cv(u, use):
                hg, m = UNITS[u]
                wait_filled(act, use)
                for a in range(4):
                    ins = func(c_v[:, a, :], bank(use)[:, a * P:a * P + P], ACT.Copy,
                               scale=gcol[:, 2 + m, 4 * hg + a:4 * hg + a + 1])
                done_bank(ins, use)

            def ck(u, use):
                hg, m = UNITS[u]
                wait_filled(act, use)
                for a in range(4):
                    ins = func(c_kd[:, a, :], bank(use)[:, a * P:a * P + P], ACT.Copy,
                               scale=gcol[:, 4, 4 * hg + a:4 * hg + a + 1])
                done_bank(ins, use)

            def cr(u, use):
                wait_filled(act, use)
                done_bank(func(c_v[:].rearrange("p a b -> p (a b)"), bank(use)[:], ACT.Copy), use)

            def co(u, use):
                hg, m = UNITS[u]
                wait_filled(act, use + 1)
                if m == 0:
                    done_bank(func(c_s[:].rearrange("p a b -> p (a b)"), bank(use + 1)[:], ACT.Copy), use + 1)
                    act.wait_ge(emptied[(use + 1) % 4], (use + 1) // 4 + 1)
                else:
                    for a in range(4):
                        ins = func(c_kb[:, a, :], bank(use + 1)[:, a * P:a * P + P], ACT.Copy,
                                   scale=gder[:, 2 + m, 4 * hg + a:4 * hg + a + 1])
                    done_bank(ins, use + 1)
                wait_read(act, "co", u)
                func(c_gam[:].rearrange("p a b -> p (a b)"), c_at[:].rearrange("p a b -> p (a b)"),
                     ACT.Square).then_inc(c_osq, 1)
                act.wait_ge(c_oss, u + 1)
                rsqrt_mean(st[:, 0:4], st[:, 0:4], HEAD).then_inc(c_or, 1)

            def bn(_, use):
                wait_stored(act, "cq", 512)
                for m in range(M):
                    ins = func(b_sq[:, 0:Q_LORA], y[:, m, 0:Q_LORA], ACT.Square, accum_out=st[:, 4 + m:5 + m])
                    step(ins)
                rsqrt_mean(st[:, 4:6], st[:, 4:6], Q_LORA).then_inc(b_act, 1)

            def bt(i, use):
                wait_filled(act, use)
                for j in range(min(2, QKT - 2 * i)):
                    kt = 2 * i + j
                    ins = func(cq_hi[:, kt, :], bank(use)[:, j * SEQ:j * SEQ + SEQ], ACT.Copy,
                               scale=par[:, R_CQ + kt:R_CQ + kt + 1])
                ins.then_inc(cq_hi_ready, 1)

            def head_norms(n):
                for m in range(M):
                    src = kv[:, m, 0:512] if n == 0 else qs[:, m, :]
                    func(b_sq[:, m * 512:m * 512 + 512], src, ACT.Square).then_inc(b_act, 1)
                act.wait_ge(b_dve, n + 1)
                rsqrt_mean(st[:, 8:16], st[:, 8:16], HEAD).then_inc(b_act, 1)

            def bkn(_, use):
                wait_stored(act, "bkv", 0)
                head_norms(0)

            def bqn(g, use):
                wait_stored(act, "bq", g)
                head_norms(g + 1)

            def bkt(_, use):
                for i in range(2):
                    wait_filled(act, use + i)
                    done_bank(func(b_kT[:, 2 * i:2 * i + 2, :].rearrange("p a b -> p (a b)"), bank(use + i)[:],
                                   ACT.Copy, scale=par[:, R_KN:R_KN + 1]), use + i)

            def bit(j, use):
                for i in range(2):
                    wait_filled(act, use + i)
                    done_bank(func(b_qT[:, 2 * i:2 * i + 2, :].rearrange("p a b -> p (a b)"), bank(use + i)[:],
                                   ACT.Copy), use + i)

            def bsc(arg, use):
                j, p = arg
                for s in range(2):
                    h = 8 * j + 2 * p + s
                    wait_filled(act, use + s)
                    if h >= 2:
                        act.wait_ge(b_score, h - 1)
                    rl = (b_s, b_p)[s][:, 0:3 * P]
                    done_bank(func(rl, bank(use + s)[:, 0:3 * P], ACT.Relu), use + s)

            def bqt(g, use):
                for i in range(2):
                    wait_filled(act, use + i)
                    done_bank(func(b_qT[:, 2 * i:2 * i + 2, :].rearrange("p a b -> p (a b)"), bank(use + i)[:],
                                   ACT.Copy, scale=par[:, R_QN:R_QN + 1]), use + i)

            def bs(arg, use):
                g, v = arg
                n, w = (4, P) if v == 0 else (2, SEQ)
                act.wait_ge(b_max, 3 * g + v + 1)
                for i in range(n):
                    ins = func(b_p[:, i * w:i * w + w], b_s[:, i * w:i * w + w], ACT.Exp,
                               bias=st[:, 24 + i:25 + i], scale=HEAD ** -0.5, accum_out=st[:, 28 + i:29 + i])
                ins.then_inc(b_exp, 1)

            def bp(arg, use):
                wait_filled(act, use)
                done_bank(func(b_pT[:].rearrange("p a b -> p (a b)"), bank(use)[:], ACT.Copy), use)

            def at(j, use):
                dst = (a_qT, a_kT)[j]
                for i in range(2):
                    wait_filled(act, use + i)
                    done_bank(func(dst[:, 2 * i:2 * i + 2, :].rearrange("p a b -> p (a b)"), bank(use + i)[:],
                                   ACT.Copy, scale=(DQK ** -0.5, 1.0)[j]), use + i)

            def ae(h, use):
                wait_read(act, "ae", h)
                func(a_m[:, 0:SEQ], a_m[:, 0:SEQ], ACT.Exp, bias=gcol[:, 5, h:h + 1])
                func(a_m[:, SEQ:3 * P], a_m[:, SEQ:3 * P], ACT.Exp, bias=gcol[:, 6, h:h + 1]).then_inc(a_exp, 1)

            def ap(h, use):
                wait_read(act, "ap", h)
                for m in range(M):
                    step(func(a_sq[:], a_h[:, m, :], ACT.Square, accum_out=st[:, 36 + m:37 + m]))
                rsqrt_mean(st[:, 36:38], st[:, 36:38], HEAD).then_inc(a_ss, 1)

            def yt(i, use):
                wait_filled(act, use)
                for j in range(2):
                    kt = 2 * i + j
                    gain = y_gain(kt)
                    ins = func(op_hi[:, kt, :], bank(use)[:, j * SEQ:j * SEQ + SEQ], ACT.Copy,
                               scale=1.0 if gain is None else gain)
                ins.then_inc(y_hi_ready, 1)

            pieces = dict(evac=evac, gt=gt, gs=gs, gb=gb, kx=kx, conv=conv, csq=csq, cn=cn, ca=ca, ct=ct, cv=cv,
                          ck=ck, cr=cr, co=co, bn=bn, bt=bt, bkn=bkn, bqn=bqn, bkt=bkt, bit=bit, bsc=bsc, bqt=bqt,
                          bs=bs, bp=bp, at=at, ae=ae, ap=ap, yt=yt)

            act.wait_ge(const_ready, 1)
            act.wait_ge(par_in_ready, PAR_DMAS)
            func(hcol[:, 4:6], hcol[:, 0:2], ACT.Copy, scale=1 / GATE_CAP)
            func(hcol[:, 6:7], hcol[:, 2:3], ACT.Exp).then_inc(head_ready, 1)
            for i in range(2):
                act.wait_ge(emptied[i], 1)
            for i in range(NX):
                use = 2 + i
                wait_filled(act, use)
                for j in range(2):
                    kt = 2 * i + j
                    ins = func(op_hi[:, kt, :], bank(use)[:, j * SEQ:j * SEQ + SEQ], ACT.Copy,
                               scale=par[:, R_NORM + kt:R_NORM + kt + 1])
                ins.then_inc(x_hi_ready, 1)
                if i == NX // 2:
                    split_hi(0)
            for c in range(1, AHEAD):
                split_hi(c)
            for q in range(4):
                for m in range(M):
                    func(y[:, m, 1024 * q:1024 * q + 1024], xs[:, m, 1024 * q:1024 * q + 1024], ACT.Square,
                         accum_out=ssq[:, 2 * q + m:2 * q + m + 1]).then_inc(ss_ready, 1)
            for c in range(len(chunks)):
                if c + AHEAD < len(chunks):
                    split_hi(c + AHEAD)
                for name, arg, use in woven[c]:
                    if name in pieces:
                        pieces[name](arg, U0 + use)

        @block.vector
        def _(dve):
            steps = [0]
            vec = nc.vector

            def step(ins):
                steps[0] += 1
                ins.then_inc(dve_step, 1)
                dve.wait_ge(dve_step, steps[0])

            def done_bank(ins, use):
                ins.then_inc(emptied[use % 4], 1)

            def split_lo(c):
                dve.wait_ge(hi_ready, c + 1)
                n = len(chunks[c][1]) * blocks[chunks[c][0]]["width"]
                vec.tensor_tensor(split_ap(w_lo, c), w_raw[:, c % RAW_BUFS, 0:n], split_ap(w_hi, c).bitcast(F32),
                                  ALU.subtract).then_inc(lo_ready, 1)

            def evac(b, _):
                blk = blocks[b]
                kind, arg = blk["kind"], blk["arg"]
                if kind == "out1":
                    dve.wait_ge(acc_ready, b + 1)
                    dve.wait_ge(x_again, 16 * (D // 512))
                    for m in range(M):
                        ins = vec.tensor_tensor(out_acc(arg)[:, m, :], acc[b % 2][m][:], out_acc(arg)[:, m, :],
                                                ALU.add)
                        if m == 0:
                            step(ins)
                    ins.then_inc(acc_read[b % 2], 1)
                elif kind == "out2":
                    dve.wait_ge(acc_ready, b + 1)
                    for m in range(M):
                        ins = vec.tensor_tensor(out_acc(arg)[:, m, :], acc[b % 2][m][:], out_acc(arg)[:, m, :],
                                                ALU.add)
                        if m == 0:
                            step(ins)
                    ins.then_inc(acc_read[b % 2], 1)
                elif kind in ("silu", "ao", "az"):
                    dve.wait_ge(sig_exp, gate_order.index(b) + 1)
                    for m in range(M):
                        s = sig[:, m, :]
                        dst = y[:, m, arg:arg + 512]
                        step(vec.tensor_scalar(s, s, 1.0, None, ALU.add))
                        if kind == "ao":
                            ins = vec.reciprocal(dst, s)
                        else:
                            step(vec.reciprocal(s, s))
                            if kind == "az":
                                step(vec.tensor_tensor(s, s, dst, ALU.mult))
                            ins = vec.scalar_tensor_tensor(dst, acc[b % 2][m][:], rstd[:, m:m + 1], s, ALU.mult,
                                                           ALU.mult)
                        if m == 0:
                            step(ins)
                    ins.then_inc(acc_read[b % 2], 1)

            def gt(_, use):
                dve.wait_ge(g_act, 3)
                step(vec.tensor_scalar(rows[:, 3, :], rows[:, 3, :], 1.0, None, ALU.add))
                step(vec.reciprocal(rows[:, 3, :], rows[:, 3, :]))
                wait_read(dve, "gt", 0, 1)
                vec.scalar_tensor_tensor(rows[:, 4, :], rows[:, 2, :], -1.0, rows[:, 2, :], ALU.mult,
                                         ALU.max).then_inc(g_dve, 1)

            def gs(_, use):
                dve.wait_ge(g_act, 4)
                step(vec.scalar_tensor_tensor(rows[:, 2, :], rows[:, 2, :], 0.0, rows[:, 4, :], ALU.max, ALU.add))
                step(vec.tensor_scalar(rows[:, 4, :], rows[:, 2, :], hcol[:, 6:7], -1.0, ALU.mult, ALU.mult))
                for m in range(M):
                    tok = slice(m * P, m * P + P)
                    ins = vec.tensor_tensor_scan(rows[:, 2, tok], ones[0:8, :], rows[:, 4, tok], 0.0, ALU.mult,
                                                 ALU.add)
                    if m == 0:
                        step(ins)
                ins.then_inc(g_dve, 1)
                dve.wait_ge(g_dve, 2)
                step(vec.tensor_tensor_scan(rows[:, 4, :], ones[0:8, 0:1].to_broadcast([8, SEQ]), rows[:, 1, :], 0.0,
                                            ALU.mult, ALU.add))
                step(vec.scalar_tensor_tensor(rows[:, 0, :], rows[:, 0, :], GATE_CAP, rows[:, 4, :], ALU.mult,
                                              ALU.add))
                step(vec.tensor_tensor_scan(rows[:, 1, :], rows[:, 0, :], rows[:, 0, :], 0.0, ALU.max, ALU.max))
                step(vec.tensor_scalar(rows[:, 1, :], rows[:, 1, :], -1.0, None, ALU.mult))
                vec.tensor_tensor(rows[:, 4, :], rows[:, 4, :], rows[:, 1, :], ALU.add).then_inc(g_dve, 1)

            def gb(_, use):
                wait_filled(dve, use)
                done_bank(vec.tensor_copy(gcol[:].rearrange("p a b -> p (a b)"), bank(use)[:, 0:72]), use)
                dve.wait_ge(emptied[use % 4], use // 4 + 1)
                vec.tensor_scalar(gder[:, 0:2, :], gcol[:, 0:2, :], -1.0, None, ALU.mult).then_inc(g_cols, 1)
                dve.wait_ge(g_cols, 2)
                vec.scalar_tensor_tensor(gder[:, 4:6, :], gcol[:, 2:4, :], -1.0, gder[:, 2:4, :], ALU.mult,
                                         ALU.mult).then_inc(g_cols, 1)

            def kx(_, use):
                wait_stored(dve, "gates")
                for m in range(M):
                    step(vec.tensor_scalar(small[:, m, G_WI:G_WI + IDX_H], small[:, m, G_WI:G_WI + IDX_H],
                                           IDX_H ** -0.5 * IDX_D ** -0.5, None, ALU.mult))
                    step(vec.bn_stats(st[:, 32:38], small[:, m, G_KI:G_KI + IDX_D]))
                    step(vec.bn_aggr(st[:, 38:40], st[:, 32:38]))
                    step(vec.tensor_copy(st[:, 18 + m:19 + m], st[:, 38:39]))
                    ins = vec.tensor_copy(st[:, 20 + m:21 + m], st[:, 39:40])
                    if m == 0:
                        step(ins)
                ins.then_inc(k_dve, 1)
                dve.wait_ge(k_act, 1)
                for m in range(M):
                    for i in range(2):
                        ins = vec.tensor_scalar(kdup[:, m, i * IDX_D:(i + 1) * IDX_D], small[:, m, G_KI:G_KI + IDX_D],
                                                st[:, 18 + m:19 + m], st[:, 20 + m:21 + m], ALU.subtract, ALU.mult)
                        if (m, i) != (1, 1):
                            step(ins)
                ins.then_inc(k_dup, 1)
                wait_filled(dve, use)
                done_bank(vec.tensor_scalar(kiT[:], bank(use)[:, 0:SEQ], par[:, R_KIG:R_KIG + 1],
                                            par[:, R_KIB:R_KIB + 1], ALU.mult, ALU.add), use)
                dve.wait_ge(emptied[use % 4], use // 4 + 1)

            def conv(i, use):
                dve.wait_ge(conv_y, i + 1)
                for d in range(1, CONV_K):
                    for j in range(2):
                        c = 2 * i + j
                        row = R_N + (CONV_K - 1 - d) * CH + c
                        ins = vec.scalar_tensor_tensor(cT[:, c, d:SEQ], bank(use)[:, j * SEQ:j * SEQ + SEQ - d],
                                                       par[:, row:row + 1], cT[:, c, d:SEQ], ALU.mult, ALU.add)
                        if (d, j) != (CONV_K - 1, 1):
                            step(ins)
                done_bank(ins, use)
                dve.wait_ge(conv_exp, i + 1)
                e = c_kb[:].rearrange("p a b -> p (a b)")
                t = cT[:, 2 * i:2 * i + 2, :].rearrange("p c t -> p (c t)")
                step(vec.tensor_scalar(e, e, 1.0, None, ALU.add))
                step(vec.reciprocal(e, e))
                vec.tensor_tensor(t, t, e, ALU.mult).then_inc(conv_ready, 1)

            def cn(i, use):
                dve.wait_ge(c_r, i + 1)
                g = c_gam[:].rearrange("p a b -> p (a b)")
                t = cT[:, 2 * i:2 * i + 2, :].rearrange("p c t -> p (c t)")
                if i < 4:
                    ins = vec.scalar_tensor_tensor(t, t, HEAD ** -0.5, g, ALU.mult, ALU.mult)
                else:
                    ins = vec.tensor_tensor(t, t, g, ALU.mult)
                ins.then_inc(c_nd, 1)

            def ca(u, use):
                hg, m = UNITS[u]
                wait_filled(dve, use)
                dve.wait_ge(c_nd, 8)
                done_bank(vec.tensor_tensor(c_kb[:], bank(use)[:].rearrange("p (a b) -> p a b", a=4),
                                            cT[:, 8 + 4 * hg:12 + 4 * hg, m * P:m * P + P], ALU.mult), use)
                wait_filled(dve, use + 1)
                done_bank(vec.tensor_tensor(c_gam[:], bank(use + 1)[:].rearrange("p (a b) -> p a b", a=4),
                                            tri[:, 0:1, :].to_broadcast([P, 4, P]), ALU.add), use + 1)

            def cg(u, use):
                dve.wait_ge(c_gam_ready, u + 1)
                for i, dst in enumerate((c_at, c_bt)):
                    wait_filled(dve, use + i)
                    done_bank(vec.tensor_tensor(dst[:], bank(use + i)[:].rearrange("p (a b) -> p a b", a=4), c_gam[:],
                                                ALU.mult), use + i)
                    dve.wait_ge(emptied[(use + i) % 4], (use + i) // 4 + 1)
                step(vec.tensor_tensor(c_u[:], c_at[:], level[:, 0:1, :].to_broadcast([P, 4, P]), ALU.mult))
                vec.tensor_tensor(c_u[:], ident[:].unsqueeze(1).to_broadcast([P, 4, P]), c_u[:],
                                  ALU.subtract).then_inc(c_u0, 1)

            def cm(arg, use):
                u, lv = arg
                wait_filled(dve, use)
                done_bank(vec.tensor_tensor(c_kb[:], bank(use)[:].rearrange("p (a b) -> p a b", a=4),
                                            level[:, lv:lv + 1, :].to_broadcast([P, 4, P]), ALU.mult), use)

            def cu(arg, use):
                wait_filled(dve, use)
                u4 = c_u[:].rearrange("p a b -> p (a b)")
                done_bank(vec.tensor_tensor(u4, u4, bank(use)[:], ALU.subtract), use)

            def cs(u, use):
                hg, m = UNITS[u]
                wait_filled(dve, use)
                wait_read(dve, "cv", u)
                for a in range(4):
                    ins = vec.scalar_tensor_tensor(c_v[:, a, :], bank(use)[:, a * P:a * P + P],
                                                   gder[:, 4 + m, 4 * hg + a:4 * hg + a + 1], c_v[:, a, :],
                                                   ALU.mult, ALU.add)
                    if a < 3:
                        step(ins)
                done_bank(ins, use)

            def co(u, use):
                hg, m = UNITS[u]
                wait_filled(dve, use)
                o = c_at[:].rearrange("p a b -> p (a b)")
                wait_read(dve, "co", u, 1)
                if m == 0:
                    done_bank(vec.tensor_copy(o, bank(use)[:]), use)
                else:
                    done_bank(vec.tensor_tensor(o, bank(use)[:], c_kb[:].rearrange("p a b -> p (a b)"), ALU.add), use)
                dve.wait_ge(c_osq, u + 1)
                vec.tensor_reduce(st[:, 0:4], c_gam[:], AX_X, ALU.add).then_inc(c_oss, 1)
                dve.wait_ge(c_or, u + 1)
                for a in range(4):
                    h = 4 * hg + a
                    dst = y[:, m, W_A + W_B + h * P:W_A + W_B + h * P + P]
                    ins = vec.scalar_tensor_tensor(dst, c_at[:, a, :], st[:, a:a + 1], dst, ALU.mult, ALU.mult)
                    if a < 3:
                        step(ins)
                ins.then_inc(c_y, 1)

            def bn(_, use):
                dve.wait_ge(b_act, 1)
                for m in range(M):
                    vec.tensor_scalar(y[:, m, 0:Q_LORA], y[:, m, 0:Q_LORA], st[:, 4 + m:5 + m], None,
                                      ALU.mult).then_inc(cq_norm, 1)

            def bt(i, use):
                dve.wait_ge(cq_hi_ready, i + 1)
                for j in range(min(2, QKT - 2 * i)):
                    kt = 2 * i + j
                    ins = vec.scalar_tensor_tensor(cq_lo[:, kt, :], bank(use)[:, j * SEQ:j * SEQ + SEQ],
                                                   par[:, R_CQ + kt:R_CQ + kt + 1], cq_hi[:, kt, :].bitcast(F32),
                                                   ALU.mult, ALU.subtract)
                    if j == 0 and i < 3:
                        step(ins)
                done_bank(ins, use)

            def head_norms(n, norm):
                dve.wait_ge(b_act, 1 + 3 * n + 2)
                for m in range(M):
                    ins = vec.tensor_reduce(st[:, 8 + 4 * m:12 + 4 * m],
                                            b_sq[:, m * 512:m * 512 + 512].rearrange("p (h d) -> p h d", h=4), AX_X,
                                            ALU.add)
                    if m == 0:
                        step(ins)
                ins.then_inc(b_dve, 1)
                dve.wait_ge(b_act, 1 + 3 * n + 3)
                for m in range(M):
                    v = (kv[:, m, 0:512] if n == 0 else qs[:, m, :]).rearrange("p (h d) -> p h d", h=4)
                    vec.tensor_tensor(v, v, st[:, 8 + 4 * m:12 + 4 * m].unsqueeze(2).to_broadcast([P, 4, P]),
                                      ALU.mult).then_inc(norm, 1)

            def bkn(_, use):
                head_norms(0, bk_norm)

            def bqn(g, use):
                head_norms(g + 1, bq_norm)

            def bsc(arg, use):
                j, p = arg
                for s in range(2):
                    h = 8 * j + 2 * p + s
                    wait_read(dve, "bsc", arg, s)
                    rl = (b_s, b_p)[s]
                    for m in range(M):
                        cols = slice(0, P) if m == 0 else slice(P, 3 * P)
                        w = small[:, m, G_WI + h:G_WI + h + 1]
                        if h == 0:
                            ins = vec.tensor_scalar(sc[:, cols], rl[:, cols], w, None, ALU.mult)
                        else:
                            ins = vec.scalar_tensor_tensor(sc[:, cols], rl[:, cols], w, sc[:, cols], ALU.mult,
                                                           ALU.add)
                        if m == 0:
                            step(ins)
                    ins.then_inc(b_score, 1)
                    dve.wait_ge(b_score, h + 1)

            def btk(arg, use):
                m, part = arg
                cols = slice(0, P) if m == 0 else slice(P, 3 * P)
                w = P * (m + 1)
                work = b_s[:, 0:w]
                gt_, eq = b_p[:, 0:w], b_p[:, 256:256 + w]
                if part == 0:
                    diag = sc[:, 2 * m * P:2 * m * P + P]
                    step(vec.tensor_tensor(diag, diag, cap[:], ALU.min))
                    step(vec.tensor_copy(work, sc[:, cols]))
                if part < 2:
                    for r in range(4 * part, 4 * part + 4):
                        step(vec.max(top8[:], work))
                        if r < TOPK // 8 - 1:
                            step(vec.match_replace(work, top8[:], work, -3.4028234e38))
                    return
                thr = top8[:, 7:8]
                step(vec.tensor_scalar(gt_, sc[:, cols], thr, None, ALU.is_gt))
                step(vec.tensor_reduce(st[:, 40:41], gt_, AX_X, ALU.add))
                step(vec.tensor_scalar(st[:, 40:41], st[:, 40:41], -1.0, float(TOPK), ALU.mult, ALU.add))
                step(vec.tensor_scalar(eq, sc[:, cols], thr, None, ALU.is_equal))
                step(vec.tensor_tensor_scan(work, ones[:, 0:1].to_broadcast([P, w]), eq, 0.0, ALU.mult, ALU.add))
                step(vec.scalar_tensor_tensor(work, work, st[:, 40:41], eq, ALU.is_le, ALU.mult))
                step(vec.tensor_tensor(work, work, gt_, ALU.add))
                step(vec.tensor_scalar(sc[:, cols], work, 1.0, -NEG, ALU.subtract, ALU.mult))
                diag = sc[:, 2 * m * P:2 * m * P + P]
                step(vec.tensor_tensor(diag, diag, low[:], ALU.min))

            def bs(arg, use):
                g, v = arg
                n, w = (4, P) if v == 0 else (2, SEQ)
                sel_ = (sc[:, 0:P] if v == 0 else sc[:, P:3 * P]).unsqueeze(1).to_broadcast([P, n, w])
                s3 = b_s[:].rearrange("p (h k) -> p h k", h=n)
                wait_filled(dve, use)
                done_bank(vec.tensor_tensor(s3, bank(use)[:].rearrange("p (h k) -> p h k", h=n), sel_, ALU.add), use)
                dve.wait_ge(emptied[use % 4], use // 4 + 1)
                step(vec.tensor_reduce(st[:, 24:24 + n], s3, AX_X, ALU.max))
                vec.tensor_scalar(st[:, 24:24 + n], st[:, 24:24 + n], -HEAD ** -0.5, None, ALU.mult).then_inc(b_max, 1)
                dve.wait_ge(b_exp, 3 * g + v + 1)
                step(vec.reciprocal(st[:, 28:28 + n], st[:, 28:28 + n]))

            def bo(arg, use):
                g, v = arg
                m = 0 if v == 0 else 1
                wait_filled(dve, use)
                for i in range(4 if v == 0 else 2):
                    h = 4 * g + (i if v == 0 else 2 * v - 2 + i)
                    dst = y[:, m, W_A + h * P:W_A + h * P + P]
                    ins = vec.scalar_tensor_tensor(dst, bank(use)[:, i * P:i * P + P], st[:, 28 + i:29 + i], dst,
                                                   ALU.mult, ALU.mult)
                    if i < (3 if v == 0 else 1):
                        step(ins)
                done_bank(ins, use)

            def at(j, use):
                if j == 0:
                    vec.memset(a_v[:, :, :, HEAD:HEAD + 1], 1.0).then_inc(a_one, 1)

            def ae(h, use):
                wait_filled(dve, use)
                done_bank(vec.tensor_tensor(a_m[:], bank(use)[:, 0:3 * P], tri[:].rearrange("p a b -> p (a b)"),
                                            ALU.add), use)
                dve.wait_ge(a_exp, h + 1)
                wait_filled(dve, use + 1)
                done_bank(vec.tensor_tensor(a_p[:], bank(use + 1)[:, 0:3 * P], a_m[:], ALU.mult), use + 1)

            def ap(h, use):
                wait_filled(dve, use)
                b2 = bank(use)[:].rearrange("p (m c) -> p m c", m=M)
                step(vec.tensor_copy(st[:, 40:42], b2[:, :, HEAD]))
                step(vec.scalar_tensor_tensor(st[:, 40:42], st[:, 40:42], -1.0, st[:, 40:42], ALU.mult, ALU.max))
                step(vec.tensor_tensor(st[:, 40:42], st[:, 40:42], gcol[:, 7:9, h], ALU.max))
                step(vec.reciprocal(st[:, 40:42], st[:, 40:42]))
                for m in range(M):
                    ins = vec.tensor_scalar(a_h[:, m, :], b2[:, m, 0:HEAD], st[:, 40 + m:41 + m], None, ALU.mult)
                    if m == 0:
                        step(ins)
                done_bank(ins, use)
                dve.wait_ge(a_ss, h + 1)
                for m in range(M):
                    dst = y[:, m, h * P:h * P + P]
                    ins = vec.scalar_tensor_tensor(dst, a_h[:, m, :], st[:, 36 + m:37 + m], dst, ALU.mult, ALU.mult)
                    if m == 0:
                        step(ins)
                ins.then_inc(a_y, 1)

            y_done = [0]

            def yt(i, use):
                y_done[0] += 1
                dve.wait_ge(y_hi_ready, y_done[0])
                for j in range(2):
                    kt = 2 * i + j
                    gain = y_gain(kt)
                    src, hi = bank(use)[:, j * SEQ:j * SEQ + SEQ], op_hi[:, kt, :].bitcast(F32)
                    if gain is None:
                        ins = vec.tensor_tensor(op_lo[:, kt, :], src, hi, ALU.subtract)
                    else:
                        ins = vec.scalar_tensor_tensor(op_lo[:, kt, :], src, gain, hi, ALU.mult, ALU.subtract)
                    if j == 0:
                        step(ins)
                done_bank(ins, use)

            pieces = dict(evac=evac, gt=gt, gs=gs, gb=gb, kx=kx, conv=conv, cn=cn, ca=ca, cg=cg, cm=cm, cu=cu, cs=cs,
                          co=co, bn=bn, bt=bt, bkn=bkn, bqn=bqn, bsc=bsc, btk=btk, bs=bs, bo=bo, at=at, ae=ae, ap=ap,
                          yt=yt)

            dve.wait_ge(const_ready, 1)
            for i, n in enumerate((R_N, N_TAP)):
                wait_filled(dve, i)
                done_bank(vec.tensor_copy(par[:, R_N * i:R_N * i + n], bank(i)[:, 0:n]), i)
            for i in range(NX):
                use = 2 + i
                dve.wait_ge(x_hi_ready, i + 1)
                for j in range(2):
                    kt = 2 * i + j
                    ins = vec.scalar_tensor_tensor(op_lo[:, kt, :], bank(use)[:, j * SEQ:j * SEQ + SEQ],
                                                   par[:, R_NORM + kt:R_NORM + kt + 1], op_hi[:, kt, :].bitcast(F32),
                                                   ALU.mult, ALU.subtract)
                    if j == 0:
                        step(ins)
                done_bank(ins, use)
            for c in range(AHEAD):
                split_lo(c)
            dve.wait_ge(ss_ready, 8)
            for q in range(1, 4):
                ins = vec.tensor_tensor(ssq[:, 0:2], ssq[:, 0:2], ssq[:, 2 * q:2 * q + 2], ALU.add)
                if q < 3:
                    step(ins)
            ins.then_inc(ss_ready, 1)
            dve.wait_ge(const_ready, 2)
            for c in range(len(chunks)):
                if c + AHEAD < len(chunks):
                    split_lo(c + AHEAD)
                for name, arg, use in woven[c]:
                    if name in pieces:
                        pieces[name](arg, U0 + use)


_INS = ["x", "norm_g", "w_in", "w_out", "m_ib", "m_fb", "m_norm_g", "a_cq_g", "a_wuq", "a_wuqi", "a_qn_g", "a_kn_g",
        "a_ki_g", "a_ki_b", "d_conv_w", "d_a_log", "d_dt_bias", "d_norm_g"]
_OUTS = [((1, SEQ, D), "float32")]


def kernel(**inputs):
    import numpy as _np
    import concourse.bacc as _bacc
    from concourse import mybir as _mybir
    from concourse.bass_utils import run_bass_kernel_spmd as _run

    nc = _bacc.Bacc("TRN2", target_bir_lowering=False, num_devices=1)
    arrays, args = {}, []
    for name in _INS:
        a = _np.ascontiguousarray(inputs[name])
        arrays[f"in_{name}_dram"] = a
        args.append(nc.dram_tensor(f"in_{name}_dram", a.shape, _mybir.dt.from_np(a.dtype), kind="ExternalInput").ap())
    for i, (shape, dtype) in enumerate(_OUTS):
        dt = _mybir.dt.from_np(_np.dtype(dtype))
        args.append(nc.dram_tensor(f"out_{i}_dram", shape, dt, kind="ExternalOutput").ap())
    hybrid_kernel(nc, *args)
    r = _run(nc, [arrays], core_ids=[0])
    return r.results[0]["out_0_dram"]
```

```python
from contextlib import ExitStack

import concourse.bass as bass
from concourse import mybir

F32 = mybir.dt.float32
F32R = mybir.dt.float32r
BF16 = mybir.dt.bfloat16
ALU = mybir.AluOpType
ACT = mybir.ActivationFunctionType
AX_X = mybir.AxisListType.X

P = 128
D = 4096
SEQ = 256
M = SEQ // P
KT = D // P
HEAD = 128
W_A, W_B, W_C = D // 4, D // 2, D // 4
H_A, H_B, H_C = W_A // HEAD, W_B // HEAD, W_C // HEAD
DQK = HEAD // 2
GATE_CAP = 15.0
HKV = 4
GRP = H_B // HKV
Q_LORA = 896
QKT = Q_LORA // P
IDX_H, IDX_D = 16, 64
TOPK = min(256, SEQ // 4)
CONV_K = 4
EPS = 1e-6
NEG = -1e30
BIG = 3.3e38

C_AQ = 0
C_AK = C_AQ + H_A * DQK
C_AV = C_AK + H_A * DQK
C_AI = C_AV + W_A
C_AO = C_AI + 2 * H_A
C_AZ = C_AO + W_A
C_BCQ = C_AZ + W_A
C_BK = C_BCQ + Q_LORA
C_BV = C_BK + HKV * HEAD
C_BKI = C_BV + HKV * HEAD
C_BZ = C_BKI + IDX_D + IDX_H
C_CQKV = C_BZ + W_B
C_CB = C_CQKV + 3 * W_C
C_CZ = C_CB + 2 * H_C
N_IN = C_CZ + W_C

G_AI, G_AF, G_CB, G_CA, G_KI, G_WI, G_W = 0, 8, 16, 24, 32, 96, 112

R_NORM, R_CQ, R_QN, R_KN, R_KIG, R_KIB, R_MN, R_DN, R_N = 0, 32, 39, 40, 41, 42, 43, 51, 52
N_TAP = CONV_K * 3 * W_C // P
CH = 3 * W_C // P

RAW_BUFS = 4
SPLIT_BUFS = 4
AHEAD = SPLIT_BUFS - 1
NX = KT // 2
RSQRT = 1597463007.0
LEVELS = 7
UNITS = [(hg, m) for hg in range(H_C // 4) for m in range(M)]

USES = {"par": 2, "gt": 2, "gb": 1, "kx": 1, "conv": 1, "cn": 1, "ca": 2, "cg": 2, "ct": 1, "cm": 1, "cu": 1, "cv": 1,
        "ck": 1, "cs": 1, "cr": 1, "co": 2, "bt": 1, "bkt": 2, "bit": 2, "bsc": 2, "bqt": 2, "bs": 1, "bp": 1,
        "bo": 1, "at": 2, "ae": 2, "ap": 1, "yt": 1}


def plan():
    wide = 2
    blocks = []

    def block(kind, arg, operand, kts, per, width, matrix, col):
        blocks.append(dict(kind=kind, arg=arg, operand=operand, kts=kts, per=per, width=width, matrix=matrix,
                           col=col))

    full = list(range(KT))

    def project(kind, arg, col, width=512):
        block(kind, arg, "h", full, wide, width, "w_in", col)

    for j in range(6):
        project("conv", j, C_CQKV + 512 * j)
    block("gates", 0, "h", full, 8, G_W, "w_in", 0)
    for j in range(2):
        project("silu", W_A + W_B + 512 * j, C_CZ + 512 * j)
    project("cq", 0, C_BCQ)
    project("cq", 512, C_BCQ + 512, Q_LORA - 512)
    project("bkv", 0, C_BK)
    project("bkv", 512, C_BV)
    for j in range(4):
        project("silu", W_A + 512 * j, C_BZ + 512 * j)
    for j in range(2):
        block("bi", j, "cq", list(range(QKT)), wide, 512, "wuqi", 512 * j)
    for j in range(4):
        project(("ao", "az")[j // 2], 512 * (j % 2), (C_AO, C_AZ)[j // 2] + 512 * (j % 2))
        block("bq", j, "cq", list(range(QKT)), wide, 512, "wuq", 512 * j)
    project("aqk", 0, C_AQ)
    project("aqk", 1, C_AK)
    project("av", 0, C_AV)
    project("av", 1, C_AV + 512)
    kt_a = W_A // P
    for n in range(D // 512):
        block("out1", n, "y", full[kt_a:], wide, 512, "w_out", 512 * n)
    for n in range(D // 512):
        block("out2", n, "y", full[:kt_a], wide, 512, "w_out", 512 * n)

    chunks, last = [], []
    for b, blk in enumerate(blocks):
        for i in range(0, len(blk["kts"]), blk["per"]):
            chunks.append((b, blk["kts"][i:i + blk["per"]]))
        last.append(len(chunks) - 1)

    woven = [[] for _ in chunks]

    def end(kind, arg=0):
        return next(last[b] for b, x in enumerate(blocks) if x["kind"] == kind and x["arg"] == arg)

    def weave(at, pieces, every=1):
        for piece in pieces:
            woven[at] += [] if piece is None else piece if isinstance(piece, list) else [piece]
            at += every
        return at

    for b, x in enumerate(blocks):
        woven[last[b]].append(("evac", b))
    woven[NX - 1].append(("par", 0))
    for j in range(6):
        at = weave(end("conv", j) + 2, [("conv", 2 * j), ("conv", 2 * j + 1)], 6)
    g = end("gates") + 2
    weave(g, [("gt", 0), ("kn", 0), ("g1", 0), ("g2", 0), None, ("g3", 0), ("kx", 0), ("g4", 0), None, ("gb", 0)])
    at = weave(max(at, g + 4), [("csq", 0)])
    for i in range(8):
        at = weave(at, [([("csq", i + 1)] if i < 7 else []) + [("cn", i)]])
    at = weave(at, [None] + [("ce", i) for i in range(8)])
    for u, (hg, m) in enumerate(UNITS):
        at = weave(at, [("ca", u), ("cg", u), None])
        for lv in range(1, LEVELS):
            at = weave(at, [("ct", (u, lv)), ("cm", (u, lv)), ("cu", (u, lv))])
        at = weave(at, [("cv", u), ("ck", u) if m == 0 else ("cs", u), ("cr", u), ("co", u), None])
    at = max(at, end("bkv", 512) + 1)
    at = weave(at, [("bn", 0), ("bkn", 0), None, None] + [("bt", i) for i in range(4)] + [("bkt", 0)])
    assert at <= end("silu", W_A + 512 * 3) + 1, (at, end("silu", W_A + 512 * 3))
    at = weave(end("bi", 0) + 1, [("bit", 0)] + [("bsc", (0, p)) for p in range(4)])
    at = weave(max(at, end("bi", 1) + 1), [("bit", 1)] + [("bsc", (1, p)) for p in range(4)])
    for m in range(M):
        at = weave(at, [("btk", (m, i)) for i in range(0, TOPK // 8, 3 - m)] + [("bts", (m, 0)), ("bts", (m, 1))])
    assert at <= end("bq", 0) + 1, (at, end("bq", 0))
    for g in range(HKV):
        at = weave(end("bq", g) + 1, [("bqn", g), None, None, ("bqt", g)])
        for v in range(3):
            at = weave(at, [("bs", (g, v)), None, ("bp", (g, v)), ("bo", (g, v))])
    assert at <= end("aqk", 0) + 1, (at, end("aqk", 0))
    weave(end("aqk", 0) + 1, [("at", 0)])
    weave(end("aqk", 1) + 1, [("at", 1)])
    first = end("av", 1)
    woven[first] += [("yt", 4), ("yt", 5)]
    at = weave(first + 1, [("yt", i) for i in range(6, 16)])
    for h in range(H_A):
        at = weave(at, [("ae", h), None, None, ("ap", h), None, None, ("ay", h), None])
    at = weave(at + 1, [("yt", i) for i in range(4)], 2)
    assert at <= end("out1", 7), (at, end("out1", 7))

    use, order = 0, {}
    for slot in woven:
        for i, (name, arg) in enumerate(slot):
            slot[i] = (name, arg, use)
            order[name] = order.get(name, 0) + 1
            use += USES.get(name, 0)
    return blocks, chunks, last, woven, use


def hybrid_kernel(nc, x, norm_g, w_in, w_out, m_ib, m_fb, m_norm_g, a_cq_g, a_wuq, a_wuqi, a_qn_g, a_kn_g,
                  a_ki_g, a_ki_b, d_conv_w, d_a_log, d_dt_bias, d_norm_g, out):
    blocks, chunks, last, woven, _ = plan()
    U0 = NX + 1

    matrix = {
        "w_in": w_in[0].rearrange("(kt p) n -> p kt n", p=P),
        "w_out": w_out[0].rearrange("(kt p) n -> p kt n", p=P),
        "wuq": a_wuq[0].rearrange("(kt p) n -> p kt n", p=P),
        "wuqi": a_wuqi[0].rearrange("(kt p) n -> p kt n", p=P),
    }
    x_dram = x[0].rearrange("(m p) d -> p m d", p=P)
    out_dram = out[0].rearrange("(m p) d -> p m d", p=P)

    with ExitStack() as ctx:
        def sb(name, shape, dt=F32, stack=ctx):
            return stack.enter_context(nc.sbuf_tensor(name, shape, dt))

        def sem(name):
            return ctx.enter_context(nc.semaphore(name))

        acc = [[ctx.enter_context(nc.psum_tensor(f"acc{b}{m}", [P, 512], F32)) for m in range(M)] for b in range(2)]
        mix = [ctx.enter_context(nc.psum_tensor(f"mix{b}", [P, 512], F32)) for b in range(4)]

        op_hi = sb("op_hi", [P, KT, SEQ], F32R)
        op_lo = sb("op_lo", [P, KT, SEQ], F32R)
        w_raw = sb("w_raw", [P, RAW_BUFS, 1024])
        w_hi = sb("w_hi", [P, SPLIT_BUFS, 1024], F32R)
        w_lo = sb("w_lo", [P, SPLIT_BUFS, 1024], F32R)
        y = sb("y", [P, M, D])
        kv = sb("kv", [P, M, 1024])
        ident = sb("ident", [P, P])
        ones = sb("ones", [P, P])
        sel = sb("sel", [8, 8, P])
        level = sb("level", [P, LEVELS, P], BF16)
        tri = sb("tri", [P, 3, P], BF16)
        cap = sb("cap", [P, P], BF16)
        low = sb("low", [P, P], BF16)
        par = sb("par", [P, R_N + N_TAP])
        small = sb("small", [P, M, G_W])
        rows = sb("rows", [8, 6, SEQ])
        gcol = sb("gcol", [P, 9, 8])
        gder = sb("gder", [P, 6, 8])
        hcol = sb("hcol", [8, 8])
        eps = sb("eps", [P, 1])
        ssq = sb("ssq", [P, M, NX // M])
        rstd = sb("rstd", [P, M])
        newton = sb("newton", [P, 8])
        newton2 = sb("newton2", [P, 8])
        st = sb("st", [P, 48])
        kiT = sb("kiT", [P, SEQ])

        def region(names):
            with ExitStack() as stack:
                return [sb(n, s, d, stack) for n, s, d in names]

        xs, norm_in = region([("xs", [P, M, D], F32), ("norm_in", [P, P], F32)])
        _, par_in, tap_in = region([("xs_", [P, M, D + P], F32), ("par_in", [P, P], F32), ("tap_in", [P, P], F32)])
        cT, c_kb, c_gam, c_at, c_bt, c_u, c_v, c_kd = region(
            [("cT", [P, CH, SEQ], F32)] + [(n, [P, 4, P], F32) for n in
             ("c_kb", "c_gam", "c_at", "c_bt", "c_u", "c_v", "c_kd")])
        c_s = c_kd
        kdup = kv[:, 1, 512:512 + SEQ].rearrange("p (m d) -> p m d", m=M)
        cq_hi, cq_lo, qs, b_sq, b_qT, b_kT, sc, b_s, b_p, b_pT, top8 = region(
            [("cq_hi", [P, QKT, SEQ], F32R), ("cq_lo", [P, QKT, SEQ], F32R), ("qs", [P, M, 512], F32),
             ("b_sq", [P, 1024], F32), ("b_qT", [P, 4, SEQ], F32), ("b_kT", [P, HKV, SEQ], F32),
             ("sc", [P, 3 * P], F32), ("b_s", [P, 512], F32), ("b_p", [P, 512], F32),
             ("b_pT", [P, 4, P], F32), ("top8", [P, 8], F32)])
        a_s, a_qT, a_kT, a_v, a_m, a_p, a_h, a_sq, acc0 = region(
            [("a_s", [P, M, 512], F32), ("a_qT", [P, 4, SEQ], F32), ("a_kT", [P, 4, SEQ], F32),
             ("a_v", [P, M, H_A, HEAD + 1], F32), ("a_m", [P, 3 * P], F32), ("a_p", [P, 3 * P], F32),
             ("a_h", [P, M, P], F32), ("a_sq", [P, P], F32), ("acc0", [P, M, W_A], F32)])

        par_in_ready = sem("par_in_ready")
        norm_in_ready = sem("norm_in_ready")
        x_ready = [sem(f"x_ready{q}") for q in range(8)]
        raw_ready = [sem(f"raw_ready{b}") for b in range(RAW_BUFS)]
        const_ready = sem("const_ready")
        pool_step = sem("pool_step")
        head_ready = sem("head_ready")
        x_hi_ready = sem("x_hi_ready")
        ss_ready = sem("ss_ready")
        rstd_ready = sem("rstd_ready")
        hi_ready = sem("hi_ready")
        lo_ready = sem("lo_ready")
        split_used = sem("split_used")
        acc_ready = sem("acc_ready")
        acc_read = [sem(f"acc_read{b}") for b in range(2)]
        filled = [sem(f"filled{b}") for b in range(4)]
        emptied = [sem(f"emptied{b}") for b in range(4)]
        act_step = sem("act_step")
        dve_step = sem("dve_step")
        az_ready = sem("az_ready")
        g_act = sem("g_act")
        g_dve = sem("g_dve")
        g_rows = sem("g_rows")
        g_cols = sem("g_cols")
        k_dup = sem("k_dup")
        conv_y = sem("conv_y")
        conv_ready = sem("conv_ready")
        c_sq = sem("c_sq")
        c_r = sem("c_r")
        c_nd = sem("c_nd")
        c_gam_ready = sem("c_gam_ready")
        c_u0 = sem("c_u0")
        c_y = sem("c_y")
        c_osq = sem("c_osq")
        cq_ss = sem("cq_ss")
        b_sq_ready = sem("b_sq_ready")
        cq_norm = sem("cq_norm")
        cq_hi_ready = sem("cq_hi_ready")
        bk_norm = sem("bk_norm")
        b_score = sem("b_score")
        bq_norm = sem("bq_norm")
        b_max = sem("b_max")
        b_exp = sem("b_exp")
        a_one = sem("a_one")
        a_exp = sem("a_exp")
        a_y = sem("a_y")
        a_ss = sem("a_ss")
        y_hi_ready = sem("y_hi_ready")
        x_again = [sem(f"x_again{n}") for n in range(D // 512)]
        out_done = sem("out_done")

        block = ctx.enter_context(nc.Block())

        def raw_dmas(c):
            b, kts = chunks[c]
            k0, n = kts[0], len(kts)
            blk = blocks[b]
            dst = w_raw[:, c % RAW_BUFS, 0:n * blk["width"]].rearrange("p (k n) -> p k n", k=n)
            src = matrix[blk["matrix"]][:, k0:k0 + n, :]
            if blk["kind"] == "gates":
                return [(dst[:, :, g:g + w], src[:, :, col:col + w]) for g, col, w in
                        ((G_AI, C_AI, 16), (G_CB, C_CB, 16), (G_KI, C_BKI, IDX_D + IDX_H))]
            return [(dst, src[:, :, blk["col"]:blk["col"] + blk["width"]])]

        def raw_count(c):
            return 16 * sum(3 if blocks[chunks[i][0]]["kind"] == "gates" else 1
                            for i in range(c % RAW_BUFS, c + 1, RAW_BUFS))

        def split_ap(tensor, c):
            b, kts = chunks[c]
            return tensor[:, c % SPLIT_BUFS, 0:len(kts) * blocks[b]["width"]]

        def bank(use):
            return mix[use % 4]

        def wait_filled(eng, use):
            eng.wait_ge(filled[use % 4], use // 4 + 1)

        def wait_emptied(eng, use):
            if use >= 4:
                eng.wait_ge(emptied[use % 4], use // 4)

        use_of = {(name, arg): U0 + use for slot in woven for name, arg, use in slot}

        def wait_read(eng, name, arg, i=0):
            use = use_of[name, arg] + i
            eng.wait_ge(emptied[use % 4], use // 4 + 1)

        def wait_stored(eng, kind, arg=0):
            b = next(i for i, x_ in enumerate(blocks) if x_["kind"] == kind and x_["arg"] == arg)
            eng.wait_ge(acc_read[b % 2], b // 2 + 1)

        def conv_stage(j):
            return y[:, :, W_A + 512 * (j % 2):W_A + 512 * (j % 2) + 512]

        def c_square(i):
            return kv[:, 0, 512 * (i % 2):512 * (i % 2) + 512]

        def c_norm(i):
            if i == 7:
                return kv[:, 1, 0:512]
            return (c_kb, c_gam, c_at, c_bt, c_u, c_v, c_kd)[i][:].rearrange("p a b -> p (a b)")

        def out_acc(n):
            return acc0[:, :, 512 * n:512 * n + 512] if n < 2 else y[:, :, 512 * n:512 * n + 512]

        def y_gain(kt):
            if kt < W_A // P:
                return par[:, R_MN + kt:R_MN + kt + 1]
            return par[:, R_DN:R_DN + 1] if kt >= (W_A + W_B) // P else None

        @block.sync
        def _(sp):
            def x_piece(q):
                sp.dma_start(xs[:, :, 512 * q:512 * q + 512], x_dram[:, :, 512 * q:512 * q + 512]).then_inc(
                    x_ready[q], 16)

            def weights(c):
                if c >= RAW_BUFS:
                    sp.wait_ge(lo_ready, c - RAW_BUFS + 1)
                for dst, src in raw_dmas(c):
                    sp.dma_start(dst, src).then_inc(raw_ready[c % RAW_BUFS], 16)

            sp.dma_start(norm_in[0:32, :], norm_g[0].rearrange("(r p) -> r p", p=P)).then_inc(norm_in_ready, 16)
            x_piece(0)
            weights(0)
            x_piece(1)
            weights(1)
            for q in range(2, 8):
                x_piece(q)
                if q < RAW_BUFS:
                    weights(q)
            for r, a in ((R_CQ, a_cq_g[0].rearrange("(r p) -> r p", p=P)), (R_QN, a_qn_g), (R_KN, a_kn_g),
                         (R_MN, m_norm_g[0].rearrange("(r p) -> r p", p=P)), (R_DN, d_norm_g)):
                sp.dma_start(par_in[r - R_CQ:r - R_CQ + a.shape[0], :], a).then_inc(par_in_ready, 16)
            for r, a in ((R_KIG, a_ki_g), (R_KIB, a_ki_b)):
                for i in range(2):
                    sp.dma_start(par_in[r - R_CQ:r - R_CQ + 1, i * IDX_D:(i + 1) * IDX_D], a).then_inc(par_in_ready, 16)
            sp.dma_start(tap_in[0:N_TAP, :], d_conv_w[0].rearrange("t (c p) -> (t c) p", p=P)).then_inc(
                par_in_ready, 16)
            for i, a in enumerate((m_ib, m_fb, d_a_log, d_dt_bias)):
                sp.dma_start(hcol[:, i:i + 1], a.rearrange("o h -> h o")).then_inc(par_in_ready, 16)
            for c in range(RAW_BUFS, len(chunks)):
                weights(c)

        PAR_DMAS = 16 * 14

        @block.gpsimd
        def _(pool):
            steps = [0]

            def step(ins):
                steps[0] += 1
                ins.then_inc(pool_step, 1)
                pool.wait_ge(pool_step, steps[0])

            def select(view, op, fill, base, pattern, cm):
                step(nc.gpsimd.affine_select(out=view, in_=view, compare_op=op, fill=fill, base=base,
                                             pattern=pattern, channel_multiplier=cm))

            step(nc.gpsimd.memset(ident[:], 0.0))
            select(ident[:], ALU.not_equal, 1.0, 0, [[-1, P]], 1)
            nc.gpsimd.engine_nop().then_inc(const_ready, 1)
            step(nc.gpsimd.memset(ones[:], 1.0))
            step(nc.gpsimd.memset(eps[:], EPS))
            step(nc.gpsimd.memset(sel[:], 0.0))
            select(sel[:], ALU.not_equal, 1.0, 0, [[-1, 8], [0, P]], 1)
            step(nc.gpsimd.memset(tri[:], 0.0))
            for i in (0, 2):
                select(tri[:, i, :], ALU.is_ge, NEG, 0, [[1, P]], -1)
            step(nc.gpsimd.memset(cap[:], BIG))
            select(cap[:], ALU.is_ge, -BIG, 0, [[-1, P]], 1)
            step(nc.gpsimd.memset(low[:], 0.0))
            select(low[:], ALU.is_ge, NEG, 0, [[-1, P]], 1)
            step(nc.gpsimd.memset(level[:], 0.0))
            select(level[:, 0, :].rearrange("p (j c) -> p j c", c=2)[:, :, 1], ALU.not_equal, 1.0, 0,
                   [[-2, P // 2]], 1)
            for lv in range(1, LEVELS):
                b = 1 << lv
                n = P // (2 * b)
                v = level[:, lv, :].rearrange("p (j c r) -> p j c r", c=2, r=b)[:, :, 0, :]
                step(nc.gpsimd.memset(v, 1.0))
                select(v, ALU.is_ge, 0.0, -b, [[-2 * b, n], [0, b]], 1)
                select(v, ALU.is_ge, 0.0, 2 * b - 1, [[2 * b, n], [0, b]], -1)
            nc.gpsimd.engine_nop().then_inc(const_ready, 1)
            wait_read(pool, "bo", (HKV - 1, 2))
            for n in range(D // 512):
                if 512 * n == W_A:
                    for i in range(12, 16):
                        wait_read(pool, "yt", i)
                pool.dma_start(out_acc(n), x_dram[:, :, 512 * n:512 * n + 512]).then_inc(x_again[n], 16)
            for n in range(D // 512):
                wait_stored(pool, "out2", n)
                pool.dma_start(out_dram[:, :, 512 * n:512 * n + 512], out_acc(n)).then_inc(out_done, 16)
            pool.wait_ge(out_done, 16 * (D // 512))

        @block.tensor
        def _(pe):
            def end_fill(ins, use):
                ins.then_inc(filled[use % 4], 1)

            def turn(dst, src, n=P):
                return nc.tensor.transpose(dst, src, ident[0:n, 0:n])

            def chunk(c):
                b, kts = chunks[c]
                blk = blocks[b]
                w = blk["width"]
                if kts[0] == blk["kts"][0] and b >= 2:
                    pe.wait_ge(acc_read[b % 2], b // 2)
                pe.wait_ge(lo_ready, c + 1)
                hi, lo = {"h": (op_hi, op_lo), "cq": (cq_hi, cq_lo), "y": (op_hi, op_lo)}[blk["operand"]]
                hv = split_ap(w_hi, c).rearrange("p (k n) -> p k n", k=len(kts))
                lv = split_ap(w_lo, c).rearrange("p (k n) -> p k n", k=len(kts))
                for i, kt in enumerate(kts):
                    if b == 0:
                        use = 1 + kt // 2
                        pe.wait_ge(emptied[use % 4], use // 4 + 1)
                    if blk["operand"] == "cq":
                        wait_read(pe, "bt", kt // 2)
                    if blk["kind"] in ("out1", "out2") and blk["arg"] == 0:
                        wait_read(pe, "yt", kt // 2)
                    for m in range(M):
                        o = acc[b % 2][m][:, 0:w]
                        tok = slice(m * P, m * P + P)
                        nc.tensor.matmul(o, hi[:, kt, tok], hv[:, i, :], start=(kt == blk["kts"][0]), stop=False)
                        nc.tensor.matmul(o, hi[:, kt, tok], lv[:, i, :], start=False, stop=False)
                        last_mm = nc.tensor.matmul(o, lo[:, kt, tok], hv[:, i, :], start=False,
                                                   stop=(kt == blk["kts"][-1]))
                if c == last[b]:
                    last_mm.then_inc(acc_ready, 1)
                    pe_done[0] += 1
                else:
                    last_mm.then_inc(split_used, 1)

            pe_done = [0]

            def gt(_, use):
                wait_stored(pe, "gates")
                for i in range(4):
                    u = use + i // 2
                    if i % 2 == 0:
                        wait_emptied(pe, u)
                    for m in range(M):
                        ins = turn(bank(u)[0:8, (i % 2) * SEQ + m * P:(i % 2) * SEQ + m * P + P],
                                   small[:, m, 8 * i:8 * i + 8])
                    if i % 2:
                        end_fill(ins, u)

            def gb(_, use):
                pe.wait_ge(g_rows, 2)
                wait_emptied(pe, use)
                for i, (r, m) in enumerate(((2, 0), (2, 1), (3, 0), (3, 1), (5, 0), (0, 0), (0, 1), (4, 0), (4, 1))):
                    ins = turn(bank(use)[:, 8 * i:8 * i + 8], rows[:, r, m * P:m * P + P], 8)
                end_fill(ins, use)

            def kx(_, use):
                pe.wait_ge(k_dup, 1)
                wait_emptied(pe, use)
                for m in range(M):
                    ins = turn(bank(use)[:, m * P:m * P + P], kdup[:, m, :])
                end_fill(ins, use)

            def conv(i, use):
                wait_stored(pe, "conv", i // 2)
                wait_emptied(pe, use)
                for j in range(2):
                    for m in range(M):
                        ins = turn(bank(use)[:, j * SEQ + m * P:j * SEQ + m * P + P],
                                   conv_stage(i // 2)[:, m, (i % 2) * SEQ + j * P:(i % 2) * SEQ + j * P + P])
                end_fill(ins, use)

            def cn(i, use):
                pe.wait_ge(c_sq, i + 1)
                wait_emptied(pe, use)
                end_fill(nc.tensor.matmul(bank(use)[:], ones[:], c_square(i), start=True, stop=True), use)

            def ca(u, use):
                hg, m = UNITS[u]
                for i, r in enumerate((3, 2)):
                    wait_emptied(pe, use + i)
                    for a in range(4):
                        ins = nc.tensor.matmul(bank(use + i)[:, a * P:a * P + P], sel[:, 4 * hg + a, :],
                                               rows[:, r, m * P:m * P + P], start=True, stop=True)
                    end_fill(ins, use + i)

            def cg(u, use):
                hg, m = UNITS[u]
                tok = slice(m * P, m * P + P)
                wait_read(pe, "ca", u)
                for i in range(2):
                    wait_emptied(pe, use + i)
                    for a in range(4):
                        h = 4 * hg + a
                        ins = nc.tensor.matmul(bank(use + i)[:, a * P:a * P + P], cT[:, 8 + h, tok],
                                               c_kb[:, a, :] if i == 0 else cT[:, h, tok], start=True, stop=True)
                    end_fill(ins, use + i)

            def ct(arg, use):
                u, lv = arg
                if lv == 1:
                    pe.wait_ge(c_u0, u + 1)
                else:
                    wait_read(pe, "cu", (u, lv - 1))
                wait_emptied(pe, use)
                for a in range(4):
                    ins = turn(bank(use)[:, a * P:a * P + P], c_u[:, a, :])
                end_fill(ins, use)

            def heads4(use, lhs, rhs):
                wait_emptied(pe, use)
                for a in range(4):
                    ins = nc.tensor.matmul(bank(use)[:, a * P:a * P + P], lhs(a), rhs(a), start=True, stop=True)
                end_fill(ins, use)

            def cm(arg, use):
                u, lv = arg
                wait_read(pe, "ct", arg)
                heads4(use, lambda a: c_at[:, a, :], lambda a: c_gam[:, a, :])

            def cu(arg, use):
                u, lv = arg
                wait_read(pe, "cm", arg)
                heads4(use, lambda a: c_kb[:, a, :], lambda a: c_u[:, a, :])

            def cv(u, use):
                hg, m = UNITS[u]
                wait_emptied(pe, use)
                for a in range(4):
                    ins = turn(bank(use)[:, a * P:a * P + P], cT[:, 16 + 4 * hg + a, m * P:m * P + P])
                end_fill(ins, use)

            def ck(u, use):
                hg, m = UNITS[u]
                wait_emptied(pe, use)
                for a in range(4):
                    ins = turn(bank(use)[:, a * P:a * P + P], cT[:, 8 + 4 * hg + a, m * P:m * P + P])
                end_fill(ins, use)

            def cs(u, use):
                hg, m = UNITS[u]
                wait_read(pe, "co", u - 1, 1)
                heads4(use, lambda a: cT[:, 8 + 4 * hg + a, m * P:m * P + P], lambda a: c_s[:, a, :])

            def cr(u, use):
                wait_read(pe, "cu", (u, LEVELS - 1))
                wait_read(pe, "cv" if UNITS[u][1] == 0 else "cs", u)
                heads4(use, lambda a: c_u[:, a, :], lambda a: c_v[:, a, :])

            def co(u, use):
                hg, m = UNITS[u]
                wait_read(pe, "cr", u)
                heads4(use, lambda a: c_bt[:, a, :], lambda a: c_v[:, a, :])
                if m == 0:
                    wait_read(pe, "ck", u)
                    heads4(use + 1, lambda a: c_kd[:, a, :], lambda a: c_v[:, a, :])
                else:
                    heads4(use + 1, lambda a: cT[:, 4 * hg + a, m * P:m * P + P], lambda a: c_s[:, a, :])

            def bt(i, use):
                pe.wait_ge(cq_norm, 2)
                wait_emptied(pe, use)
                for j in range(min(2, QKT - 2 * i)):
                    for m in range(M):
                        ins = turn(bank(use)[:, j * SEQ + m * P:j * SEQ + m * P + P],
                                   y[:, m, (2 * i + j) * P:(2 * i + j) * P + P])
                end_fill(ins, use)

            def turn8(use, src):
                for i in range(4):
                    u = use + i // 2
                    if i % 2 == 0:
                        wait_emptied(pe, u)
                    for m in range(M):
                        ins = turn(bank(u)[:, (i % 2) * SEQ + m * P:(i % 2) * SEQ + m * P + P],
                                   src[:, m, i * P:i * P + P])
                    if i % 2:
                        end_fill(ins, u)

            def bkt(_, use):
                pe.wait_ge(bk_norm, 2)
                turn8(use, kv[:, :, 0:512])

            def bit(j, use):
                wait_stored(pe, "bi", j)
                turn8(use, qs)

            def bsc(arg, use):
                j, p = arg
                wait_read(pe, "kx", 0)
                wait_read(pe, "bit", j, p // 2)
                for s in range(2):
                    half = slice(64 * s, 64 * s + 64)
                    wait_emptied(pe, use + s)
                    nc.tensor.matmul(bank(use + s)[:, 0:P], b_qT[half, p, 0:P], kiT[half, 0:P], start=True,
                                     stop=True)
                    end_fill(nc.tensor.matmul(bank(use + s)[:, P:3 * P], b_qT[half, p, P:SEQ], kiT[half, :],
                                              start=True, stop=True), use + s)

            def bqt(g, use):
                pe.wait_ge(bq_norm, 2 * (g + 1))
                turn8(use, qs)

            def bs(arg, use):
                g, v = arg
                for i in range(2):
                    wait_read(pe, "bkt", 0, i)
                    wait_read(pe, "bqt", g, i)
                wait_emptied(pe, use)
                for i in range(4 if v == 0 else 2):
                    if v == 0:
                        ins = nc.tensor.matmul(bank(use)[:, i * P:i * P + P], b_qT[:, i, 0:P], b_kT[:, g, 0:P],
                                               start=True, stop=True)
                    else:
                        ins = nc.tensor.matmul(bank(use)[:, i * SEQ:i * SEQ + SEQ], b_qT[:, 2 * v - 2 + i, P:SEQ],
                                               b_kT[:, g, :], start=True, stop=True)
                end_fill(ins, use)

            def bp(arg, use):
                g, v = arg
                pe.wait_ge(b_exp, 3 * g + v + 1)
                wait_emptied(pe, use)
                for i in range(4):
                    ins = turn(bank(use)[:, i * P:i * P + P], b_p[:, i * P:i * P + P])
                end_fill(ins, use)

            def bo(arg, use):
                g, v = arg
                wait_read(pe, "bp", arg)
                wait_emptied(pe, use)
                for i in range(4):
                    val = kv[:, 0 if v == 0 else i % 2, 512 + g * P:512 + g * P + P]
                    o = i if v == 0 else i // 2
                    ins = nc.tensor.matmul(bank(use)[:, o * P:o * P + P], b_pT[:, i, :], val,
                                           start=(v == 0 or i % 2 == 0), stop=(v == 0 or i % 2 == 1))
                end_fill(ins, use)

            def at(j, use):
                wait_stored(pe, "aqk", j)
                turn8(use, a_s)

            def ae(h, use):
                half = slice(64 * (h % 2), 64 * (h % 2) + 64)
                for i in range(2):
                    wait_read(pe, "at", 0, i)
                    wait_read(pe, "at", 1, i)
                for i in range(2):
                    wait_emptied(pe, use + i)
                    b = bank(use + i)
                    if i == 0:
                        nc.tensor.matmul(b[:, 0:SEQ], sel[:, h, :], rows[:, 1, :], start=True, stop=True)
                        ins = nc.tensor.matmul(b[:, SEQ:3 * P], sel[:, h, :], rows[:, 1, P:SEQ], start=True,
                                               stop=True)
                    else:
                        nc.tensor.matmul(b[:, 0:SEQ], a_kT[half, h // 2, 0:P], a_qT[half, h // 2, :], start=True,
                                         stop=True)
                        ins = nc.tensor.matmul(b[:, SEQ:3 * P], a_kT[half, h // 2, P:SEQ],
                                               a_qT[half, h // 2, P:SEQ], start=True, stop=True)
                    end_fill(ins, use + i)

            def ap(h, use):
                wait_read(pe, "ae", h, 1)
                pe.wait_ge(a_one, 1)
                wait_stored(pe, "av", 1)
                wait_emptied(pe, use)
                w = HEAD + 1
                b = bank(use)
                nc.tensor.matmul(b[:, 0:w], a_p[:, 0:P], a_v[:, 0, h, :], start=True, stop=True)
                nc.tensor.matmul(b[:, 256:256 + w], a_p[:, P:2 * P], a_v[:, 0, h, :], start=True, stop=False)
                end_fill(nc.tensor.matmul(b[:, 256:256 + w], a_p[:, 2 * P:3 * P], a_v[:, 1, h, :], start=False,
                                          stop=True), use)

            def yt(i, use):
                if i < 4:
                    pe.wait_ge(a_y, H_A)
                elif i < 12:
                    wait_read(pe, "bo", (HKV - 1, 2))
                else:
                    pe.wait_ge(c_y, len(UNITS))
                wait_emptied(pe, use)
                for j in range(2):
                    for m in range(M):
                        ins = turn(bank(use)[:, j * SEQ + m * P:j * SEQ + m * P + P],
                                   y[:, m, (2 * i + j) * P:(2 * i + j) * P + P])
                end_fill(ins, use)

            def par_columns(_, use):
                pe.wait_ge(par_in_ready, PAR_DMAS)
                wait_emptied(pe, use)
                end_fill(turn(bank(use)[:, 0:R_N - R_CQ], par_in[0:R_N - R_CQ, :], R_N - R_CQ), use)
                wait_emptied(pe, use + 1)
                end_fill(turn(bank(use + 1)[:, 0:N_TAP], tap_in[0:N_TAP, :], N_TAP), use + 1)

            pieces = dict(par=par_columns, gt=gt, gb=gb, kx=kx, conv=conv, cn=cn, ca=ca, cg=cg, ct=ct, cm=cm, cu=cu, cv=cv, ck=ck,
                          cs=cs, cr=cr, co=co, bt=bt, bkt=bkt, bit=bit, bsc=bsc, bqt=bqt, bs=bs, bp=bp, bo=bo,
                          at=at, ae=ae, ap=ap, yt=yt)

            def x_columns(i):
                use = 1 + i
                pe.wait_ge(x_ready[i // 2], 16)
                wait_emptied(pe, use)
                for j in range(2):
                    for m in range(M):
                        ins = turn(bank(use)[:, j * SEQ + m * P:j * SEQ + m * P + P],
                                   xs[:, m, (2 * i + j) * P:(2 * i + j) * P + P])
                end_fill(ins, use)

            pe.wait_ge(const_ready, 1)
            pe.wait_ge(norm_in_ready, 16)
            end_fill(turn(bank(0)[:, 0:R_CQ], norm_in[0:R_CQ, :], R_CQ), 0)
            for i in range(AHEAD):
                x_columns(i)
            for c in range(len(chunks)):
                chunk(c)
                if c + AHEAD < NX:
                    x_columns(c + AHEAD)
                if c == NX:
                    pe.wait_ge(const_ready, 2)
                for name, arg, use in woven[c]:
                    if name in pieces:
                        pieces[name](arg, U0 + use)

        @block.scalar
        def _(act):
            steps = [0]
            func = nc.scalar.activation

            def step(ins):
                steps[0] += 1
                ins.then_inc(act_step, 1)
                act.wait_ge(act_step, steps[0])

            def done_bank(ins, use):
                ins.then_inc(emptied[use % 4], 1)

            def split_hi(c):
                act.wait_ge(raw_ready[c % RAW_BUFS], raw_count(c))
                if c >= SPLIT_BUFS:
                    d = c - SPLIT_BUFS
                    b = chunks[d][0]
                    if d == last[b]:
                        act.wait_ge(acc_ready, b + 1)
                    else:
                        act.wait_ge(split_used, d + 1 - b)
                n = len(chunks[c][1]) * blocks[chunks[c][0]]["width"]
                func(split_ap(w_hi, c), w_raw[:, c % RAW_BUFS, 0:n], ACT.Copy).then_inc(hi_ready, 1)

            def evac(b, _):
                blk = blocks[b]
                kind, arg, w = blk["kind"], blk["arg"], blk["width"]
                if kind in ("out1", "out2"):
                    return
                act.wait_ge(rstd_ready, 1)
                act.wait_ge(acc_ready, b + 1)
                if kind in ("silu", "ao", "az"):
                    for m in range(M):
                        dst = acc[b % 2][m][:] if kind == "az" else y[:, m, arg:arg + 512]
                        ins = func(dst, acc[b % 2][m][:], ACT.Sigmoid if kind == "ao" else ACT.Silu,
                                   scale=rstd[:, m:m + 1])
                        if m == 0:
                            step(ins)
                    ins.then_inc(az_ready if kind == "az" else acc_read[b % 2], 1)
                    return
                for m in range(M):
                    src = acc[b % 2][m][:, 0:w]
                    if kind == "gates":
                        dst = small[:, m, :]
                    elif kind == "conv":
                        dst = conv_stage(arg)[:, m, :]
                    elif kind == "cq":
                        dst = y[:, m, arg:arg + w]
                    elif kind == "bkv":
                        dst = kv[:, m, arg:arg + w]
                    elif kind in ("bi", "bq"):
                        dst = qs[:, m, :]
                    elif kind == "aqk":
                        dst = a_s[:, m, :]
                    else:
                        dst = a_v[:, m, 4 * arg:4 * arg + 4, 0:HEAD]
                        src = src.rearrange("p (h d) -> p h d", h=4)
                    if kind in ("bi", "bq"):
                        ins = func(dst, src, ACT.Copy)
                    else:
                        ins = func(dst, src, ACT.Copy, scale=rstd[:, m:m + 1])
                    if m == 0:
                        step(ins)
                ins.then_inc(acc_read[b % 2], 1)

            def gt(_, use):
                wait_filled(act, use)
                act.wait_ge(head_ready, 1)
                b = bank(use)
                func(rows[:, 0, :], b[0:8, 0:SEQ], ACT.Tanh, bias=hcol[:, 4:5], scale=1 / GATE_CAP).then_inc(g_act, 1)
                done_bank(func(rows[:, 1, :], b[0:8, SEQ:2 * SEQ], ACT.Tanh, bias=hcol[:, 5:6],
                               scale=1 / GATE_CAP), use)
                act.wait_ge(emptied[use % 4], use // 4 + 1)
                step(func(rows[:, 1, :], rows[:, 1, :], ACT.Exp, scale=-GATE_CAP))
                func(rows[:, 1, :], rows[:, 1, :], ACT.Ln, bias=1.0).then_inc(g_act, 1)
                wait_filled(act, use + 1)
                b = bank(use + 1)
                func(rows[:, 3, :], b[0:8, 0:SEQ], ACT.Exp, scale=-1.0).then_inc(g_act, 1)
                done_bank(func(rows[:, 2, :], b[0:8, SEQ:2 * SEQ], ACT.Identity, bias=hcol[:, 3:4]), use + 1)

            def g2(_, use):
                act.wait_ge(g_dve, 1)
                step(func(rows[:, 4, :], rows[:, 4, :], ACT.Exp, scale=-1.0))
                func(rows[:, 4, :], rows[:, 4, :], ACT.Ln, bias=1.0).then_inc(g_act, 1)

            def g4(_, use):
                act.wait_ge(g_dve, 2)
                func(rows[:, 5, 0:P], rows[:, 2, 0:P], ACT.Exp, bias=rows[:, 2, P - 1:P], scale=-1.0).then_inc(
                    g_rows, 1)
                act.wait_ge(g_dve, 3)
                func(rows[:, 4, :], rows[:, 4, :], ACT.Exp).then_inc(g_rows, 1)

            def gb(_, use):
                act.wait_ge(g_cols, 1)
                func(gder[:, 2:4, :], gcol[:, 0:2, :], ACT.Exp).then_inc(g_cols, 1)

            def conv(i, use):
                wait_read(act, "par", 0, 1)
                wait_filled(act, use)
                for j in range(2):
                    c = 2 * i + j
                    ins = func(cT[:, c, :], bank(use)[:, j * SEQ:j * SEQ + SEQ], ACT.Copy,
                               scale=par[:, R_N + 3 * CH + c:R_N + 3 * CH + c + 1])
                ins.then_inc(conv_y, 1)
                wait_read(act, "conv", i)
                t = cT[:, 2 * i:2 * i + 2, :].rearrange("p c t -> p (c t)")
                func(t, t, ACT.Silu).then_inc(conv_ready, 1)

            def csq(i, use):
                act.wait_ge(conv_ready, 12)
                func(c_square(i), cT[:, 2 * i:2 * i + 2, :].rearrange("p c t -> p (c t)"), ACT.Square).then_inc(
                    c_sq, 1)

            def cn(i, use):
                wait_filled(act, use)
                done_bank(func(c_norm(i), bank(use)[:], ACT.Ln, bias=eps[:]), use)

            def ce(i, use):
                wait_read(act, "cn", i)
                func(c_norm(i), c_norm(i), ACT.Exp, scale=-0.5).then_inc(c_r, 1)

            def ca(u, use):
                hg, m = UNITS[u]
                wait_read(act, "ca", u, 1)
                act.wait_ge(g_cols, 3)
                for a in range(4):
                    ins = func(c_gam[:, a, :], c_gam[:, a, :], ACT.Exp, bias=gder[:, m, 4 * hg + a:4 * hg + a + 1])
                ins.then_inc(c_gam_ready, 1)

            def ct(arg, use):
                wait_filled(act, use)
                done_bank(func(c_gam[:].rearrange("p a b -> p (a b)"), bank(use)[:], ACT.Copy), use)

            def cv(u, use):
                hg, m = UNITS[u]
                wait_filled(act, use)
                for a in range(4):
                    ins = func(c_v[:, a, :], bank(use)[:, a * P:a * P + P], ACT.Copy,
                               scale=gcol[:, 2 + m, 4 * hg + a:4 * hg + a + 1])
                done_bank(ins, use)

            def ck(u, use):
                hg, m = UNITS[u]
                wait_filled(act, use)
                for a in range(4):
                    ins = func(c_kd[:, a, :], bank(use)[:, a * P:a * P + P], ACT.Copy,
                               scale=gcol[:, 4, 4 * hg + a:4 * hg + a + 1])
                done_bank(ins, use)

            def cr(u, use):
                wait_filled(act, use)
                done_bank(func(c_v[:].rearrange("p a b -> p (a b)"), bank(use)[:], ACT.Copy), use)

            def co(u, use):
                hg, m = UNITS[u]
                wait_filled(act, use + 1)
                if m == 0:
                    done_bank(func(c_s[:].rearrange("p a b -> p (a b)"), bank(use + 1)[:], ACT.Copy), use + 1)
                    act.wait_ge(emptied[(use + 1) % 4], (use + 1) // 4 + 1)
                else:
                    for a in range(4):
                        ins = func(c_kb[:, a, :], bank(use + 1)[:, a * P:a * P + P], ACT.Copy,
                                   scale=gder[:, 2 + m, 4 * hg + a:4 * hg + a + 1])
                    done_bank(ins, use + 1)
                wait_read(act, "co", u)
                func(c_gam[:].rearrange("p a b -> p (a b)"), c_at[:].rearrange("p a b -> p (a b)"),
                     ACT.Square).then_inc(c_osq, 1)

            def bn(_, use):
                wait_stored(act, "cq", 512)
                for m in range(M):
                    ins = func(b_sq[:, 0:Q_LORA], y[:, m, 0:Q_LORA], ACT.Square, accum_out=st[:, 4 + m:5 + m])
                    if m == 0:
                        step(ins)
                ins.then_inc(cq_ss, 1)

            def bt(i, use):
                wait_filled(act, use)
                for j in range(min(2, QKT - 2 * i)):
                    kt = 2 * i + j
                    ins = func(cq_hi[:, kt, :], bank(use)[:, j * SEQ:j * SEQ + SEQ], ACT.Copy,
                               scale=par[:, R_CQ + kt:R_CQ + kt + 1])
                ins.then_inc(cq_hi_ready, 1)

            def head_norms(n):
                for m in range(M):
                    src = kv[:, m, 0:512] if n == 0 else qs[:, m, :]
                    func(b_sq[:, m * 512:m * 512 + 512], src, ACT.Square).then_inc(b_sq_ready, 1)

            def bkn(_, use):
                wait_stored(act, "bkv", 0)
                act.wait_ge(cq_ss, 1)
                head_norms(0)

            def bqn(g, use):
                wait_stored(act, "bq", g)
                head_norms(g + 1)

            def bkt(_, use):
                for i in range(2):
                    wait_filled(act, use + i)
                    done_bank(func(b_kT[:, 2 * i:2 * i + 2, :].rearrange("p a b -> p (a b)"), bank(use + i)[:],
                                   ACT.Copy, scale=par[:, R_KN:R_KN + 1]), use + i)

            def bit(j, use):
                for i in range(2):
                    wait_filled(act, use + i)
                    done_bank(func(b_qT[:, 2 * i:2 * i + 2, :].rearrange("p a b -> p (a b)"), bank(use + i)[:],
                                   ACT.Copy), use + i)

            def bsc(arg, use):
                j, p = arg
                for s in range(2):
                    h = 8 * j + 2 * p + s
                    wait_filled(act, use + s)
                    if h >= 2:
                        act.wait_ge(b_score, h - 1)
                    rl = (b_s, b_p)[s][:, 0:3 * P]
                    done_bank(func(rl, bank(use + s)[:, 0:3 * P], ACT.Relu), use + s)

            def bqt(g, use):
                for i in range(2):
                    wait_filled(act, use + i)
                    done_bank(func(b_qT[:, 2 * i:2 * i + 2, :].rearrange("p a b -> p (a b)"), bank(use + i)[:],
                                   ACT.Copy, scale=par[:, R_QN:R_QN + 1]), use + i)

            def bs(arg, use):
                g, v = arg
                n, w = (4, P) if v == 0 else (2, SEQ)
                act.wait_ge(b_max, 3 * g + v + 1)
                for i in range(n):
                    ins = func(b_p[:, i * w:i * w + w], b_s[:, i * w:i * w + w], ACT.Exp,
                               bias=st[:, 24 + i:25 + i], scale=HEAD ** -0.5, accum_out=st[:, 28 + i:29 + i])
                ins.then_inc(b_exp, 1)

            def bp(arg, use):
                wait_filled(act, use)
                done_bank(func(b_pT[:].rearrange("p a b -> p (a b)"), bank(use)[:], ACT.Copy), use)

            def at(j, use):
                dst = (a_qT, a_kT)[j]
                for i in range(2):
                    wait_filled(act, use + i)
                    done_bank(func(dst[:, 2 * i:2 * i + 2, :].rearrange("p a b -> p (a b)"), bank(use + i)[:],
                                   ACT.Copy, scale=(DQK ** -0.5, 1.0)[j]), use + i)

            def ae(h, use):
                wait_read(act, "ae", h)
                func(a_m[:, 0:SEQ], a_m[:, 0:SEQ], ACT.Exp, bias=gcol[:, 5, h:h + 1])
                func(a_m[:, SEQ:3 * P], a_m[:, SEQ:3 * P], ACT.Exp, bias=gcol[:, 6, h:h + 1]).then_inc(a_exp, 1)

            def ap(h, use):
                wait_read(act, "ap", h)
                for m in range(M):
                    ins = func(a_sq[:], a_h[:, m, :], ACT.Square, accum_out=st[:, 36 + m:37 + m])
                    if m == 0:
                        step(ins)
                ins.then_inc(a_ss, 1)

            def yt(i, use):
                wait_filled(act, use)
                for j in range(2):
                    kt = 2 * i + j
                    gain = y_gain(kt)
                    ins = func(op_hi[:, kt, :], bank(use)[:, j * SEQ:j * SEQ + SEQ], ACT.Copy,
                               scale=1.0 if gain is None else gain)
                ins.then_inc(y_hi_ready, 1)

            pieces = dict(evac=evac, gt=gt, g2=g2, g4=g4, gb=gb, conv=conv, csq=csq, cn=cn, ce=ce, ca=ca, ct=ct, cv=cv,
                          ck=ck, cr=cr, co=co, bn=bn, bt=bt, bkn=bkn, bqn=bqn, bkt=bkt, bit=bit, bsc=bsc, bqt=bqt,
                          bs=bs, bp=bp, at=at, ae=ae, ap=ap, yt=yt)

            def x_hi(i):
                use = 1 + i
                wait_filled(act, use)
                for j in range(2):
                    kt = 2 * i + j
                    ins = func(op_hi[:, kt, :], bank(use)[:, j * SEQ:j * SEQ + SEQ], ACT.Copy,
                               scale=par[:, R_NORM + kt:R_NORM + kt + 1])
                ins.then_inc(x_hi_ready, 1)

            def x_square(i):
                q, m = i // M, i % M
                act.wait_ge(x_ready[q], 16)
                func(y[:, m, 512 * q:512 * q + 512], xs[:, m, 512 * q:512 * q + 512], ACT.Square,
                     accum_out=ssq[:, m, q:q + 1]).then_inc(ss_ready, 1)

            act.wait_ge(emptied[0], 1)
            for c in range(AHEAD):
                x_hi(c)
                split_hi(c)
            for c in range(len(chunks)):
                if c + AHEAD < len(chunks):
                    split_hi(c + AHEAD)
                if c + AHEAD < NX:
                    x_hi(c + AHEAD)
                if c < NX - 1:
                    x_square(c)
                    if c == NX - 2:
                        x_square(c + 1)
                        act.wait_ge(par_in_ready, PAR_DMAS)
                        func(hcol[:, 4:6], hcol[:, 0:2], ACT.Copy, scale=1 / GATE_CAP)
                        func(hcol[:, 6:7], hcol[:, 2:3], ACT.Exp).then_inc(head_ready, 1)
                        act.wait_ge(const_ready, 2)
                for name, arg, use in woven[c]:
                    if name in pieces:
                        pieces[name](arg, U0 + use)

        @block.vector
        def _(dve):
            steps = [0]
            vec = nc.vector

            def step(ins):
                steps[0] += 1
                ins.then_inc(dve_step, 1)
                dve.wait_ge(dve_step, steps[0])

            def done_bank(ins, use):
                ins.then_inc(emptied[use % 4], 1)

            def split_lo(c):
                dve.wait_ge(hi_ready, c + 1)
                n = len(chunks[c][1]) * blocks[chunks[c][0]]["width"]
                vec.tensor_tensor(split_ap(w_lo, c), w_raw[:, c % RAW_BUFS, 0:n], split_ap(w_hi, c).bitcast(F32),
                                  ALU.subtract).then_inc(lo_ready, 1)

            def evac(b, _):
                blk = blocks[b]
                kind, arg = blk["kind"], blk["arg"]
                if kind == "out1":
                    dve.wait_ge(acc_ready, b + 1)
                    dve.wait_ge(x_again[arg], 16)
                    for m in range(M):
                        ins = vec.tensor_tensor(out_acc(arg)[:, m, :], acc[b % 2][m][:], out_acc(arg)[:, m, :],
                                                ALU.add)
                        if m == 0:
                            step(ins)
                    ins.then_inc(acc_read[b % 2], 1)
                elif kind == "out2":
                    dve.wait_ge(acc_ready, b + 1)
                    for m in range(M):
                        ins = vec.tensor_tensor(out_acc(arg)[:, m, :], acc[b % 2][m][:], out_acc(arg)[:, m, :],
                                                ALU.add)
                        if m == 0:
                            step(ins)
                    ins.then_inc(acc_read[b % 2], 1)
                elif kind == "az":
                    dve.wait_ge(az_ready, arg // 512 + 1)
                    wait_stored(dve, "ao", arg)
                    for m in range(M):
                        dst = y[:, m, arg:arg + 512]
                        ins = vec.tensor_tensor(dst, acc[b % 2][m][:], dst, ALU.mult)
                        if m == 0:
                            step(ins)
                    ins.then_inc(acc_read[b % 2], 1)

            def rsqrt_mean(v, n, signal=None):
                w = v.shape[1]
                r, t = newton[:, 0:w], newton2[:, 0:w]
                step(vec.tensor_scalar(v, v, 1.0 / n, EPS, ALU.mult, ALU.add))
                step(vec.tensor_scalar(r.bitcast(mybir.dt.int32), v.bitcast(mybir.dt.int32), -0.5, RSQRT, ALU.mult,
                                       ALU.add))
                for i in range(4):
                    step(vec.tensor_tensor(t, r, r, ALU.mult))
                    step(vec.scalar_tensor_tensor(t, t, -0.5, v, ALU.mult, ALU.mult))
                    ins = vec.scalar_tensor_tensor(v if i == 3 else r, t, 1.5, r, ALU.add, ALU.mult)
                    if i == 3 and signal is not None:
                        ins.then_inc(signal, 1)
                    else:
                        step(ins)

            def g1(_, use):
                dve.wait_ge(g_act, 3)
                step(vec.tensor_scalar(rows[:, 3, :], rows[:, 3, :], 1.0, None, ALU.add))
                step(vec.reciprocal(rows[:, 3, :], rows[:, 3, :]))
                wait_read(dve, "gt", 0, 1)
                vec.scalar_tensor_tensor(rows[:, 4, :], rows[:, 2, :], -1.0, rows[:, 2, :], ALU.mult,
                                         ALU.max).then_inc(g_dve, 1)

            def g3(_, use):
                dve.wait_ge(g_act, 4)
                step(vec.scalar_tensor_tensor(rows[:, 2, :], rows[:, 2, :], 0.0, rows[:, 4, :], ALU.max, ALU.add))
                step(vec.tensor_scalar(rows[:, 4, :], rows[:, 2, :], hcol[:, 6:7], -1.0, ALU.mult, ALU.mult))
                for m in range(M):
                    tok = slice(m * P, m * P + P)
                    ins = vec.tensor_tensor_scan(rows[:, 2, tok], ones[0:8, :], rows[:, 4, tok], 0.0, ALU.mult,
                                                 ALU.add)
                    if m == 0:
                        step(ins)
                ins.then_inc(g_dve, 1)
                dve.wait_ge(g_dve, 2)
                step(vec.tensor_tensor_scan(rows[:, 4, :], ones[0:8, 0:1].to_broadcast([8, SEQ]), rows[:, 1, :], 0.0,
                                            ALU.mult, ALU.add))
                step(vec.scalar_tensor_tensor(rows[:, 0, :], rows[:, 0, :], GATE_CAP, rows[:, 4, :], ALU.mult,
                                              ALU.add))
                step(vec.tensor_tensor_scan(rows[:, 1, :], rows[:, 0, :], rows[:, 0, :], 0.0, ALU.max, ALU.max))
                step(vec.tensor_scalar(rows[:, 1, :], rows[:, 1, :], -1.0, None, ALU.mult))
                vec.tensor_tensor(rows[:, 4, :], rows[:, 4, :], rows[:, 1, :], ALU.add).then_inc(g_dve, 1)

            def gb(_, use):
                wait_filled(dve, use)
                done_bank(vec.tensor_copy(gcol[:].rearrange("p a b -> p (a b)"), bank(use)[:, 0:72]), use)
                dve.wait_ge(emptied[use % 4], use // 4 + 1)
                vec.tensor_scalar(gder[:, 0:2, :], gcol[:, 0:2, :], -1.0, None, ALU.mult).then_inc(g_cols, 1)
                dve.wait_ge(g_cols, 2)
                vec.scalar_tensor_tensor(gder[:, 4:6, :], gcol[:, 2:4, :], -1.0, gder[:, 2:4, :], ALU.mult,
                                         ALU.mult).then_inc(g_cols, 1)

            def kn(_, use):
                wait_stored(dve, "gates")
                for m in range(M):
                    step(vec.tensor_scalar(small[:, m, G_WI:G_WI + IDX_H], small[:, m, G_WI:G_WI + IDX_H],
                                           IDX_H ** -0.5 * IDX_D ** -0.5, None, ALU.mult))
                    step(vec.bn_stats(st[:, 32:38], small[:, m, G_KI:G_KI + IDX_D]))
                    step(vec.bn_aggr(st[:, 38:40], st[:, 32:38]))
                    step(vec.tensor_copy(st[:, 18 + m:19 + m], st[:, 38:39]))
                    step(vec.tensor_copy(st[:, 20 + m:21 + m], st[:, 39:40]))
                rsqrt_mean(st[:, 20:22], 1)
                for m in range(M):
                    for i in range(2):
                        ins = vec.tensor_scalar(kdup[:, m, i * IDX_D:(i + 1) * IDX_D], small[:, m, G_KI:G_KI + IDX_D],
                                                st[:, 18 + m:19 + m], st[:, 20 + m:21 + m], ALU.subtract, ALU.mult)
                        if (m, i) != (1, 1):
                            step(ins)
                ins.then_inc(k_dup, 1)

            def kx(_, use):
                wait_filled(dve, use)
                done_bank(vec.tensor_scalar(kiT[:], bank(use)[:, 0:SEQ], par[:, R_KIG:R_KIG + 1],
                                            par[:, R_KIB:R_KIB + 1], ALU.mult, ALU.add), use)
                dve.wait_ge(emptied[use % 4], use // 4 + 1)

            def conv(i, use):
                dve.wait_ge(conv_y, i + 1)
                for d in range(1, CONV_K):
                    for j in range(2):
                        c = 2 * i + j
                        row = R_N + (CONV_K - 1 - d) * CH + c
                        ins = vec.scalar_tensor_tensor(cT[:, c, d:SEQ], bank(use)[:, j * SEQ:j * SEQ + SEQ - d],
                                                       par[:, row:row + 1], cT[:, c, d:SEQ], ALU.mult, ALU.add)
                        if (d, j) != (CONV_K - 1, 1):
                            step(ins)
                done_bank(ins, use)

            def ce(i, use):
                dve.wait_ge(c_r, i + 1)
                g = c_norm(i)
                t = cT[:, 2 * i:2 * i + 2, :].rearrange("p c t -> p (c t)")
                if i < 4:
                    ins = vec.scalar_tensor_tensor(t, t, HEAD ** -0.5, g, ALU.mult, ALU.mult)
                else:
                    ins = vec.tensor_tensor(t, t, g, ALU.mult)
                ins.then_inc(c_nd, 1)

            def ca(u, use):
                hg, m = UNITS[u]
                wait_filled(dve, use)
                dve.wait_ge(c_nd, 8)
                done_bank(vec.tensor_tensor(c_kb[:], bank(use)[:].rearrange("p (a b) -> p a b", a=4),
                                            cT[:, 8 + 4 * hg:12 + 4 * hg, m * P:m * P + P], ALU.mult), use)
                wait_filled(dve, use + 1)
                done_bank(vec.tensor_tensor(c_gam[:], bank(use + 1)[:].rearrange("p (a b) -> p a b", a=4),
                                            tri[:, 0:1, :].to_broadcast([P, 4, P]), ALU.add), use + 1)

            def cg(u, use):
                dve.wait_ge(c_gam_ready, u + 1)
                for i, dst in enumerate((c_at, c_bt)):
                    wait_filled(dve, use + i)
                    done_bank(vec.tensor_tensor(dst[:], bank(use + i)[:].rearrange("p (a b) -> p a b", a=4), c_gam[:],
                                                ALU.mult), use + i)
                    dve.wait_ge(emptied[(use + i) % 4], (use + i) // 4 + 1)
                step(vec.tensor_tensor(c_u[:], c_at[:], level[:, 0:1, :].to_broadcast([P, 4, P]), ALU.mult))
                vec.tensor_tensor(c_u[:], ident[:].unsqueeze(1).to_broadcast([P, 4, P]), c_u[:],
                                  ALU.subtract).then_inc(c_u0, 1)

            def cm(arg, use):
                u, lv = arg
                wait_filled(dve, use)
                done_bank(vec.tensor_tensor(c_kb[:], bank(use)[:].rearrange("p (a b) -> p a b", a=4),
                                            level[:, lv:lv + 1, :].to_broadcast([P, 4, P]), ALU.mult), use)

            def cu(arg, use):
                wait_filled(dve, use)
                u4 = c_u[:].rearrange("p a b -> p (a b)")
                done_bank(vec.tensor_tensor(u4, u4, bank(use)[:], ALU.subtract), use)

            def cs(u, use):
                hg, m = UNITS[u]
                wait_filled(dve, use)
                wait_read(dve, "cv", u)
                for a in range(4):
                    ins = vec.scalar_tensor_tensor(c_v[:, a, :], bank(use)[:, a * P:a * P + P],
                                                   gder[:, 4 + m, 4 * hg + a:4 * hg + a + 1], c_v[:, a, :],
                                                   ALU.mult, ALU.add)
                    if a < 3:
                        step(ins)
                done_bank(ins, use)

            def co(u, use):
                hg, m = UNITS[u]
                wait_filled(dve, use)
                o = c_at[:].rearrange("p a b -> p (a b)")
                wait_read(dve, "co", u, 1)
                if m == 0:
                    done_bank(vec.tensor_copy(o, bank(use)[:]), use)
                else:
                    done_bank(vec.tensor_tensor(o, bank(use)[:], c_kb[:].rearrange("p a b -> p (a b)"), ALU.add), use)
                dve.wait_ge(c_osq, u + 1)
                step(vec.tensor_reduce(st[:, 0:4], c_gam[:], AX_X, ALU.add))
                rsqrt_mean(st[:, 0:4], HEAD)
                for a in range(4):
                    h = 4 * hg + a
                    dst = y[:, m, W_A + W_B + h * P:W_A + W_B + h * P + P]
                    ins = vec.scalar_tensor_tensor(dst, c_at[:, a, :], st[:, a:a + 1], dst, ALU.mult, ALU.mult)
                    if a < 3:
                        step(ins)
                ins.then_inc(c_y, 1)

            def bn(_, use):
                dve.wait_ge(cq_ss, 1)
                rsqrt_mean(st[:, 4:6], Q_LORA)
                for m in range(M):
                    vec.tensor_scalar(y[:, m, 0:Q_LORA], y[:, m, 0:Q_LORA], st[:, 4 + m:5 + m], None,
                                      ALU.mult).then_inc(cq_norm, 1)

            def bt(i, use):
                dve.wait_ge(cq_hi_ready, i + 1)
                for j in range(min(2, QKT - 2 * i)):
                    kt = 2 * i + j
                    ins = vec.scalar_tensor_tensor(cq_lo[:, kt, :], bank(use)[:, j * SEQ:j * SEQ + SEQ],
                                                   par[:, R_CQ + kt:R_CQ + kt + 1], cq_hi[:, kt, :].bitcast(F32),
                                                   ALU.mult, ALU.subtract)
                    if j == 0 and i < 3:
                        step(ins)
                done_bank(ins, use)

            def head_norms(n, norm):
                dve.wait_ge(b_sq_ready, M * (n + 1))
                for m in range(M):
                    ins = vec.tensor_reduce(st[:, 8 + 4 * m:12 + 4 * m],
                                            b_sq[:, m * 512:m * 512 + 512].rearrange("p (h d) -> p h d", h=4), AX_X,
                                            ALU.add)
                    step(ins)
                rsqrt_mean(st[:, 8:16], HEAD)
                for m in range(M):
                    v = (kv[:, m, 0:512] if n == 0 else qs[:, m, :]).rearrange("p (h d) -> p h d", h=4)
                    vec.tensor_tensor(v, v, st[:, 8 + 4 * m:12 + 4 * m].unsqueeze(2).to_broadcast([P, 4, P]),
                                      ALU.mult).then_inc(norm, 1)

            def bkn(_, use):
                head_norms(0, bk_norm)

            def bqn(g, use):
                head_norms(g + 1, bq_norm)

            def bsc(arg, use):
                j, p = arg
                for s in range(2):
                    h = 8 * j + 2 * p + s
                    wait_read(dve, "bsc", arg, s)
                    rl = (b_s, b_p)[s]
                    for m in range(M):
                        cols = slice(0, P) if m == 0 else slice(P, 3 * P)
                        w = small[:, m, G_WI + h:G_WI + h + 1]
                        if h == 0:
                            ins = vec.tensor_scalar(sc[:, cols], rl[:, cols], w, None, ALU.mult)
                        else:
                            ins = vec.scalar_tensor_tensor(sc[:, cols], rl[:, cols], w, sc[:, cols], ALU.mult,
                                                           ALU.add)
                        if m == 0:
                            step(ins)
                    ins.then_inc(b_score, 1)
                    dve.wait_ge(b_score, h + 1)

            def btk(arg, use):
                m, part = arg
                cols = slice(0, P) if m == 0 else slice(P, 3 * P)
                w = P * (m + 1)
                work = b_s[:, 0:w]
                if part == 0:
                    diag = sc[:, 2 * m * P:2 * m * P + P]
                    step(vec.tensor_tensor(diag, diag, cap[:], ALU.min))
                    step(vec.tensor_copy(work, sc[:, cols]))
                for r in range(part, min(part + 3 - m, TOPK // 8)):
                    step(vec.max(top8[:], work))
                    if r < TOPK // 8 - 1:
                        step(vec.match_replace(work, top8[:], work, -3.4028234e38))

            def bts(arg, use):
                m, part = arg
                cols = slice(0, P) if m == 0 else slice(P, 3 * P)
                w = P * (m + 1)
                work = b_s[:, 0:w]
                gt_, eq = b_p[:, 0:w], b_p[:, 256:256 + w]
                thr = top8[:, 7:8]
                if part == 1:
                    step(vec.tensor_tensor_scan(work, ones[:, 0:1].to_broadcast([P, w]), eq, 0.0, ALU.mult, ALU.add))
                    step(vec.scalar_tensor_tensor(work, work, st[:, 40:41], eq, ALU.is_le, ALU.mult))
                    step(vec.tensor_tensor(work, work, gt_, ALU.add))
                    step(vec.tensor_scalar(sc[:, cols], work, 1.0, -NEG, ALU.subtract, ALU.mult))
                    diag = sc[:, 2 * m * P:2 * m * P + P]
                    step(vec.tensor_tensor(diag, diag, low[:], ALU.min))
                    return
                step(vec.tensor_scalar(gt_, sc[:, cols], thr, None, ALU.is_gt))
                step(vec.tensor_reduce(st[:, 40:41], gt_, AX_X, ALU.add))
                step(vec.tensor_scalar(st[:, 40:41], st[:, 40:41], -1.0, float(TOPK), ALU.mult, ALU.add))
                step(vec.tensor_scalar(eq, sc[:, cols], thr, None, ALU.is_equal))

            def bs(arg, use):
                g, v = arg
                n, w = (4, P) if v == 0 else (2, SEQ)
                sel_ = (sc[:, 0:P] if v == 0 else sc[:, P:3 * P]).unsqueeze(1).to_broadcast([P, n, w])
                s3 = b_s[:].rearrange("p (h k) -> p h k", h=n)
                wait_filled(dve, use)
                done_bank(vec.tensor_tensor(s3, bank(use)[:].rearrange("p (h k) -> p h k", h=n), sel_, ALU.add), use)
                dve.wait_ge(emptied[use % 4], use // 4 + 1)
                step(vec.tensor_reduce(st[:, 24:24 + n], s3, AX_X, ALU.max))
                vec.tensor_scalar(st[:, 24:24 + n], st[:, 24:24 + n], -HEAD ** -0.5, None, ALU.mult).then_inc(b_max, 1)
                dve.wait_ge(b_exp, 3 * g + v + 1)
                step(vec.reciprocal(st[:, 28:28 + n], st[:, 28:28 + n]))

            def bo(arg, use):
                g, v = arg
                m = 0 if v == 0 else 1
                wait_filled(dve, use)
                for i in range(4 if v == 0 else 2):
                    h = 4 * g + (i if v == 0 else 2 * v - 2 + i)
                    dst = y[:, m, W_A + h * P:W_A + h * P + P]
                    ins = vec.scalar_tensor_tensor(dst, bank(use)[:, i * P:i * P + P], st[:, 28 + i:29 + i], dst,
                                                   ALU.mult, ALU.mult)
                    if i < (3 if v == 0 else 1):
                        step(ins)
                done_bank(ins, use)

            def at(j, use):
                if j == 0:
                    vec.memset(a_v[:, :, :, HEAD:HEAD + 1], 1.0).then_inc(a_one, 1)

            def ae(h, use):
                wait_filled(dve, use)
                done_bank(vec.tensor_tensor(a_m[:], bank(use)[:, 0:3 * P], tri[:].rearrange("p a b -> p (a b)"),
                                            ALU.add), use)
                dve.wait_ge(a_exp, h + 1)
                wait_filled(dve, use + 1)
                done_bank(vec.tensor_tensor(a_p[:], bank(use + 1)[:, 0:3 * P], a_m[:], ALU.mult), use + 1)

            def ap(h, use):
                wait_filled(dve, use)
                b2 = bank(use)[:].rearrange("p (m c) -> p m c", m=M)
                step(vec.tensor_copy(st[:, 40:42], b2[:, :, HEAD]))
                step(vec.scalar_tensor_tensor(st[:, 40:42], st[:, 40:42], -1.0, st[:, 40:42], ALU.mult, ALU.max))
                step(vec.tensor_tensor(st[:, 40:42], st[:, 40:42], gcol[:, 7:9, h], ALU.max))
                step(vec.reciprocal(st[:, 40:42], st[:, 40:42]))
                for m in range(M):
                    ins = vec.tensor_scalar(a_h[:, m, :], b2[:, m, 0:HEAD], st[:, 40 + m:41 + m], None, ALU.mult)
                    if m == 0:
                        step(ins)
                done_bank(ins, use)

            def ay(h, use):
                dve.wait_ge(a_ss, h + 1)
                rsqrt_mean(st[:, 36:38], HEAD)
                for m in range(M):
                    dst = y[:, m, h * P:h * P + P]
                    ins = vec.scalar_tensor_tensor(dst, a_h[:, m, :], st[:, 36 + m:37 + m], dst, ALU.mult, ALU.mult)
                    if m == 0:
                        step(ins)
                ins.then_inc(a_y, 1)

            y_done = [0]

            def yt(i, use):
                y_done[0] += 1
                dve.wait_ge(y_hi_ready, y_done[0])
                for j in range(2):
                    kt = 2 * i + j
                    gain = y_gain(kt)
                    src, hi = bank(use)[:, j * SEQ:j * SEQ + SEQ], op_hi[:, kt, :].bitcast(F32)
                    if gain is None:
                        ins = vec.tensor_tensor(op_lo[:, kt, :], src, hi, ALU.subtract)
                    else:
                        ins = vec.scalar_tensor_tensor(op_lo[:, kt, :], src, gain, hi, ALU.mult, ALU.subtract)
                    if j == 0:
                        step(ins)
                done_bank(ins, use)

            def par_columns(_, use):
                for i, (c0, n) in enumerate(((R_CQ, R_N - R_CQ), (R_N, N_TAP))):
                    wait_filled(dve, use + i)
                    done_bank(vec.tensor_copy(par[:, c0:c0 + n], bank(use + i)[:, 0:n]), use + i)

            pieces = dict(par=par_columns, evac=evac, g1=g1, g3=g3, gb=gb, kn=kn, kx=kx, conv=conv, ce=ce, ca=ca, cg=cg, cm=cm, cu=cu, cs=cs,
                          co=co, bn=bn, bt=bt, bkn=bkn, bqn=bqn, bsc=bsc, btk=btk, bts=bts, bs=bs, bo=bo, at=at, ae=ae, ap=ap, ay=ay,
                          yt=yt)

            def x_lo(i):
                use = 1 + i
                dve.wait_ge(x_hi_ready, i + 1)
                for j in range(2):
                    kt = 2 * i + j
                    ins = vec.scalar_tensor_tensor(op_lo[:, kt, :], bank(use)[:, j * SEQ:j * SEQ + SEQ],
                                                   par[:, R_NORM + kt:R_NORM + kt + 1], op_hi[:, kt, :].bitcast(F32),
                                                   ALU.mult, ALU.subtract)
                    if j == 0:
                        step(ins)
                done_bank(ins, use)

            wait_filled(dve, 0)
            done_bank(vec.tensor_copy(par[:, 0:R_CQ], bank(0)[:, 0:R_CQ]), 0)
            dve.wait_ge(emptied[0], 1)
            for c in range(AHEAD):
                x_lo(c)
                split_lo(c)
            for c in range(len(chunks)):
                if c + AHEAD < len(chunks):
                    split_lo(c + AHEAD)
                if c + AHEAD < NX:
                    x_lo(c + AHEAD)
                if c == NX - 1:
                    dve.wait_ge(ss_ready, NX)
                    step(vec.tensor_reduce(rstd[:], ssq[:], AX_X, ALU.add))
                    rsqrt_mean(rstd[:], D, rstd_ready)
                    dve.wait_ge(const_ready, 2)
                for name, arg, use in woven[c]:
                    if name in pieces:
                        pieces[name](arg, U0 + use)


_INS = ["x", "norm_g", "w_in", "w_out", "m_ib", "m_fb", "m_norm_g", "a_cq_g", "a_wuq", "a_wuqi", "a_qn_g", "a_kn_g",
        "a_ki_g", "a_ki_b", "d_conv_w", "d_a_log", "d_dt_bias", "d_norm_g"]
_OUTS = [((1, SEQ, D), "float32")]


def kernel(**inputs):
    import numpy as _np
    import concourse.bacc as _bacc
    from concourse import mybir as _mybir
    from concourse.bass_utils import run_bass_kernel_spmd as _run

    nc = _bacc.Bacc("TRN2", target_bir_lowering=False, num_devices=1)
    arrays, args = {}, []
    for name in _INS:
        a = _np.ascontiguousarray(inputs[name])
        arrays[f"in_{name}_dram"] = a
        args.append(nc.dram_tensor(f"in_{name}_dram", a.shape, _mybir.dt.from_np(a.dtype), kind="ExternalInput").ap())
    for i, (shape, dtype) in enumerate(_OUTS):
        dt = _mybir.dt.from_np(_np.dtype(dtype))
        args.append(nc.dram_tensor(f"out_{i}_dram", shape, dt, kind="ExternalOutput").ap())
    hybrid_kernel(nc, *args)
    r = _run(nc, [arrays], core_ids=[0])
    return r.results[0]["out_0_dram"]
```

```python
from contextlib import ExitStack

import concourse.bass as bass
from concourse import mybir

F32 = mybir.dt.float32
F32R = mybir.dt.float32r
BF16 = mybir.dt.bfloat16
ALU = mybir.AluOpType
ACT = mybir.ActivationFunctionType
AX_X = mybir.AxisListType.X

P = 128
D = 4096
SEQ = 256
M = SEQ // P
KT = D // P
HEAD = 128
W_A, W_B, W_C = D // 4, D // 2, D // 4
H_A, H_B, H_C = W_A // HEAD, W_B // HEAD, W_C // HEAD
DQK = HEAD // 2
GATE_CAP = 15.0
HKV = 4
Q_LORA = 896
QKT = Q_LORA // P
IDX_H, IDX_D = 16, 64
TOPK = min(256, SEQ // 4)
CONV_K = 4
EPS = 1e-6
NEG = -1e30
BIG = 3.3e38

C_AQ = 0
C_AK = C_AQ + H_A * DQK
C_AV = C_AK + H_A * DQK
C_AI = C_AV + W_A
C_AO = C_AI + 2 * H_A
C_AZ = C_AO + W_A
C_BCQ = C_AZ + W_A
C_BK = C_BCQ + Q_LORA
C_BV = C_BK + HKV * HEAD
C_BKI = C_BV + HKV * HEAD
C_BZ = C_BKI + IDX_D + IDX_H
C_CQKV = C_BZ + W_B
C_CB = C_CQKV + 3 * W_C
C_CZ = C_CB + 2 * H_C

G_AI, G_AF, G_CB, G_CA, G_KI, G_WI, G_W = 0, 8, 16, 24, 32, 96, 112

R_NORM, R_CQ, R_QN, R_KN, R_KIG, R_KIB, R_MN, R_DN, R_N = 0, 32, 39, 40, 41, 42, 43, 51, 52
N_TAP = CONV_K * 3 * W_C // P
CH = 3 * W_C // P

CHUNK_KT = 2
RAW_BUFS = 4
SPLIT_BUFS = 4
AHEAD = SPLIT_BUFS - 1
X_AHEAD = 2
NX = KT // 2
X_PARTS = [(0, SEQ), (SEQ, 512)] + [(q, q + 512) for q in range(512, D, 512)]
RSQRT = 1597463007.0
NEWTON = 3
LEVELS = 7
UNITS = [(hg, m) for hg in range(H_C // 4) for m in range(M)]

USES = {"par": 2, "gt": 2, "gb": 1, "kx": 1, "conv": 1, "cn": 1, "ca": 2, "cg": 2, "ct": 1, "cm": 1, "cu": 1, "cv": 1,
        "ck": 1, "cs": 1, "cr": 1, "co": 2, "bt": 1, "bkt": 2, "bit": 2, "bsc": 2, "bqt": 2, "bs": 1, "bp": 1,
        "bo": 1, "at": 2, "ae": 2, "ap": 1, "yt": 1}


def plan():
    blocks = []

    def block(kind, arg, operand, kts, per, width, matrix, col):
        blocks.append(dict(kind=kind, arg=arg, operand=operand, kts=kts, per=per, width=width, matrix=matrix,
                           col=col))

    full = list(range(KT))

    def project(kind, arg, col, width=512):
        block(kind, arg, "h", full, CHUNK_KT, width, "w_in", col)

    for j in range(6):
        project("conv", j, C_CQKV + 512 * j)
    project("gates", 512, C_BCQ + 512, Q_LORA - 512 + G_W)
    for j in range(2):
        project("silu", W_A + W_B + 512 * j, C_CZ + 512 * j)
    project("cq", 0, C_BCQ)
    project("bkv", 0, C_BK)
    project("bkv", 512, C_BV)
    for j in range(4):
        project("silu", W_A + 512 * j, C_BZ + 512 * j)
    for j in range(2):
        block("bi", j, "cq", list(range(QKT)), CHUNK_KT, 512, "wuqi", 512 * j)
    for j in range(4):
        project(("ao", "az")[j // 2], 512 * (j % 2), (C_AO, C_AZ)[j // 2] + 512 * (j % 2))
        block("bq", j, "cq", list(range(QKT)), CHUNK_KT, 512, "wuq", 512 * j)
    project("aqk", 0, C_AQ)
    project("aqk", 1, C_AK)
    project("av", 0, C_AV)
    project("av", 1, C_AV + 512)
    kt_a = W_A // P
    for n in range(D // 512):
        block("out1", n, "y", full[kt_a:], CHUNK_KT, 512, "w_out", 512 * n)
    for n in range(D // 512):
        block("out2", n, "y", full[:kt_a], CHUNK_KT, 512, "w_out", 512 * n)

    chunks, last = [], []
    for b, blk in enumerate(blocks):
        for i in range(0, len(blk["kts"]), blk["per"]):
            chunks.append((b, blk["kts"][i:i + blk["per"]]))
        last.append(len(chunks) - 1)

    woven = [[] for _ in chunks]

    def end(kind, arg=0):
        return next(last[b] for b, x in enumerate(blocks) if x["kind"] == kind and x["arg"] == arg)

    def weave(at, pieces, every=1):
        for piece in pieces:
            woven[at] += [] if piece is None else piece if isinstance(piece, list) else [piece]
            at += every
        return at

    for b, x in enumerate(blocks):
        woven[last[b]].append(("evac", b))
    woven[NX - 1].append(("par", 0))
    for j in range(6):
        at = weave(end("conv", j) + 2, [("conv", 2 * j), ("conv", 2 * j + 1)], 6)
    for i in range(10):
        at = weave(at, [([("csq", i)] if i < 8 else []) + ([("cn", i - 2)] if i > 1 else [])])
    g_end = weave(max(at, end("gates", 512) + 2), [(name, 0) for name in ("gt", "g1", "g2", "g3", "g4", "gb", "gs")], 2)
    at = max(weave(at + 1, [("ce", i) for i in range(8)]), g_end)
    weave(at + 4, [("kn", 0), ("kr", 0), ("kd", 0), ("kx", 0)], 3)
    for u, (hg, m) in enumerate(UNITS):
        at = weave(at, [("ca", u), None, ("cg", u), None])
        for lv in range(1, LEVELS):
            at = weave(at, [("ct", (u, lv)), ("cm", (u, lv)), ("cu", (u, lv))])
        at = weave(at, [("cv", u), ("ck", u) if m == 0 else ("cs", u), ("cr", u), ("co", u), ("cy", u), None])
    at = max(at, end("bkv", 512) + 1)
    at = weave(at, [("bn", 0), None, None, ("bkn", 0), None, None] + [("bt", i) for i in range(4)] + [("bkt", 0)])
    assert at <= end("silu", W_A + 512 * 3) + 1, (at, end("silu", W_A + 512 * 3))
    at = weave(end("bi", 0) + 1, [("bit", 0)] + [("bsc", (0, p)) for p in range(4)])
    at = weave(max(at, end("bi", 1) + 1), [("bit", 1)] + [("bsc", (1, p)) for p in range(4)])
    for m in range(M):
        at = weave(at, [("btk", (m, i)) for i in range(0, TOPK // 8, 3 - m)] + [("bts", (m, 0)), ("bts", (m, 1))])
    assert at <= end("bq", 0) + 1, (at, end("bq", 0))
    for g in range(HKV):
        at = weave(end("bq", g) + 1, [("bqn", g), None, None, ("bqt", g)])
        for v in range(3):
            at = weave(at, [("bs", (g, v)), None, ("bp", (g, v)), ("bo", (g, v))])
    assert at <= end("aqk", 0) + 1, (at, end("aqk", 0))
    weave(end("aqk", 0) + 1, [("at", 0)])
    weave(end("aqk", 1) + 1, [("at", 1)])
    first = end("av", 0) + 1
    weave(first + 4, [("yt", i) for i in range(4, 16)])
    at = end("av", 1) + 2
    for h in range(H_A):
        at = weave(at, [("ae", h), None, None, ("ap", h), None, None, ("ay", h), None])
    at = weave(at + 1, [("yt", i) for i in range(4)], 2)
    assert at <= end("out1", 7), (at, end("out1", 7))

    use = 0
    for slot in woven:
        for i, (name, arg) in enumerate(slot):
            slot[i] = (name, arg, use)
            use += USES.get(name, 0)
    return blocks, chunks, last, woven, use


def hybrid_kernel(nc, x, norm_g, w_in, w_out, m_ib, m_fb, m_norm_g, a_cq_g, a_wuq, a_wuqi, a_qn_g, a_kn_g,
                  a_ki_g, a_ki_b, d_conv_w, d_a_log, d_dt_bias, d_norm_g, out):
    blocks, chunks, last, woven, _ = plan()
    U0 = NX + 1

    matrix = {
        "w_in": w_in[0].rearrange("(kt p) n -> p kt n", p=P),
        "w_out": w_out[0].rearrange("(kt p) n -> p kt n", p=P),
        "wuq": a_wuq[0].rearrange("(kt p) n -> p kt n", p=P),
        "wuqi": a_wuqi[0].rearrange("(kt p) n -> p kt n", p=P),
    }
    x_dram = x[0].rearrange("(m p) d -> p m d", p=P)
    out_dram = out[0].rearrange("(m p) d -> p m d", p=P)

    with ExitStack() as ctx:
        def sb(name, shape, dt=F32, stack=ctx):
            return stack.enter_context(nc.sbuf_tensor(name, shape, dt))

        def sem(name):
            return ctx.enter_context(nc.semaphore(name))

        def region(names):
            with ExitStack() as stack:
                return [sb(n, s, d, stack) for n, s, d in names]

        acc = [[ctx.enter_context(nc.psum_tensor(f"acc{b}{m}", [P, 512], F32)) for m in range(M)] for b in range(2)]
        mix = [ctx.enter_context(nc.psum_tensor(f"mix{b}", [P, 512], F32)) for b in range(4)]

        op_hi = sb("op_hi", [P, KT, SEQ], F32R)
        op_lo = sb("op_lo", [P, KT, SEQ], F32R)
        w_raw = sb("w_raw", [P, RAW_BUFS, 1024])
        w_hi = sb("w_hi", [P, SPLIT_BUFS, 1024], F32R)
        w_lo = sb("w_lo", [P, SPLIT_BUFS, 1024], F32R)
        _, csq_hi, _, csq_lo = region([("y_0", [P, W_A + 1024], F32), ("csq_hi", [P, 2, 512], F32R),
                                       ("y_1", [P, D - 1024], F32), ("csq_lo", [P, 2, 512], F32R)])
        y = sb("y", [P, M, D])
        kv = sb("kv", [P, M, 1024])
        ident = sb("ident", [P, P])
        ones = sb("ones", [P, P], F32R)
        sel = sb("sel", [8, 8, P], F32R)
        level = sb("level", [P, LEVELS, P], BF16)
        tri = sb("tri", [P, 2, P], BF16)
        cap = sb("cap", [P, P], BF16)
        low = sb("low", [P, P], BF16)
        par = sb("par", [P, R_N + N_TAP])
        small = sb("small", [P, M, G_W])
        rows_r, = region([("rows_r", [8, 6, SEQ], F32R)])
        rows = sb("rows", [8, 6, SEQ])
        gcol = sb("gcol", [P, 9, 8])
        gder = sb("gder", [P, 6, 8])
        hcol = sb("hcol", [8, 8])
        eps = sb("eps", [P, 1])
        ssq = sb("ssq", [P, M, NX // M])
        rstd = sb("rstd", [P, M])
        newton = sb("newton", [P, 8])
        newton2 = sb("newton2", [P, 8])
        newton_act = sb("newton_act", [P, 1])
        st = sb("st", [P, 48])
        kiT = sb("kiT", [P, SEQ])

        xs, norm_in = region([("xs", [P, M, D], F32), ("norm_in", [P, P], F32)])
        _, par_in, tap_in = region([("xs_", [P, M, D + P], F32), ("par_in", [P, P], F32), ("tap_in", [P, P], F32)])
        cT, c_kb, c_gam, c_at, c_bt, c_u, c_v, c_kd = region(
            [("cT", [P, CH, SEQ], F32)] + [(n, [P, 4, P], F32) for n in
             ("c_kb", "c_gam", "c_at", "c_bt", "c_u", "c_v", "c_kd")])
        c_s = c_kd
        kdup = kv[:, 1, 512:512 + SEQ].rearrange("p (m d) -> p m d", m=M)
        cq_hi, cq_lo, qs, b_sq, b_qT, b_kT, sc, b_s, b_p, b_pT, top8 = region(
            [("cq_hi", [P, QKT, SEQ], F32R), ("cq_lo", [P, QKT, SEQ], F32R), ("qs", [P, M, 512], F32),
             ("b_sq", [P, 1024], F32), ("b_qT", [P, 4, SEQ], F32), ("b_kT", [P, HKV, SEQ], F32),
             ("sc", [P, 3 * P], F32), ("b_s", [P, 512], F32), ("b_p", [P, 512], F32),
             ("b_pT", [P, 4, P], F32), ("top8", [P, 8], F32)])
        a_s, a_qT, a_kT, a_v, a_m, a_p, a_h, a_sq, acc0 = region(
            [("a_s", [P, M, 512], F32), ("a_qT", [P, 4, SEQ], F32), ("a_kT", [P, 4, SEQ], F32),
             ("a_v", [P, M, H_A, HEAD + 1], F32), ("a_m", [P, 3 * P], F32), ("a_p", [P, 3 * P], F32),
             ("a_h", [P, M, P], F32), ("a_sq", [P, P], F32), ("acc0", [P, M, W_A], F32)])

        par_in_ready = sem("par_in_ready")
        norm_in_ready = sem("norm_in_ready")
        x_ready = [sem(f"x_ready{q}") for q in range(len(X_PARTS))]
        raw_ready = [sem(f"raw_ready{b}") for b in range(RAW_BUFS)]
        const_ready = sem("const_ready")
        pool_step = sem("pool_step")
        head_ready = sem("head_ready")
        x_hi_ready = sem("x_hi_ready")
        ss_ready = sem("ss_ready")
        rstd_ready = sem("rstd_ready")
        hi_ready = sem("hi_ready")
        lo_ready = sem("lo_ready")
        split_used = sem("split_used")
        acc_ready = sem("acc_ready")
        acc_read = [sem(f"acc_read{b}") for b in range(2)]
        filled = [sem(f"filled{b}") for b in range(4)]
        emptied = [sem(f"emptied{b}") for b in range(4)]
        act_step = sem("act_step")
        dve_step = sem("dve_step")
        az_ready = sem("az_ready")
        g_act = sem("g_act")
        g_dve = sem("g_dve")
        g_rows = sem("g_rows")
        g_cols = sem("g_cols")
        g_hi = sem("g_hi")
        g_split = sem("g_split")
        k_dup = sem("k_dup")
        conv_y = sem("conv_y")
        conv_ready = sem("conv_ready")
        c_sq = sem("c_sq")
        c_sq_lo = sem("c_sq_lo")
        c_r = sem("c_r")
        c_nd = sem("c_nd")
        c_gam_ready = sem("c_gam_ready")
        c_u0 = sem("c_u0")
        c_y = sem("c_y")
        c_osq = sem("c_osq")
        cq_ss = sem("cq_ss")
        b_sq_ready = sem("b_sq_ready")
        cq_norm = sem("cq_norm")
        cq_hi_ready = sem("cq_hi_ready")
        bk_norm = sem("bk_norm")
        b_score = sem("b_score")
        bq_norm = sem("bq_norm")
        b_max = sem("b_max")
        b_exp = sem("b_exp")
        a_one = sem("a_one")
        a_exp = sem("a_exp")
        a_y = sem("a_y")
        a_ss = sem("a_ss")
        y_hi_ready = sem("y_hi_ready")
        x_again = [sem(f"x_again{n}") for n in range(D // 512)]
        last_half = sem("last_half")
        last_out = sem("last_out")
        out_done = sem("out_done")
        last_done = sem("last_done")

        block = ctx.enter_context(nc.Block())

        def raw_dmas(c):
            b, kts = chunks[c]
            k0, n = kts[0], len(kts)
            blk = blocks[b]
            dst = w_raw[:, c % RAW_BUFS, 0:n * blk["width"]].rearrange("p (k n) -> p k n", k=n)
            src = matrix[blk["matrix"]][:, k0:k0 + n, :]
            if blk["kind"] == "gates":
                g0 = blk["width"] - G_W
                return [(dst[:, :, g:g + w], src[:, :, col:col + w]) for g, col, w in
                        ((0, blk["col"], g0), (g0 + G_AI, C_AI, 2 * H_A), (g0 + G_CB, C_CB, 2 * H_C),
                         (g0 + G_KI, C_BKI, IDX_D + IDX_H))]
            return [(dst, src[:, :, blk["col"]:blk["col"] + blk["width"]])]

        def raw_count(c):
            return 16 * sum(4 if blocks[chunks[i][0]]["kind"] == "gates" else 1
                            for i in range(c % RAW_BUFS, c + 1, RAW_BUFS))

        def split_ap(tensor, c):
            b, kts = chunks[c]
            return tensor[:, c % SPLIT_BUFS, 0:len(kts) * blocks[b]["width"]]

        def bank(use):
            return mix[use % 4]

        def wait_filled(eng, use):
            eng.wait_ge(filled[use % 4], use // 4 + 1)

        def wait_emptied(eng, use):
            if use >= 4:
                eng.wait_ge(emptied[use % 4], use // 4)

        def halves(v, lv):
            return v.rearrange("p (j c r) -> p j c r", c=2, r=1 << lv)

        def halves4(v, lv):
            return v.rearrange("p (a j c r) -> p a j c r", a=4, c=2, r=1 << lv)

        use_of = {(name, arg): U0 + use for slot in woven for name, arg, use in slot}

        def wait_read(eng, name, arg, i=0):
            use = use_of[name, arg] + i
            eng.wait_ge(emptied[use % 4], use // 4 + 1)

        def wait_stored(eng, kind, arg=0):
            b = next(i for i, x_ in enumerate(blocks) if x_["kind"] == kind and x_["arg"] == arg)
            eng.wait_ge(acc_read[b % 2], b // 2 + 1)

        def conv_stage(j):
            return y[:, :, W_A + 512 * (j % 2):W_A + 512 * (j % 2) + 512]

        def c_square(i):
            return kv[:, 0, 512 * (i % 2):512 * (i % 2) + 512]

        def c_norm(i):
            if i == 7:
                return kv[:, 1, 0:512]
            return (c_kb, c_gam, c_at, c_bt, c_u, c_v, c_kd)[i][:].rearrange("p a b -> p (a b)")

        def out_acc(n):
            return acc0[:, :, 512 * n:512 * n + 512] if n < 2 else y[:, :, 512 * n:512 * n + 512]

        def y_gain(kt):
            if kt < W_A // P:
                return par[:, R_MN + kt:R_MN + kt + 1]
            return par[:, R_DN:R_DN + 1] if kt >= (W_A + W_B) // P else None

        @block.sync
        def _(sp):
            def x_piece(q):
                a, z = X_PARTS[q]
                sp.dma_start(xs[:, :, a:z], x_dram[:, :, a:z]).then_inc(x_ready[q], 16)

            def weights(c):
                if c >= RAW_BUFS:
                    sp.wait_ge(lo_ready, c - RAW_BUFS + 1)
                for dst, src in raw_dmas(c):
                    sp.dma_start(dst, src).then_inc(raw_ready[c % RAW_BUFS], 16)

            sp.dma_start(norm_in[0:32, :], norm_g[0].rearrange("(r p) -> r p", p=P)).then_inc(norm_in_ready, 16)
            x_piece(0)
            weights(0)
            x_piece(1)
            for c in range(1, NX - 2):
                weights(c)
                if c % 2 == 1:
                    x_piece((c + 3) // 2)
            for r, a in ((R_CQ, a_cq_g[0].rearrange("(r p) -> r p", p=P)), (R_QN, a_qn_g), (R_KN, a_kn_g),
                         (R_MN, m_norm_g[0].rearrange("(r p) -> r p", p=P)), (R_DN, d_norm_g)):
                sp.dma_start(par_in[r - R_CQ:r - R_CQ + a.shape[0], :], a).then_inc(par_in_ready, 16)
            for r, a in ((R_KIG, a_ki_g), (R_KIB, a_ki_b)):
                for i in range(2):
                    sp.dma_start(par_in[r - R_CQ:r - R_CQ + 1, i * IDX_D:(i + 1) * IDX_D], a).then_inc(par_in_ready, 16)
            sp.dma_start(tap_in[0:N_TAP, :], d_conv_w[0].rearrange("t (c p) -> (t c) p", p=P)).then_inc(
                par_in_ready, 16)
            for i, a in enumerate((m_ib, m_fb, d_a_log, d_dt_bias)):
                sp.dma_start(hcol[:, i:i + 1], a.rearrange("o h -> h o")).then_inc(par_in_ready, 16)
            for c in range(NX - 2, len(chunks)):
                weights(c)
            for m in range(M):
                sp.wait_ge(last_out, m + 1)
                n = D - 512
                sp.dma_start(out_dram[:, m, n:D], out_acc(n // 512)[:, m, :]).then_inc(last_done, 16)
            sp.wait_ge(last_done, 16 * M)

        PAR_DMAS = 16 * 14

        @block.gpsimd
        def _(pool):
            steps = [0]

            def step(ins):
                steps[0] += 1
                ins.then_inc(pool_step, 1)
                pool.wait_ge(pool_step, steps[0])

            def select(view, op, fill, base, pattern, cm):
                step(nc.gpsimd.affine_select(out=view, in_=view, compare_op=op, fill=fill, base=base,
                                             pattern=pattern, channel_multiplier=cm))

            step(nc.gpsimd.memset(ident[:], 0.0))
            select(ident[:], ALU.not_equal, 1.0, 0, [[-1, P]], 1)
            nc.gpsimd.engine_nop().then_inc(const_ready, 1)
            step(nc.gpsimd.memset(ones[:].bitcast(F32), 1.0))
            step(nc.gpsimd.memset(eps[:], EPS))
            step(nc.gpsimd.memset(sel[:].bitcast(F32), 0.0))
            select(sel[:], ALU.not_equal, 1.0, 0, [[-1, 8], [0, P]], 1)
            step(nc.gpsimd.memset(tri[:], 0.0))
            select(tri[:, 0, :], ALU.is_ge, NEG, 0, [[1, P]], -1)
            step(nc.gpsimd.memset(cap[:], BIG))
            select(cap[:], ALU.is_ge, -BIG, 0, [[-1, P]], 1)
            step(nc.gpsimd.memset(low[:], 0.0))
            select(low[:], ALU.is_ge, NEG, 0, [[-1, P]], 1)
            step(nc.gpsimd.memset(level[:], 0.0))
            select(level[:, 0, :].rearrange("p (j c) -> p j c", c=2)[:, :, 1], ALU.not_equal, 1.0, 0,
                   [[-2, P // 2]], 1)
            for lv in range(1, LEVELS):
                b = 1 << lv
                n = P // (2 * b)
                v = level[:, lv, :].rearrange("p (j c r) -> p j c r", c=2, r=b)[:, :, 0, :]
                step(nc.gpsimd.memset(v, 1.0))
                select(v, ALU.is_ge, 0.0, -b, [[-2 * b, n], [0, b]], 1)
                select(v, ALU.is_ge, 0.0, 2 * b - 1, [[2 * b, n], [0, b]], -1)
            nc.gpsimd.engine_nop().then_inc(const_ready, 1)
            wait_read(pool, "bo", (HKV - 1, 2))
            for n in range(D // 512):
                if 512 * n == W_A:
                    for i in range(12, 16):
                        wait_read(pool, "yt", i)
                pool.dma_start(out_acc(n), x_dram[:, :, 512 * n:512 * n + 512]).then_inc(x_again[n], 16)
            for n in range(D // 512 - 1):
                wait_stored(pool, "out2", n)
                pool.dma_start(out_dram[:, :, 512 * n:512 * n + 512], out_acc(n)).then_inc(out_done, 16)
            pool.wait_ge(out_done, 16 * (D // 512 - 1))

        @block.tensor
        def _(pe):
            def end_fill(ins, use):
                ins.then_inc(filled[use % 4], 1)

            def turn(dst, src, n=P):
                return nc.tensor.transpose(dst, src, ident[0:n, 0:n])

            def chunk(c):
                b, kts = chunks[c]
                blk = blocks[b]
                w = blk["width"]
                if kts[0] == blk["kts"][0] and b >= 2:
                    pe.wait_ge(acc_read[b % 2], b // 2)
                pe.wait_ge(lo_ready, c + 1)
                hi, lo = {"h": (op_hi, op_lo), "cq": (cq_hi, cq_lo), "y": (op_hi, op_lo)}[blk["operand"]]
                hv = split_ap(w_hi, c).rearrange("p (k n) -> p k n", k=len(kts))
                lv = split_ap(w_lo, c).rearrange("p (k n) -> p k n", k=len(kts))
                if c == len(chunks) - 1:
                    order = [(i, kt, [m]) for m in range(M) for i, kt in enumerate(kts)]
                else:
                    order = [(i, kt, range(M)) for i, kt in enumerate(kts)]
                for i, kt, ms in order:
                    if b == 0:
                        use = 1 + kt // 2
                        pe.wait_ge(emptied[use % 4], use // 4 + 1)
                    if blk["operand"] == "cq":
                        wait_read(pe, "bt", kt // 2)
                    if blk["kind"] in ("out1", "out2") and blk["arg"] == 0:
                        wait_read(pe, "yt", kt // 2)
                    for m in ms:
                        o = acc[b % 2][m][:, 0:w]
                        tok = slice(m * P, m * P + P)
                        nc.tensor.matmul(o, hi[:, kt, tok], hv[:, i, :], start=(kt == blk["kts"][0]), stop=False)
                        nc.tensor.matmul(o, hi[:, kt, tok], lv[:, i, :], start=False, stop=False)
                        last_mm = nc.tensor.matmul(o, lo[:, kt, tok], hv[:, i, :], start=False,
                                                   stop=(kt == blk["kts"][-1]))
                        if c == len(chunks) - 1 and m == 0 and kt == kts[-1]:
                            last_mm.then_inc(last_half, 1)
                if c == last[b]:
                    last_mm.then_inc(acc_ready, 1)
                    pe_done[0] += 1
                else:
                    last_mm.then_inc(split_used, 1)

            pe_done = [0]

            def gt(_, use):
                wait_stored(pe, "gates", 512)
                for i in range(4):
                    u = use + i // 2
                    if i % 2 == 0:
                        wait_emptied(pe, u)
                    for m in range(M):
                        ins = turn(bank(u)[0:8, (i % 2) * SEQ + m * P:(i % 2) * SEQ + m * P + P],
                                   small[:, m, 8 * i:8 * i + 8])
                    if i % 2:
                        end_fill(ins, u)

            def gb(_, use):
                pe.wait_ge(g_rows, 2)
                wait_emptied(pe, use)
                for i, (r, m) in enumerate(((2, 0), (2, 1), (3, 0), (3, 1), (5, 0), (0, 0), (0, 1), (4, 0), (4, 1))):
                    ins = turn(bank(use)[:, 8 * i:8 * i + 8], rows[:, r, m * P:m * P + P], 8)
                end_fill(ins, use)

            def kx(_, use):
                pe.wait_ge(k_dup, 1)
                wait_emptied(pe, use)
                for m in range(M):
                    ins = turn(bank(use)[:, m * P:m * P + P], kdup[:, m, :])
                end_fill(ins, use)

            def conv(i, use):
                wait_stored(pe, "conv", i // 2)
                wait_emptied(pe, use)
                for j in range(2):
                    for m in range(M):
                        ins = turn(bank(use)[:, j * SEQ + m * P:j * SEQ + m * P + P],
                                   conv_stage(i // 2)[:, m, (i % 2) * SEQ + j * P:(i % 2) * SEQ + j * P + P])
                end_fill(ins, use)

            def cn(i, use):
                pe.wait_ge(c_sq_lo, i + 1)
                wait_emptied(pe, use)
                nc.tensor.matmul(bank(use)[:], ones[:], csq_hi[:, i % 2, :], start=True, stop=False)
                end_fill(nc.tensor.matmul(bank(use)[:], ones[:], csq_lo[:, i % 2, :], start=False, stop=True), use)

            def spread(o, h, hi, lo):
                nc.tensor.matmul(o, sel[:, h, :], hi, start=True, stop=False)
                return nc.tensor.matmul(o, sel[:, h, :], lo, start=False, stop=True)

            def ca(u, use):
                hg, m = UNITS[u]
                pe.wait_ge(g_split, 1)
                for a in range(4):
                    i = a // 2
                    if a % 2 == 0:
                        wait_emptied(pe, use + i)
                    ins = spread(bank(use + i)[:, (a % 2) * SEQ:(a % 2) * SEQ + SEQ], 4 * hg + a,
                                 rows_r[:, 4:6, m * P:m * P + P], rows_r[:, 2:4, m * P:m * P + P])
                    if a % 2:
                        end_fill(ins, use + i)

            def cg(u, use):
                hg, m = UNITS[u]
                tok = slice(m * P, m * P + P)
                for i in range(2):
                    wait_read(pe, "ca", u, i)
                for i in range(2):
                    wait_emptied(pe, use + i)
                    for a in range(4):
                        h = 4 * hg + a
                        ins = nc.tensor.matmul(bank(use + i)[:, a * P:a * P + P], cT[:, 8 + h, tok],
                                               c_kb[:, a, :] if i == 0 else cT[:, h, tok], start=True, stop=True)
                    end_fill(ins, use + i)

            def ct(arg, use):
                u, lv = arg
                if lv == 1:
                    pe.wait_ge(c_u0, u + 1)
                else:
                    wait_read(pe, "cu", (u, lv - 1))
                wait_emptied(pe, use)
                for a in range(4):
                    ins = turn(bank(use)[:, a * P:a * P + P], c_u[:, a, :])
                end_fill(ins, use)

            def heads4(use, lhs, rhs, n=P):
                wait_emptied(pe, use)
                for a in range(4):
                    ins = nc.tensor.matmul(bank(use)[:, a * n:a * n + n], lhs(a), rhs(a), start=True, stop=True)
                end_fill(ins, use)

            def cm(arg, use):
                u, lv = arg
                wait_read(pe, "ct", arg)
                heads4(use, lambda a: c_at[:, a, :], lambda a: c_gam[:, a, 0:P // 2], P // 2)

            def cu(arg, use):
                u, lv = arg
                wait_read(pe, "cm", arg)
                heads4(use, lambda a: c_kb[:, a, :], lambda a: halves(c_u[:, a, :], lv)[:, :, 1, :], P // 2)

            def cv(u, use):
                hg, m = UNITS[u]
                wait_emptied(pe, use)
                for a in range(4):
                    ins = turn(bank(use)[:, a * P:a * P + P], cT[:, 16 + 4 * hg + a, m * P:m * P + P])
                end_fill(ins, use)

            def ck(u, use):
                hg, m = UNITS[u]
                wait_emptied(pe, use)
                for a in range(4):
                    ins = turn(bank(use)[:, a * P:a * P + P], cT[:, 8 + 4 * hg + a, m * P:m * P + P])
                end_fill(ins, use)

            def cs(u, use):
                hg, m = UNITS[u]
                wait_read(pe, "co", u - 1, 1)
                heads4(use, lambda a: cT[:, 8 + 4 * hg + a, m * P:m * P + P], lambda a: c_s[:, a, :])

            def cr(u, use):
                wait_read(pe, "cu", (u, LEVELS - 1))
                wait_read(pe, "cv" if UNITS[u][1] == 0 else "cs", u)
                heads4(use, lambda a: c_u[:, a, :], lambda a: c_v[:, a, :])

            def co(u, use):
                hg, m = UNITS[u]
                wait_read(pe, "cr", u)
                heads4(use, lambda a: c_bt[:, a, :], lambda a: c_v[:, a, :])
                if m == 0:
                    wait_read(pe, "ck", u)
                    heads4(use + 1, lambda a: c_kd[:, a, :], lambda a: c_v[:, a, :])
                else:
                    heads4(use + 1, lambda a: cT[:, 4 * hg + a, m * P:m * P + P], lambda a: c_s[:, a, :])

            def bt(i, use):
                pe.wait_ge(cq_norm, 2)
                wait_emptied(pe, use)
                for j in range(min(2, QKT - 2 * i)):
                    for m in range(M):
                        ins = turn(bank(use)[:, j * SEQ + m * P:j * SEQ + m * P + P],
                                   y[:, m, (2 * i + j) * P:(2 * i + j) * P + P])
                end_fill(ins, use)

            def turn8(use, src):
                for i in range(4):
                    u = use + i // 2
                    if i % 2 == 0:
                        wait_emptied(pe, u)
                    for m in range(M):
                        ins = turn(bank(u)[:, (i % 2) * SEQ + m * P:(i % 2) * SEQ + m * P + P],
                                   src[:, m, i * P:i * P + P])
                    if i % 2:
                        end_fill(ins, u)

            def bkt(_, use):
                pe.wait_ge(bk_norm, 2)
                turn8(use, kv[:, :, 0:512])

            def bit(j, use):
                wait_stored(pe, "bi", j)
                turn8(use, qs)

            def bsc(arg, use):
                j, p = arg
                wait_read(pe, "kx", 0)
                wait_read(pe, "bit", j, p // 2)
                for s in range(2):
                    half = slice(64 * s, 64 * s + 64)
                    wait_emptied(pe, use + s)
                    nc.tensor.matmul(bank(use + s)[:, 0:P], b_qT[half, p, 0:P], kiT[half, 0:P], start=True,
                                     stop=True)
                    end_fill(nc.tensor.matmul(bank(use + s)[:, P:3 * P], b_qT[half, p, P:SEQ], kiT[half, :],
                                              start=True, stop=True), use + s)

            def bqt(g, use):
                pe.wait_ge(bq_norm, 2 * (g + 1))
                turn8(use, qs)

            def bs(arg, use):
                g, v = arg
                for i in range(2):
                    wait_read(pe, "bkt", 0, i)
                    wait_read(pe, "bqt", g, i)
                wait_emptied(pe, use)
                for i in range(4 if v == 0 else 2):
                    if v == 0:
                        ins = nc.tensor.matmul(bank(use)[:, i * P:i * P + P], b_qT[:, i, 0:P], b_kT[:, g, 0:P],
                                               start=True, stop=True)
                    else:
                        ins = nc.tensor.matmul(bank(use)[:, i * SEQ:i * SEQ + SEQ], b_qT[:, 2 * v - 2 + i, P:SEQ],
                                               b_kT[:, g, :], start=True, stop=True)
                end_fill(ins, use)

            def bp(arg, use):
                g, v = arg
                pe.wait_ge(b_exp, 3 * g + v + 1)
                wait_emptied(pe, use)
                for i in range(4):
                    ins = turn(bank(use)[:, i * P:i * P + P], b_p[:, i * P:i * P + P])
                end_fill(ins, use)

            def bo(arg, use):
                g, v = arg
                wait_read(pe, "bp", arg)
                wait_emptied(pe, use)
                for i in range(4):
                    val = kv[:, 0 if v == 0 else i % 2, 512 + g * P:512 + g * P + P]
                    o = i if v == 0 else i // 2
                    ins = nc.tensor.matmul(bank(use)[:, o * P:o * P + P], b_pT[:, i, :], val,
                                           start=(v == 0 or i % 2 == 0), stop=(v == 0 or i % 2 == 1))
                end_fill(ins, use)

            def at(j, use):
                wait_stored(pe, "aqk", j)
                turn8(use, a_s)

            def ae(h, use):
                half = slice(64 * (h % 2), 64 * (h % 2) + 64)
                for i in range(2):
                    wait_read(pe, "at", 0, i)
                    wait_read(pe, "at", 1, i)
                for i in range(2):
                    wait_emptied(pe, use + i)
                    b = bank(use + i)
                    if i == 0:
                        ins = spread(b[:, 0:SEQ], h, rows_r[:, 0, :], rows_r[:, 1, :])
                    else:
                        nc.tensor.matmul(b[:, 0:SEQ], a_kT[half, h // 2, 0:P], a_qT[half, h // 2, :], start=True,
                                         stop=True)
                        ins = nc.tensor.matmul(b[:, SEQ:3 * P], a_kT[half, h // 2, P:SEQ],
                                               a_qT[half, h // 2, P:SEQ], start=True, stop=True)
                    end_fill(ins, use + i)

            def ap(h, use):
                wait_read(pe, "ae", h, 1)
                pe.wait_ge(a_one, 1)
                wait_stored(pe, "av", 1)
                wait_emptied(pe, use)
                w = HEAD + 1
                b = bank(use)
                nc.tensor.matmul(b[:, 0:w], a_p[:, 0:P], a_v[:, 0, h, :], start=True, stop=True)
                nc.tensor.matmul(b[:, 256:256 + w], a_p[:, P:2 * P], a_v[:, 0, h, :], start=True, stop=False)
                end_fill(nc.tensor.matmul(b[:, 256:256 + w], a_p[:, 2 * P:3 * P], a_v[:, 1, h, :], start=False,
                                          stop=True), use)

            def yt(i, use):
                if i < 4:
                    pe.wait_ge(a_y, H_A)
                elif i < 12:
                    wait_read(pe, "bo", (HKV - 1, 2))
                else:
                    pe.wait_ge(c_y, len(UNITS))
                wait_emptied(pe, use)
                for j in range(2):
                    for m in range(M):
                        ins = turn(bank(use)[:, j * SEQ + m * P:j * SEQ + m * P + P],
                                   y[:, m, (2 * i + j) * P:(2 * i + j) * P + P])
                end_fill(ins, use)

            def par_columns(_, use):
                pe.wait_ge(par_in_ready, PAR_DMAS)
                wait_emptied(pe, use)
                end_fill(turn(bank(use)[:, 0:R_N - R_CQ], par_in[0:R_N - R_CQ, :], R_N - R_CQ), use)
                wait_emptied(pe, use + 1)
                end_fill(turn(bank(use + 1)[:, 0:N_TAP], tap_in[0:N_TAP, :], N_TAP), use + 1)

            pieces = dict(par=par_columns, gt=gt, gb=gb, kx=kx, conv=conv, cn=cn, ca=ca, cg=cg, ct=ct, cm=cm,
                          cu=cu, cv=cv, ck=ck, cs=cs, cr=cr, co=co, bt=bt, bkt=bkt, bit=bit, bsc=bsc,
                          bqt=bqt, bs=bs, bp=bp, bo=bo,
                          at=at, ae=ae, ap=ap, yt=yt)

            def x_columns(i):
                use = 1 + i
                pe.wait_ge(x_ready[i if i < 2 else i // 2 + 1], 16)
                wait_emptied(pe, use)
                for j in range(2):
                    for m in range(M):
                        ins = turn(bank(use)[:, j * SEQ + m * P:j * SEQ + m * P + P],
                                   xs[:, m, (2 * i + j) * P:(2 * i + j) * P + P])
                end_fill(ins, use)

            pe.wait_ge(const_ready, 1)
            pe.wait_ge(norm_in_ready, 16)
            end_fill(turn(bank(0)[:, 0:R_CQ], norm_in[0:R_CQ, :], R_CQ), 0)
            for i in range(X_AHEAD):
                x_columns(i)
            for c in range(len(chunks)):
                chunk(c)
                if c + X_AHEAD < NX:
                    x_columns(c + X_AHEAD)
                if c == NX:
                    pe.wait_ge(const_ready, 2)
                for name, arg, use in woven[c]:
                    if name in pieces:
                        pieces[name](arg, U0 + use)

        @block.scalar
        def _(act):
            steps = [0]
            func = nc.scalar.activation

            def step(ins):
                steps[0] += 1
                ins.then_inc(act_step, 1)
                act.wait_ge(act_step, steps[0])

            def done_bank(ins, use):
                ins.then_inc(emptied[use % 4], 1)

            def split_hi(c):
                act.wait_ge(raw_ready[c % RAW_BUFS], raw_count(c))
                if c >= SPLIT_BUFS:
                    d = c - SPLIT_BUFS
                    b = chunks[d][0]
                    if d == last[b]:
                        act.wait_ge(acc_ready, b + 1)
                    else:
                        act.wait_ge(split_used, d + 1 - b)
                n = len(chunks[c][1]) * blocks[chunks[c][0]]["width"]
                func(split_ap(w_hi, c), w_raw[:, c % RAW_BUFS, 0:n], ACT.Copy).then_inc(hi_ready, 1)

            def evac(b, _):
                blk = blocks[b]
                kind, arg, w = blk["kind"], blk["arg"], blk["width"]
                if kind in ("out1", "out2"):
                    return
                act.wait_ge(rstd_ready, 1)
                act.wait_ge(acc_ready, b + 1)
                if kind in ("silu", "ao", "az"):
                    for m in range(M):
                        dst = acc[b % 2][m][:] if kind == "az" else y[:, m, arg:arg + 512]
                        ins = func(dst, acc[b % 2][m][:], ACT.Sigmoid if kind == "ao" else ACT.Silu,
                                   scale=rstd[:, m:m + 1])
                        if m == 0:
                            step(ins)
                    ins.then_inc(az_ready if kind == "az" else acc_read[b % 2], 1)
                    return
                for m in range(M):
                    src = acc[b % 2][m][:, 0:w]
                    if kind == "gates":
                        func(small[:, m, :], src[:, w - G_W:w], ACT.Copy, scale=rstd[:, m:m + 1])
                        dst, src = y[:, m, arg:arg + w - G_W], src[:, 0:w - G_W]
                    elif kind == "conv":
                        dst = conv_stage(arg)[:, m, :]
                    elif kind == "cq":
                        dst = y[:, m, 0:w]
                    elif kind == "bkv":
                        dst = kv[:, m, arg:arg + w]
                    elif kind in ("bi", "bq"):
                        dst = qs[:, m, :]
                    elif kind == "aqk":
                        dst = a_s[:, m, :]
                    else:
                        dst = a_v[:, m, 4 * arg:4 * arg + 4, 0:HEAD]
                        src = src.rearrange("p (h d) -> p h d", h=4)
                    if kind in ("bi", "bq"):
                        ins = func(dst, src, ACT.Copy)
                    else:
                        ins = func(dst, src, ACT.Copy, scale=rstd[:, m:m + 1])
                    if m == 0:
                        step(ins)
                ins.then_inc(acc_read[b % 2], 1)

            def gt(_, use):
                wait_filled(act, use)
                act.wait_ge(head_ready, 1)
                b = bank(use)
                func(rows[:, 0, :], b[0:8, 0:SEQ], ACT.Tanh, bias=hcol[:, 4:5], scale=1 / GATE_CAP).then_inc(g_act, 1)
                done_bank(func(rows[:, 1, :], b[0:8, SEQ:2 * SEQ], ACT.Tanh, bias=hcol[:, 5:6],
                               scale=1 / GATE_CAP), use)
                act.wait_ge(emptied[use % 4], use // 4 + 1)
                func(rows[:, 1, :], rows[:, 1, :], ACT.Exp, scale=-GATE_CAP)
                wait_filled(act, use + 1)
                b = bank(use + 1)
                func(rows[:, 3, :], b[0:8, 0:SEQ], ACT.Exp, scale=-1.0).then_inc(g_act, 1)
                ins = func(rows[:, 2, :], b[0:8, SEQ:2 * SEQ], ACT.Identity, bias=hcol[:, 3:4])
                done_bank(ins, use + 1)
                act.wait_ge(emptied[(use + 1) % 4], (use + 1) // 4 + 1)
                func(rows[:, 1, :], rows[:, 1, :], ACT.Ln, bias=1.0).then_inc(g_act, 1)

            def g2(_, use):
                act.wait_ge(g_dve, 1)
                step(func(rows[:, 4, :], rows[:, 4, :], ACT.Exp, scale=-1.0))
                func(rows[:, 4, :], rows[:, 4, :], ACT.Ln, bias=1.0).then_inc(g_act, 1)

            def g4(_, use):
                act.wait_ge(g_dve, 2)
                func(rows[:, 5, 0:P], rows[:, 2, 0:P], ACT.Exp, bias=rows[:, 2, P - 1:P], scale=-1.0).then_inc(
                    g_rows, 1)
                act.wait_ge(g_dve, 3)
                func(rows[:, 4, :], rows[:, 4, :], ACT.Exp).then_inc(g_rows, 1)

            def gb(_, use):
                act.wait_ge(g_cols, 1)
                func(gder[:, 2:4, :], gcol[:, 0:2, :], ACT.Exp).then_inc(g_cols, 1)

            def gs(_, use):
                wait_filled(act, use_of["gb", 0])
                func(rows_r[:, 0, :], rows[:, 1, :], ACT.Copy)
                func(rows_r[:, 4:6, :], rows[:, 2:4, :], ACT.Copy).then_inc(g_hi, 1)

            def conv(i, use):
                wait_read(act, "par", 0, 1)
                wait_filled(act, use)
                for j in range(2):
                    c = 2 * i + j
                    ins = func(cT[:, c, :], bank(use)[:, j * SEQ:j * SEQ + SEQ], ACT.Copy,
                               scale=par[:, R_N + 3 * CH + c:R_N + 3 * CH + c + 1])
                ins.then_inc(conv_y, 1)
                wait_read(act, "conv", i)
                t = cT[:, 2 * i:2 * i + 2, :].rearrange("p c t -> p (c t)")
                func(t, t, ACT.Silu).then_inc(conv_ready, 1)

            def csq(i, use):
                act.wait_ge(conv_ready, 12)
                if i >= 2:
                    act.wait_ge(c_sq_lo, i - 1)
                step(func(c_square(i), cT[:, 2 * i:2 * i + 2, :].rearrange("p c t -> p (c t)"), ACT.Square))
                if i >= 2:
                    wait_filled(act, use_of["cn", i - 2])
                func(csq_hi[:, i % 2, :], c_square(i), ACT.Copy).then_inc(c_sq, 1)

            def cn(i, use):
                wait_filled(act, use)
                done_bank(func(c_norm(i), bank(use)[:], ACT.Ln, bias=eps[:]), use)

            def ce(i, use):
                wait_read(act, "cn", i)
                func(c_norm(i), c_norm(i), ACT.Exp, scale=-0.5).then_inc(c_r, 1)

            def ca(u, use):
                hg, m = UNITS[u]
                wait_read(act, "ca", u, 1)
                act.wait_ge(g_cols, 3)
                for a in range(4):
                    ins = func(c_gam[:, a, :], c_gam[:, a, :], ACT.Exp, bias=gder[:, m, 4 * hg + a:4 * hg + a + 1])
                ins.then_inc(c_gam_ready, 1)

            def ct(arg, use):
                wait_filled(act, use)
                lv = arg[1]
                done_bank(func(c_gam[:, :, 0:P // 2].rearrange("p a (j r) -> p a j r", r=1 << lv),
                               halves4(bank(use)[:], lv)[:, :, :, 0, :], ACT.Copy), use)

            def cv(u, use):
                hg, m = UNITS[u]
                wait_filled(act, use)
                for a in range(4):
                    ins = func(c_v[:, a, :], bank(use)[:, a * P:a * P + P], ACT.Copy,
                               scale=gcol[:, 2 + m, 4 * hg + a:4 * hg + a + 1])
                done_bank(ins, use)

            def ck(u, use):
                hg, m = UNITS[u]
                wait_filled(act, use)
                for a in range(4):
                    ins = func(c_kd[:, a, :], bank(use)[:, a * P:a * P + P], ACT.Copy,
                               scale=gcol[:, 4, 4 * hg + a:4 * hg + a + 1])
                done_bank(ins, use)

            def cr(u, use):
                wait_filled(act, use)
                done_bank(func(c_v[:].rearrange("p a b -> p (a b)"), bank(use)[:], ACT.Copy), use)

            def co(u, use):
                hg, m = UNITS[u]
                wait_filled(act, use + 1)
                if m == 0:
                    done_bank(func(c_s[:].rearrange("p a b -> p (a b)"), bank(use + 1)[:], ACT.Copy), use + 1)
                    act.wait_ge(emptied[(use + 1) % 4], (use + 1) // 4 + 1)
                else:
                    for a in range(4):
                        ins = func(c_kb[:, a, :], bank(use + 1)[:, a * P:a * P + P], ACT.Copy,
                                   scale=gder[:, 2 + m, 4 * hg + a:4 * hg + a + 1])
                    done_bank(ins, use + 1)
                wait_read(act, "co", u)
                func(c_gam[:].rearrange("p a b -> p (a b)"), c_at[:].rearrange("p a b -> p (a b)"),
                     ACT.Square).then_inc(c_osq, 1)

            def bn(_, use):
                wait_stored(act, "cq")
                wait_stored(act, "gates", 512)
                for m in range(M):
                    ins = func(b_sq[:, 0:Q_LORA], y[:, m, 0:Q_LORA], ACT.Square, accum_out=st[:, 4 + m:5 + m])
                    if m == 0:
                        step(ins)
                ins.then_inc(cq_ss, 1)

            def bt(i, use):
                wait_filled(act, use)
                for j in range(min(2, QKT - 2 * i)):
                    kt = 2 * i + j
                    ins = func(cq_hi[:, kt, :], bank(use)[:, j * SEQ:j * SEQ + SEQ], ACT.Copy,
                               scale=par[:, R_CQ + kt:R_CQ + kt + 1])
                ins.then_inc(cq_hi_ready, 1)

            def head_norms(n):
                for m in range(M):
                    src = kv[:, m, 0:512] if n == 0 else qs[:, m, :]
                    func(b_sq[:, m * 512:m * 512 + 512], src, ACT.Square).then_inc(b_sq_ready, 1)

            def bkn(_, use):
                wait_stored(act, "bkv", 0)
                act.wait_ge(cq_ss, 1)
                head_norms(0)

            def bqn(g, use):
                wait_stored(act, "bq", g)
                head_norms(g + 1)

            def bkt(_, use):
                for i in range(2):
                    wait_filled(act, use + i)
                    done_bank(func(b_kT[:, 2 * i:2 * i + 2, :].rearrange("p a b -> p (a b)"), bank(use + i)[:],
                                   ACT.Copy, scale=par[:, R_KN:R_KN + 1]), use + i)

            def bit(j, use):
                for i in range(2):
                    wait_filled(act, use + i)
                    done_bank(func(b_qT[:, 2 * i:2 * i + 2, :].rearrange("p a b -> p (a b)"), bank(use + i)[:],
                                   ACT.Copy), use + i)

            def bsc(arg, use):
                j, p = arg
                for s in range(2):
                    h = 8 * j + 2 * p + s
                    wait_filled(act, use + s)
                    if h >= 2:
                        act.wait_ge(b_score, h - 1)
                    rl = (b_s, b_p)[s][:, 0:3 * P]
                    done_bank(func(rl, bank(use + s)[:, 0:3 * P], ACT.Relu), use + s)

            def bqt(g, use):
                for i in range(2):
                    wait_filled(act, use + i)
                    done_bank(func(b_qT[:, 2 * i:2 * i + 2, :].rearrange("p a b -> p (a b)"), bank(use + i)[:],
                                   ACT.Copy, scale=par[:, R_QN:R_QN + 1]), use + i)

            def bs(arg, use):
                g, v = arg
                n, w = (4, P) if v == 0 else (2, SEQ)
                act.wait_ge(b_max, 3 * g + v + 1)
                for i in range(n):
                    ins = func(b_p[:, i * w:i * w + w], b_s[:, i * w:i * w + w], ACT.Exp,
                               bias=st[:, 24 + i:25 + i], scale=HEAD ** -0.5, accum_out=st[:, 28 + i:29 + i])
                ins.then_inc(b_exp, 1)

            def bp(arg, use):
                wait_filled(act, use)
                done_bank(func(b_pT[:].rearrange("p a b -> p (a b)"), bank(use)[:], ACT.Copy), use)

            def at(j, use):
                dst = (a_qT, a_kT)[j]
                for i in range(2):
                    wait_filled(act, use + i)
                    done_bank(func(dst[:, 2 * i:2 * i + 2, :].rearrange("p a b -> p (a b)"), bank(use + i)[:],
                                   ACT.Copy, scale=(DQK ** -0.5, 1.0)[j]), use + i)

            def ae(h, use):
                wait_read(act, "ae", h)
                func(a_m[:, 0:SEQ], a_m[:, 0:SEQ], ACT.Exp, bias=gcol[:, 5, h:h + 1])
                func(a_m[:, SEQ:3 * P], a_m[:, SEQ:3 * P], ACT.Exp, bias=gcol[:, 6, h:h + 1]).then_inc(a_exp, 1)

            def ap(h, use):
                wait_read(act, "ap", h)
                for m in range(M):
                    ins = func(a_sq[:], a_h[:, m, :], ACT.Square, accum_out=st[:, 36 + m:37 + m])
                    if m == 0:
                        step(ins)
                ins.then_inc(a_ss, 1)

            def yt(i, use):
                wait_filled(act, use)
                for j in range(2):
                    kt = 2 * i + j
                    gain = y_gain(kt)
                    ins = func(op_hi[:, kt, :], bank(use)[:, j * SEQ:j * SEQ + SEQ], ACT.Copy,
                               scale=1.0 if gain is None else gain)
                ins.then_inc(y_hi_ready, 1)

            pieces = dict(evac=evac, gt=gt, g2=g2, g4=g4, gb=gb, gs=gs, conv=conv, csq=csq, cn=cn, ce=ce, ca=ca,
                          ct=ct, cv=cv, ck=ck, cr=cr, co=co, bn=bn, bt=bt, bkn=bkn, bqn=bqn, bkt=bkt, bit=bit,
                          bsc=bsc, bqt=bqt,
                          bs=bs, bp=bp, at=at, ae=ae, ap=ap, yt=yt)

            def x_hi(i):
                use = 1 + i
                wait_filled(act, use)
                for j in range(2):
                    kt = 2 * i + j
                    ins = func(op_hi[:, kt, :], bank(use)[:, j * SEQ:j * SEQ + SEQ], ACT.Copy,
                               scale=par[:, R_NORM + kt:R_NORM + kt + 1])
                ins.then_inc(x_hi_ready, 1)

            def x_square(i):
                q, m = i // M, i % M
                for part in ((0, 1) if q == 0 else (q + 1,)):
                    act.wait_ge(x_ready[part], 16)
                func(y[:, m, 512 * q:512 * q + 512], xs[:, m, 512 * q:512 * q + 512], ACT.Square,
                     accum_out=ssq[:, m, q:q + 1]).then_inc(ss_ready, 1)

            act.wait_ge(const_ready, 1)
            func(newton_act[:], ident[:, 0:1], ACT.Copy)
            act.wait_ge(emptied[0], 1)
            for c in range(AHEAD):
                if c < X_AHEAD:
                    x_hi(c)
                split_hi(c)
            for c in range(len(chunks)):
                if c + AHEAD < len(chunks):
                    split_hi(c + AHEAD)
                if c + X_AHEAD < NX:
                    x_hi(c + X_AHEAD)
                if c < NX - 1:
                    x_square(c)
                    if c == NX - 2:
                        x_square(c + 1)
                        act.wait_ge(par_in_ready, PAR_DMAS)
                        func(hcol[:, 4:6], hcol[:, 0:2], ACT.Copy, scale=1 / GATE_CAP)
                        func(hcol[:, 6:7], hcol[:, 2:3], ACT.Exp).then_inc(head_ready, 1)
                        act.wait_ge(const_ready, 2)
                for name, arg, use in woven[c]:
                    if name in pieces:
                        pieces[name](arg, U0 + use)

        @block.vector
        def _(dve):
            steps = [0]
            vec = nc.vector
            ones_f = ones[:].bitcast(F32)

            def step(ins, but=0):
                steps[0] += 1
                ins.then_inc(dve_step, 1)
                dve.wait_ge(dve_step, steps[0] - but)

            def done_bank(ins, use):
                ins.then_inc(emptied[use % 4], 1)

            def split_lo(c):
                dve.wait_ge(hi_ready, c + 1)
                n = len(chunks[c][1]) * blocks[chunks[c][0]]["width"]
                vec.tensor_tensor(split_ap(w_lo, c), w_raw[:, c % RAW_BUFS, 0:n], split_ap(w_hi, c).bitcast(F32),
                                  ALU.subtract).then_inc(lo_ready, 1)

            def evac(b, _):
                blk = blocks[b]
                kind, arg = blk["kind"], blk["arg"]
                if kind == "out1":
                    dve.wait_ge(acc_ready, b + 1)
                    dve.wait_ge(x_again[arg], 16)
                    for m in range(M):
                        ins = vec.tensor_tensor(out_acc(arg)[:, m, :], acc[b % 2][m][:], out_acc(arg)[:, m, :],
                                                ALU.add)
                        if m == 0:
                            step(ins)
                    ins.then_inc(acc_read[b % 2], 1)
                elif kind == "out2" and b == len(blocks) - 1:
                    for m in range(M):
                        dve.wait_ge(*((last_half, 1) if m == 0 else (acc_ready, b + 1)))
                        vec.tensor_tensor(out_acc(arg)[:, m, :], acc[b % 2][m][:], out_acc(arg)[:, m, :],
                                          ALU.add).then_inc(last_out, 1)
                elif kind == "out2":
                    dve.wait_ge(acc_ready, b + 1)
                    for m in range(M):
                        ins = vec.tensor_tensor(out_acc(arg)[:, m, :], acc[b % 2][m][:], out_acc(arg)[:, m, :],
                                                ALU.add)
                        if m == 0:
                            step(ins)
                    ins.then_inc(acc_read[b % 2], 1)
                elif kind == "az":
                    dve.wait_ge(az_ready, arg // 512 + 1)
                    wait_stored(dve, "ao", arg)
                    for m in range(M):
                        dst = y[:, m, arg:arg + 512]
                        ins = vec.tensor_tensor(dst, acc[b % 2][m][:], dst, ALU.mult)
                        if m == 0:
                            step(ins)
                    ins.then_inc(acc_read[b % 2], 1)

            def rsqrt_mean(v, n, signal=None):
                w = v.shape[1]
                r, t = newton[:, 0:w], newton2[:, 0:w]
                step(vec.tensor_scalar(v, v, 1.0 / n, EPS, ALU.mult, ALU.add))
                step(vec.tensor_scalar(r.bitcast(mybir.dt.int32), v.bitcast(mybir.dt.int32), -0.5, RSQRT, ALU.mult,
                                       ALU.add))
                for i in range(NEWTON):
                    step(vec.tensor_tensor(t, r, r, ALU.mult))
                    step(vec.scalar_tensor_tensor(t, t, -0.5, v, ALU.mult, ALU.mult))
                    ins = vec.scalar_tensor_tensor(v if i == NEWTON - 1 else r, t, 1.5, r, ALU.add, ALU.mult)
                    if i == NEWTON - 1 and signal is not None:
                        ins.then_inc(signal, 1)
                    else:
                        step(ins)

            def g1(_, use):
                dve.wait_ge(g_act, 3)
                step(vec.tensor_scalar(rows[:, 3, :], rows[:, 3, :], 1.0, None, ALU.add))
                step(vec.reciprocal(rows[:, 3, :], rows[:, 3, :]))
                wait_read(dve, "gt", 0, 1)
                vec.scalar_tensor_tensor(rows[:, 4, :], rows[:, 2, :], -1.0, rows[:, 2, :], ALU.mult,
                                         ALU.max).then_inc(g_dve, 1)

            def g3(_, use):
                dve.wait_ge(g_act, 4)
                step(vec.scalar_tensor_tensor(rows[:, 2, :], rows[:, 2, :], 0.0, rows[:, 4, :], ALU.max, ALU.add))
                step(vec.tensor_scalar(rows[:, 4, :], rows[:, 2, :], hcol[:, 6:7], -1.0, ALU.mult, ALU.mult))
                for m in range(M):
                    tok = slice(m * P, m * P + P)
                    ins = vec.tensor_tensor_scan(rows[:, 2, tok], ones_f[0:8, :], rows[:, 4, tok], 0.0, ALU.mult,
                                                 ALU.add)
                    if m == 0:
                        step(ins)
                ins.then_inc(g_dve, 1)
                dve.wait_ge(g_dve, 2)
                step(vec.tensor_tensor_scan(rows[:, 4, :], ones_f[0:8, 0:1].to_broadcast([8, SEQ]), rows[:, 1, :], 0.0,
                                            ALU.mult, ALU.add))
                step(vec.scalar_tensor_tensor(rows[:, 0, :], rows[:, 0, :], GATE_CAP, rows[:, 4, :], ALU.mult,
                                              ALU.add))
                step(vec.tensor_tensor_scan(rows[:, 1, :], rows[:, 0, :], rows[:, 0, :], 0.0, ALU.max, ALU.max))
                step(vec.tensor_scalar(rows[:, 1, :], rows[:, 1, :], -1.0, None, ALU.mult))
                vec.tensor_tensor(rows[:, 4, :], rows[:, 4, :], rows[:, 1, :], ALU.add).then_inc(g_dve, 1)

            def gb(_, use):
                wait_filled(dve, use)
                done_bank(vec.tensor_copy(gcol[:].rearrange("p a b -> p (a b)"), bank(use)[:, 0:72]), use)
                dve.wait_ge(emptied[use % 4], use // 4 + 1)
                vec.tensor_scalar(gder[:, 0:2, :], gcol[:, 0:2, :], -1.0, None, ALU.mult).then_inc(g_cols, 1)
                dve.wait_ge(g_cols, 2)
                vec.scalar_tensor_tensor(gder[:, 4:6, :], gcol[:, 2:4, :], -1.0, gder[:, 2:4, :], ALU.mult,
                                         ALU.mult).then_inc(g_cols, 1)

            def gs(_, use):
                dve.wait_ge(g_hi, 1)
                vec.tensor_tensor(rows_r[:, 1, :], rows[:, 1, :], rows_r[:, 0, :].bitcast(F32), ALU.subtract)
                vec.tensor_tensor(rows_r[:, 2:4, :], rows[:, 2:4, :], rows_r[:, 4:6, :].bitcast(F32),
                                  ALU.subtract).then_inc(g_split, 1)

            def kn(_, use):
                wait_stored(dve, "gates", 512)
                for m in range(M):
                    step(vec.tensor_scalar(small[:, m, G_WI:G_WI + IDX_H], small[:, m, G_WI:G_WI + IDX_H],
                                           IDX_H ** -0.5 * IDX_D ** -0.5, None, ALU.mult))
                    step(vec.bn_stats(st[:, 32:38], small[:, m, G_KI:G_KI + IDX_D]))
                    step(vec.bn_aggr(st[:, 38:40], st[:, 32:38]))
                    step(vec.tensor_copy(st[:, 18 + m:19 + m], st[:, 38:39]))
                    step(vec.tensor_copy(st[:, 20 + m:21 + m], st[:, 39:40]))

            def kr(_, use):
                rsqrt_mean(st[:, 20:22], 1)

            def kd(_, use):
                for m in range(M):
                    for i in range(2):
                        ins = vec.tensor_scalar(kdup[:, m, i * IDX_D:(i + 1) * IDX_D], small[:, m, G_KI:G_KI + IDX_D],
                                                st[:, 18 + m:19 + m], st[:, 20 + m:21 + m], ALU.subtract, ALU.mult)
                ins.then_inc(k_dup, 1)

            def kx(_, use):
                wait_filled(dve, use)
                done_bank(vec.tensor_scalar(kiT[:], bank(use)[:, 0:SEQ], par[:, R_KIG:R_KIG + 1],
                                            par[:, R_KIB:R_KIB + 1], ALU.mult, ALU.add), use)
                dve.wait_ge(emptied[use % 4], use // 4 + 1)

            def conv(i, use):
                dve.wait_ge(conv_y, i + 1)
                for d in range(1, CONV_K):
                    for j in range(2):
                        c = 2 * i + j
                        row = R_N + (CONV_K - 1 - d) * CH + c
                        ins = vec.scalar_tensor_tensor(cT[:, c, d:SEQ], bank(use)[:, j * SEQ:j * SEQ + SEQ - d],
                                                       par[:, row:row + 1], cT[:, c, d:SEQ], ALU.mult, ALU.add)
                        if (d, j) != (CONV_K - 1, 1):
                            step(ins, but=1)
                done_bank(ins, use)

            def csq(i, use):
                dve.wait_ge(c_sq, i + 1)
                vec.tensor_tensor(csq_lo[:, i % 2, :], c_square(i), csq_hi[:, i % 2, :].bitcast(F32),
                                  ALU.subtract).then_inc(c_sq_lo, 1)

            def ce(i, use):
                dve.wait_ge(c_r, i + 1)
                g = c_norm(i)
                t = cT[:, 2 * i:2 * i + 2, :].rearrange("p c t -> p (c t)")
                if i < 4:
                    ins = vec.scalar_tensor_tensor(t, t, HEAD ** -0.5, g, ALU.mult, ALU.mult)
                else:
                    ins = vec.tensor_tensor(t, t, g, ALU.mult)
                ins.then_inc(c_nd, 1)

            def ca(u, use):
                hg, m = UNITS[u]
                dve.wait_ge(c_nd, 8)
                for i in range(2):
                    wait_filled(dve, use + i)
                    pair = slice(2 * i, 2 * i + 2)
                    b = bank(use + i)[:].rearrange("p (a r s) -> p a r s", a=2, r=2)
                    k = 8 + 4 * hg + 2 * i
                    vec.tensor_tensor(c_kb[:, pair, :], b[:, :, 1, :], cT[:, k:k + 2, m * P:m * P + P], ALU.mult)
                    done_bank(vec.tensor_tensor(c_gam[:, pair, :], b[:, :, 0, :],
                                                tri[:, 0:1, :].to_broadcast([P, 2, P]), ALU.add), use + i)

            def cg(u, use):
                dve.wait_ge(c_gam_ready, u + 1)
                for i, dst in enumerate((c_at, c_bt)):
                    wait_filled(dve, use + i)
                    done_bank(vec.tensor_tensor(dst[:], bank(use + i)[:].rearrange("p (a b) -> p a b", a=4), c_gam[:],
                                                ALU.mult), use + i)
                    dve.wait_ge(emptied[(use + i) % 4], (use + i) // 4 + 1)
                step(vec.tensor_tensor(c_u[:], c_at[:], level[:, 0:1, :].to_broadcast([P, 4, P]), ALU.mult))
                vec.tensor_tensor(c_u[:], ident[:].unsqueeze(1).to_broadcast([P, 4, P]), c_u[:],
                                  ALU.subtract).then_inc(c_u0, 1)

            def cm(arg, use):
                u, lv = arg
                wait_filled(dve, use)
                n, b = P >> (lv + 1), 1 << lv
                new = bank(use)[:, 0:2 * P].rearrange("p (a j r) -> p a j r", a=4, r=b)
                mask = halves(level[:, lv, :], lv).unsqueeze(1)
                done_bank(vec.tensor_tensor(c_kb[:].rearrange("p a (j c r) -> p a j c r", c=2, r=b),
                                            new.unsqueeze(3).to_broadcast([P, 4, n, 2, b]),
                                            mask.to_broadcast([P, 4, n, 2, b]), ALU.mult), use)

            def cu(arg, use):
                u, lv = arg
                wait_filled(dve, use)
                b = 1 << lv
                right = c_u[:].rearrange("p a (j c r) -> p a j c r", c=2, r=b)[:, :, :, 1, :]
                done_bank(vec.tensor_tensor(right, right, bank(use)[:, 0:2 * P].rearrange(
                    "p (a j r) -> p a j r", a=4, r=b), ALU.subtract), use)

            def cs(u, use):
                hg, m = UNITS[u]
                wait_filled(dve, use)
                wait_read(dve, "cv", u)
                for a in range(4):
                    ins = vec.scalar_tensor_tensor(c_v[:, a, :], bank(use)[:, a * P:a * P + P],
                                                   gder[:, 4 + m, 4 * hg + a:4 * hg + a + 1], c_v[:, a, :],
                                                   ALU.mult, ALU.add)
                done_bank(ins, use)

            def co(u, use):
                hg, m = UNITS[u]
                wait_filled(dve, use)
                o = c_at[:].rearrange("p a b -> p (a b)")
                wait_read(dve, "co", u, 1)
                if m == 0:
                    done_bank(vec.tensor_copy(o, bank(use)[:]), use)
                else:
                    done_bank(vec.tensor_tensor(o, bank(use)[:], c_kb[:].rearrange("p a b -> p (a b)"), ALU.add), use)
                dve.wait_ge(c_osq, u + 1)
                step(vec.tensor_reduce(st[:, 0:4], c_gam[:], AX_X, ALU.add))

            def cy(u, use):
                hg, m = UNITS[u]
                rsqrt_mean(st[:, 0:4], HEAD)
                for a in range(4):
                    h = 4 * hg + a
                    dst = y[:, m, W_A + W_B + h * P:W_A + W_B + h * P + P]
                    ins = vec.scalar_tensor_tensor(dst, c_at[:, a, :], st[:, a:a + 1], dst, ALU.mult, ALU.mult)
                ins.then_inc(c_y, 1)

            def bn(_, use):
                dve.wait_ge(cq_ss, 1)
                rsqrt_mean(st[:, 4:6], Q_LORA)
                for m in range(M):
                    vec.tensor_scalar(y[:, m, 0:Q_LORA], y[:, m, 0:Q_LORA], st[:, 4 + m:5 + m], None,
                                      ALU.mult).then_inc(cq_norm, 1)

            def bt(i, use):
                dve.wait_ge(cq_hi_ready, i + 1)
                for j in range(min(2, QKT - 2 * i)):
                    kt = 2 * i + j
                    ins = vec.scalar_tensor_tensor(cq_lo[:, kt, :], bank(use)[:, j * SEQ:j * SEQ + SEQ],
                                                   par[:, R_CQ + kt:R_CQ + kt + 1], cq_hi[:, kt, :].bitcast(F32),
                                                   ALU.mult, ALU.subtract)
                done_bank(ins, use)

            def head_norms(n, norm):
                dve.wait_ge(b_sq_ready, M * (n + 1))
                for m in range(M):
                    ins = vec.tensor_reduce(st[:, 8 + 4 * m:12 + 4 * m],
                                            b_sq[:, m * 512:m * 512 + 512].rearrange("p (h d) -> p h d", h=4), AX_X,
                                            ALU.add)
                    step(ins)
                rsqrt_mean(st[:, 8:16], HEAD)
                for m in range(M):
                    v = (kv[:, m, 0:512] if n == 0 else qs[:, m, :]).rearrange("p (h d) -> p h d", h=4)
                    vec.tensor_tensor(v, v, st[:, 8 + 4 * m:12 + 4 * m].unsqueeze(2).to_broadcast([P, 4, P]),
                                      ALU.mult).then_inc(norm, 1)

            def bkn(_, use):
                head_norms(0, bk_norm)

            def bqn(g, use):
                head_norms(g + 1, bq_norm)

            def bsc(arg, use):
                j, p = arg
                for s in range(2):
                    h = 8 * j + 2 * p + s
                    wait_read(dve, "bsc", arg, s)
                    rl = (b_s, b_p)[s]
                    for m in range(M):
                        cols = slice(0, P) if m == 0 else slice(P, 3 * P)
                        w = small[:, m, G_WI + h:G_WI + h + 1]
                        if h == 0:
                            ins = vec.tensor_scalar(sc[:, cols], rl[:, cols], w, None, ALU.mult)
                        else:
                            ins = vec.scalar_tensor_tensor(sc[:, cols], rl[:, cols], w, sc[:, cols], ALU.mult,
                                                           ALU.add)
                        if m == 0:
                            step(ins)
                    ins.then_inc(b_score, 1)
                    dve.wait_ge(b_score, h + 1)

            def btk(arg, use):
                m, part = arg
                cols = slice(0, P) if m == 0 else slice(P, 3 * P)
                w = P * (m + 1)
                work = b_s[:, 0:w]
                if part == 0:
                    diag = sc[:, 2 * m * P:2 * m * P + P]
                    step(vec.tensor_tensor(diag, diag, cap[:], ALU.min))
                    step(vec.tensor_copy(work, sc[:, cols]))
                for r in range(part, min(part + 3 - m, TOPK // 8)):
                    step(vec.max(top8[:], work))
                    if r < TOPK // 8 - 1:
                        step(vec.match_replace(work, top8[:], work, -3.4028234e38))

            def bts(arg, use):
                m, part = arg
                cols = slice(0, P) if m == 0 else slice(P, 3 * P)
                w = P * (m + 1)
                work = b_s[:, 0:w]
                gt_, eq = b_p[:, 0:w], b_p[:, 256:256 + w]
                thr = top8[:, 7:8]
                if part == 1:
                    step(vec.tensor_tensor_scan(work, ones_f[:, 0:1].to_broadcast([P, w]), eq, 0.0, ALU.mult, ALU.add))
                    step(vec.scalar_tensor_tensor(work, work, st[:, 40:41], eq, ALU.is_le, ALU.mult))
                    step(vec.tensor_tensor(work, work, gt_, ALU.add))
                    step(vec.tensor_scalar(sc[:, cols], work, 1.0, -NEG, ALU.subtract, ALU.mult))
                    diag = sc[:, 2 * m * P:2 * m * P + P]
                    step(vec.tensor_tensor(diag, diag, low[:], ALU.min))
                    return
                step(vec.tensor_scalar(gt_, sc[:, cols], thr, None, ALU.is_gt))
                step(vec.tensor_reduce(st[:, 40:41], gt_, AX_X, ALU.add))
                step(vec.tensor_scalar(st[:, 40:41], st[:, 40:41], -1.0, float(TOPK), ALU.mult, ALU.add))
                step(vec.tensor_scalar(eq, sc[:, cols], thr, None, ALU.is_equal))

            def bs(arg, use):
                g, v = arg
                n, w = (4, P) if v == 0 else (2, SEQ)
                sel_ = (sc[:, 0:P] if v == 0 else sc[:, P:3 * P]).unsqueeze(1).to_broadcast([P, n, w])
                s3 = b_s[:].rearrange("p (h k) -> p h k", h=n)
                wait_filled(dve, use)
                done_bank(vec.tensor_tensor(s3, bank(use)[:].rearrange("p (h k) -> p h k", h=n), sel_, ALU.add), use)
                dve.wait_ge(emptied[use % 4], use // 4 + 1)
                step(vec.tensor_reduce(st[:, 24:24 + n], s3, AX_X, ALU.max))
                vec.tensor_scalar(st[:, 24:24 + n], st[:, 24:24 + n], -HEAD ** -0.5, None, ALU.mult).then_inc(b_max, 1)
                dve.wait_ge(b_exp, 3 * g + v + 1)
                step(vec.reciprocal(st[:, 28:28 + n], st[:, 28:28 + n]))

            def bo(arg, use):
                g, v = arg
                m = 0 if v == 0 else 1
                wait_filled(dve, use)
                for i in range(4 if v == 0 else 2):
                    h = 4 * g + (i if v == 0 else 2 * v - 2 + i)
                    dst = y[:, m, W_A + h * P:W_A + h * P + P]
                    ins = vec.scalar_tensor_tensor(dst, bank(use)[:, i * P:i * P + P], st[:, 28 + i:29 + i], dst,
                                                   ALU.mult, ALU.mult)
                done_bank(ins, use)

            def at(j, use):
                if j == 0:
                    vec.memset(a_v[:, :, :, HEAD:HEAD + 1], 1.0).then_inc(a_one, 1)

            def ae(h, use):
                wait_filled(dve, use)
                vec.tensor_tensor(a_m[:, 0:SEQ], bank(use)[:, 0:SEQ], tri[:].rearrange("p a b -> p (a b)"), ALU.add)
                done_bank(vec.tensor_tensor(a_m[:, SEQ:3 * P], bank(use)[:, P:SEQ], tri[:, 0, :], ALU.add), use)
                dve.wait_ge(a_exp, h + 1)
                wait_filled(dve, use + 1)
                done_bank(vec.tensor_tensor(a_p[:], bank(use + 1)[:, 0:3 * P], a_m[:], ALU.mult), use + 1)

            def ap(h, use):
                wait_filled(dve, use)
                b2 = bank(use)[:].rearrange("p (m c) -> p m c", m=M)
                step(vec.tensor_copy(st[:, 40:42], b2[:, :, HEAD]))
                step(vec.scalar_tensor_tensor(st[:, 40:42], st[:, 40:42], -1.0, st[:, 40:42], ALU.mult, ALU.max))
                step(vec.tensor_tensor(st[:, 40:42], st[:, 40:42], gcol[:, 7:9, h], ALU.max))
                step(vec.reciprocal(st[:, 40:42], st[:, 40:42]))
                for m in range(M):
                    ins = vec.tensor_scalar(a_h[:, m, :], b2[:, m, 0:HEAD], st[:, 40 + m:41 + m], None, ALU.mult)
                    if m == 0:
                        step(ins)
                done_bank(ins, use)

            def ay(h, use):
                dve.wait_ge(a_ss, h + 1)
                rsqrt_mean(st[:, 36:38], HEAD)
                for m in range(M):
                    dst = y[:, m, h * P:h * P + P]
                    ins = vec.scalar_tensor_tensor(dst, a_h[:, m, :], st[:, 36 + m:37 + m], dst, ALU.mult, ALU.mult)
                    if m == 0:
                        step(ins)
                ins.then_inc(a_y, 1)

            y_done = [0]

            def yt(i, use):
                y_done[0] += 1
                dve.wait_ge(y_hi_ready, y_done[0])
                for j in range(2):
                    kt = 2 * i + j
                    gain = y_gain(kt)
                    src, hi = bank(use)[:, j * SEQ:j * SEQ + SEQ], op_hi[:, kt, :].bitcast(F32)
                    if gain is None:
                        ins = vec.tensor_tensor(op_lo[:, kt, :], src, hi, ALU.subtract)
                    else:
                        ins = vec.scalar_tensor_tensor(op_lo[:, kt, :], src, gain, hi, ALU.mult, ALU.subtract)
                done_bank(ins, use)

            def par_columns(_, use):
                for i, (c0, n) in enumerate(((R_CQ, R_N - R_CQ), (R_N, N_TAP))):
                    wait_filled(dve, use + i)
                    done_bank(vec.tensor_copy(par[:, c0:c0 + n], bank(use + i)[:, 0:n]), use + i)

            pieces = dict(par=par_columns, evac=evac, g1=g1, g3=g3, gb=gb, gs=gs, kn=kn, kr=kr, kd=kd, kx=kx,
                          conv=conv, csq=csq, ce=ce, ca=ca, cg=cg, cm=cm, cu=cu, cs=cs, co=co, cy=cy, bn=bn, bt=bt,
                          bkn=bkn, bqn=bqn, bsc=bsc, btk=btk, bts=bts, bs=bs, bo=bo, at=at, ae=ae, ap=ap, ay=ay,
                          yt=yt)

            def x_lo(i):
                use = 1 + i
                dve.wait_ge(x_hi_ready, i + 1)
                for j in range(2):
                    kt = 2 * i + j
                    ins = vec.scalar_tensor_tensor(op_lo[:, kt, :], bank(use)[:, j * SEQ:j * SEQ + SEQ],
                                                   par[:, R_NORM + kt:R_NORM + kt + 1], op_hi[:, kt, :].bitcast(F32),
                                                   ALU.mult, ALU.subtract)
                done_bank(ins, use)

            wait_filled(dve, 0)
            done_bank(vec.tensor_copy(par[:, 0:R_CQ], bank(0)[:, 0:R_CQ]), 0)
            dve.wait_ge(emptied[0], 1)
            for c in range(AHEAD):
                if c < X_AHEAD:
                    x_lo(c)
                split_lo(c)
            for c in range(len(chunks)):
                if c + AHEAD < len(chunks):
                    split_lo(c + AHEAD)
                if c + X_AHEAD < NX:
                    x_lo(c + X_AHEAD)
                if c == NX - 1:
                    dve.wait_ge(ss_ready, NX)
                    step(vec.tensor_reduce(rstd[:], ssq[:], AX_X, ALU.add))
                    rsqrt_mean(rstd[:], D, rstd_ready)
                    dve.wait_ge(const_ready, 2)
                for name, arg, use in woven[c]:
                    if name in pieces:
                        pieces[name](arg, U0 + use)


_INS = ["x", "norm_g", "w_in", "w_out", "m_ib", "m_fb", "m_norm_g", "a_cq_g", "a_wuq", "a_wuqi", "a_qn_g", "a_kn_g",
        "a_ki_g", "a_ki_b", "d_conv_w", "d_a_log", "d_dt_bias", "d_norm_g"]
_OUTS = [((1, SEQ, D), "float32")]


def kernel(**inputs):
    import numpy as _np
    import concourse.bacc as _bacc
    from concourse import mybir as _mybir
    from concourse.bass_utils import run_bass_kernel_spmd as _run

    nc = _bacc.Bacc("TRN2", target_bir_lowering=False, num_devices=1)
    arrays, args = {}, []
    for name in _INS:
        a = _np.ascontiguousarray(inputs[name])
        arrays[f"in_{name}_dram"] = a
        args.append(nc.dram_tensor(f"in_{name}_dram", a.shape, _mybir.dt.from_np(a.dtype), kind="ExternalInput").ap())
    for i, (shape, dtype) in enumerate(_OUTS):
        dt = _mybir.dt.from_np(_np.dtype(dtype))
        args.append(nc.dram_tensor(f"out_{i}_dram", shape, dt, kind="ExternalOutput").ap())
    hybrid_kernel(nc, *args)
    r = _run(nc, [arrays], core_ids=[0])
    return r.results[0]["out_0_dram"]
```
